# Optimizing a Trainium2 kernel written in Bass

```python
import math
import jax
import jax.numpy as jnp
from jax import lax
import numpy as np

D_MODEL = 1024
BATCH = 1
SEQ = 128
DEPTH = 2
DEC_BATCH = 1
DEC_SEQ = 128
PAST_LEN = 128

GRID_W = 64
N_EVEN = (DEPTH + 1) // 2
N_ODD = DEPTH // 2
N_MOD = 6
NORM_EPS = 1e-6

HY_W = D_MODEL // 2
HY_ORDER = 2
HY_SHORT = 3
HY_EMB = 33
HY_BANDS = (HY_EMB - 1) // 2
HY_FFN = 64
HY_TARGET = 1e-2
HY_FAST = 0.3
HY_SLOW = 1.5

RW_W = D_MODEL // 2
RW_N = 64
RW_H = RW_W // RW_N
RW_WLORA = 32
RW_ALORA = 32
RW_GLORA = 96
RW_LN_EPS = 64e-5
RW_PROJ = 3 * RW_W + 2 * RW_WLORA + 2 * RW_ALORA + RW_GLORA
P_EVEN = 3 * HY_W + RW_PROJ

GD_H = 8
GD_DK = 128
GD_DV = 128
GD_QK = GD_H * GD_DK
GD_W = GD_H * GD_DV
GD_CONV = 3
GD_CHUNK = 64
P_ODD = 2 * GD_QK + 2 * GD_W + 4 * GD_H

D_FF = 2816
N_EXP = 8
TOP_K = 2
E_FF = 3584

kernel_name = 'hybrid_hyena_rwkv7_gdn_diffusion_step'

def _split(x, sizes):
    return jnp.split(x, np.cumsum(sizes)[:-1].tolist(), axis=-1)

def rmsnorm(x, g):
    xf = x.astype(jnp.float32)
    y = xf * lax.rsqrt(jnp.mean(xf * xf, -1, keepdims=True) + NORM_EPS)
    return (y * g.astype(jnp.float32)).astype(x.dtype)

def dwconv_centred(x, w):
    K = w.shape[0]
    p = K // 2
    L = x.shape[1]
    xp = jnp.pad(x, ((0, 0), (p, p), (0, 0)))
    y = xp[:, 0:L] * w[0]
    for j in range(1, K):
        y = y + xp[:, j:j + L] * w[j]
    return y

def grid_pos_embed(n_tokens):
    rows = n_tokens // GRID_W
    t = jnp.arange(rows * GRID_W)
    row = (t // GRID_W).astype(jnp.float32)
    col = (t % GRID_W).astype(jnp.float32)
    q = D_MODEL // 4
    omega = jnp.exp(-math.log(10000.0) * jnp.arange(q, dtype=jnp.float32) / q)
    enc = lambda pos: jnp.concatenate([jnp.sin(pos[:, None] * omega), jnp.cos(pos[:, None] * omega)], -1)
    return jnp.concatenate([enc(row), enc(col)], -1)

def hyena_filters(L, w1, b1, f1, w2, b2, f2, w3):
    k = jnp.arange(L, dtype=jnp.float32)
    t = k / (L - 1)
    bands = jnp.linspace(1e-4, HY_BANDS - 1, HY_BANDS, dtype=jnp.float32)
    ang = (2.0 * math.pi * k / L)[:, None] * bands[None, :]
    feats = jnp.concatenate([t[:, None], jnp.cos(ang), -jnp.sin(ang)], -1)
    h = jnp.sin(f1 * (feats @ w1 + b1))
    h = jnp.sin(f2 * (h @ w2 + b2))
    h = (h @ w3).reshape(L, 2, HY_ORDER, HY_W)
    deltas = jnp.abs(jnp.linspace(math.log(HY_TARGET) / HY_FAST, math.log(HY_TARGET) / HY_SLOW, HY_W, dtype=jnp.float32))
    window = jnp.exp(-t[:, None] * deltas[None, :])
    h = h * window[:, None, None, :]
    fwd = h[:, 0]
    bwd = h[1:, 1][::-1]
    full = jnp.concatenate([fwd, jnp.zeros((1, HY_ORDER, HY_W), jnp.float32), bwd], 0)
    return full / jnp.sum(jnp.abs(full), 0, keepdims=True)

def hyena_mix(u, filt, bias):
    L = u.shape[1]
    v, x1, x2 = jnp.split(u, 3, -1)
    hf = jnp.fft.rfft(filt, axis=0)
    z = v
    for o, gate in enumerate((x1, x2)):
        zf = jnp.fft.rfft(z, n=2 * L, axis=1)
        conv = jnp.fft.irfft(zf * hf[None, :, o], n=2 * L, axis=1)[:, :L]
        z = gate * (conv + z * bias[o])
    return z

def token_shift_centred(p, mu):
    pp = jnp.pad(p, ((0, 0), (1, 1), (0, 0)))
    nb = 0.5 * (pp[:, :-2] + pp[:, 2:])
    return p + (nb - p) * mu

def rwkv7_scan(r, decay, k, v, a, b, s0, reverse):
    def step(S, inp):
        r_t, d_t, k_t, v_t, a_t, b_t = inp
        sa = jnp.einsum('bhvk,bhk->bhv', S, a_t)
        S = S * d_t[:, :, None, :] + sa[..., None] * b_t[:, :, None, :] + v_t[..., None] * k_t[:, :, None, :]
        return S, jnp.einsum('bhvk,bhk->bhv', S, r_t)
    xs = tuple(jnp.swapaxes(t, 0, 1) for t in (r, decay, k, v, a, b))
    s_fin, ys = lax.scan(step, s0, xs, reverse=reverse)
    return jnp.swapaxes(ys, 0, 1), s_fin

def rwkv7_mix(p, s0, mu, w0, w2, a0, a2, g2, k_k, k_a, r_k, ln_w, ln_b):
    B, L, _ = p.shape
    p = token_shift_centred(p, mu)
    r, k, v, wd, ad, gd = _split(p, (RW_W, RW_W, RW_W, 2 * RW_WLORA, 2 * RW_ALORA, RW_GLORA))
    wd = wd.reshape(B, L, 2, RW_WLORA)
    ad = ad.reshape(B, L, 2, RW_ALORA)
    w = -jax.nn.softplus(-(w0 + jnp.einsum('bldr,drc->bldc', jnp.tanh(wd), w2))) - 0.5
    decay = jnp.exp(-jnp.exp(w))
    a = jax.nn.sigmoid(a0 + jnp.einsum('bldr,drc->bldc', ad, a2))
    g = jax.nn.sigmoid(gd) @ g2
    heads = lambda t: t.reshape(t.shape[:-1] + (RW_H, RW_N))
    kk = heads(k * k_k)
    kk = kk / jnp.maximum(jnp.linalg.norm(kk, axis=-1, keepdims=True), 1e-12)
    k_dir = k[:, :, None, :] * (1.0 + (a - 1.0) * k_a)
    rh, vh = heads(r), heads(v)
    ys, bonus, states = [], [], []
    for d in range(2):
        a_d = heads(a[:, :, d])
        k_d = heads(k_dir[:, :, d])
        y_d, s_d = rwkv7_scan(rh, heads(decay[:, :, d]), k_d, vh, -kk, kk * a_d, s0[:, d], d == 1)
        ys.append(y_d)
        bonus.append(jnp.sum(rh * k_d * r_k, -1, keepdims=True) * vh)
        states.append(s_d)
    y = ys[0] + ys[1]
    mean = jnp.mean(y, -1, keepdims=True)
    var = jnp.mean(jnp.square(y - mean), -1, keepdims=True)
    y = ((y - mean) * lax.rsqrt(var + RW_LN_EPS)).reshape(B, L, RW_W) * ln_w + ln_b
    y = (y + (bonus[0] + bonus[1]).reshape(B, L, RW_W)) * g
    return y, jnp.stack(states, 1)

def even_mixer(h, s0, P, j):
    f32 = jnp.float32
    B, L, _ = h.shape
    p = (h @ P['e_w_in'][j]).astype(f32)
    p_hy, p_rw = p[..., :3 * HY_W], p[..., 3 * HY_W:]
    u = dwconv_centred(p_hy, P['e_hy_conv_w'][j].astype(f32)) + P['e_hy_conv_b'][j].astype(f32)
    filt = hyena_filters(L, P['e_hf_w1'][j].astype(f32), P['e_hf_b1'][j].astype(f32), P['e_hf_freq1'][j].astype(f32),
                         P['e_hf_w2'][j].astype(f32), P['e_hf_b2'][j].astype(f32), P['e_hf_freq2'][j].astype(f32),
                         P['e_hf_w3'][j].astype(f32))
    y_hy = hyena_mix(u, filt, P['e_hy_bias'][j].astype(f32))
    y_rw, s_new = rwkv7_mix(p_rw, s0.astype(f32), P['e_rw_mu'][j].astype(f32), P['e_rw_w0'][j].astype(f32),
                            P['e_rw_w2'][j].astype(f32), P['e_rw_a0'][j].astype(f32), P['e_rw_a2'][j].astype(f32),
                            P['e_rw_g2'][j].astype(f32), P['e_rw_kk'][j].astype(f32), P['e_rw_ka'][j].astype(f32),
                            P['e_rw_rk'][j].astype(f32), P['e_rw_ln_w'][j].astype(f32), P['e_rw_ln_b'][j].astype(f32))
    y = jnp.concatenate([y_hy, y_rw], -1).astype(h.dtype) @ P['e_w_out'][j]
    return y, s_new

def gdn_chunked(q, k, v, g, beta, s0):
    B, L, H, DK = q.shape
    DV = v.shape[-1]
    C = GD_CHUNK
    NC = L // C
    to_chunks = lambda t: jnp.swapaxes(t.reshape((B, NC, C, H) + t.shape[3:]), 2, 3)
    q = to_chunks(q * DK ** -0.5)
    k = to_chunks(k)
    v = to_chunks(v)
    g = jnp.cumsum(to_chunks(g), axis=-1)
    beta = to_chunks(beta)
    idx = jnp.arange(C)
    causal = idx[:, None] >= idx[None, :]
    strict = idx[:, None] > idx[None, :]
    gamma = jnp.exp(jnp.where(causal, g[..., :, None] - g[..., None, :], -jnp.inf))
    kb = k * beta[..., None]
    A = jnp.where(strict, jnp.einsum('bnhid,bnhjd->bnhij', kb, k) * gamma, 0.0)
    eye = jnp.eye(C, dtype=jnp.float32)
    T = lax.linalg.triangular_solve(A + eye, jnp.broadcast_to(eye, A.shape), left_side=True, lower=True, unit_diagonal=True)
    u = T @ (v * beta[..., None])
    w = T @ (kb * jnp.exp(g)[..., None])
    qk = jnp.where(causal, jnp.einsum('bnhid,bnhjd->bnhij', q, k) * gamma, 0.0)
    q_dec = q * jnp.exp(g)[..., None]
    k_dec = k * jnp.exp(g[..., -1:] - g)[..., None]
    g_tot = jnp.exp(g[..., -1])

    def step(S, inp):
        u_n, w_n, qk_n, qd_n, kd_n, gt_n = inp
        v_new = u_n - jnp.einsum('bhck,bhkv->bhcv', w_n, S)
        o = jnp.einsum('bhck,bhkv->bhcv', qd_n, S) + jnp.einsum('bhij,bhjv->bhiv', qk_n, v_new)
        S = S * gt_n[..., None, None] + jnp.einsum('bhck,bhcv->bhkv', kd_n, v_new)
        return S, o

    xs = tuple(jnp.swapaxes(t, 0, 1) for t in (u, w, qk, q_dec, k_dec, g_tot))
    s_fin, o = lax.scan(step, s0, xs)
    o = jnp.transpose(o, (1, 0, 3, 2, 4)).reshape(B, L, H, DV)
    return o, s_fin

def gdn_mix(p, s0, conv_w, A_log, dt_bias, norm_g):
    B, L, _ = p.shape
    qkv, z, a, b = _split(p, (2 * GD_QK + GD_W, GD_W, 2 * GD_H, 2 * GD_H))
    qkv = jax.nn.silu(dwconv_centred(qkv, conv_w))
    q, k, v = _split(qkv, (GD_QK, GD_QK, GD_W))
    l2n = lambda t: t * lax.rsqrt(jnp.sum(t * t, -1, keepdims=True) + 1e-6)
    q = l2n(q.reshape(B, L, GD_H, GD_DK))
    k = l2n(k.reshape(B, L, GD_H, GD_DK))
    v = v.reshape(B, L, GD_H, GD_DV)
    g = -jnp.exp(A_log) * jax.nn.softplus(a.reshape(B, L, 2, GD_H) + dt_bias)
    beta = jax.nn.sigmoid(b.reshape(B, L, 2, GD_H))
    o_f, s_f = gdn_chunked(q, k, v, g[:, :, 0], beta[:, :, 0], s0[:, 0])
    flip = lambda t: t[:, ::-1]
    o_b, s_b = gdn_chunked(flip(q), flip(k), flip(v), flip(g[:, :, 1]), flip(beta[:, :, 1]), s0[:, 1])
    o = o_f + flip(o_b)
    o = o * lax.rsqrt(jnp.mean(o * o, -1, keepdims=True) + NORM_EPS) * norm_g
    o = o * jax.nn.silu(z.reshape(B, L, GD_H, GD_DV))
    return o.reshape(B, L, GD_W), jnp.stack([s_f, s_b], 1)

def odd_mixer(h, s0, P, j):
    f32 = jnp.float32
    p = (h @ P['o_w_in'][j]).astype(f32)
    y, s_new = gdn_mix(p, s0.astype(f32), P['o_conv_w'][j].astype(f32), P['o_A_log'][j].astype(f32),
                       P['o_dt_bias'][j].astype(f32), P['o_norm_g'][j].astype(f32))
    return y.astype(h.dtype) @ P['o_w_out'][j], s_new

def dense_swiglu(h, w_in, w_out):
    gate, up = jnp.split(h @ w_in, 2, -1)
    return (jax.nn.silu(gate) * up) @ w_out

def moe_swiglu(h, router, w_in, w_out):
    logits = (h @ router).astype(jnp.float32)
    top_val, top_idx = lax.top_k(logits, TOP_K)
    gates = jax.nn.softmax(top_val, -1)
    combine = jnp.einsum('blk,blke->ble', gates, jax.nn.one_hot(top_idx, N_EXP, dtype=jnp.float32)).astype(h.dtype)
    out = dense_swiglu(h, w_in[0], w_out[0]) * combine[..., 0:1]
    for e in range(1, N_EXP):
        out = out + dense_swiglu(h, w_in[e], w_out[e]) * combine[..., e:e + 1]
    return out

def trunk(x, cond, rw_s0, gd_s0, P):
    rw_states, gd_states = [], []
    for i in range(DEPTH):
        j = i // 2
        mod = (jax.nn.silu(cond) @ P['ada_w'][i] + P['ada_b'][i])[:, None, :]
        sh1, sc1, g1, sh2, sc2, g2 = jnp.split(mod, N_MOD, -1)
        h = rmsnorm(x, P['norm_mix_g'][i]) * (1 + sc1) + sh1
        if i % 2 == 0:
            out, s = even_mixer(h, rw_s0[:, j], P, j)
            rw_states.append(s)
        else:
            out, s = odd_mixer(h, gd_s0[:, j], P, j)
            gd_states.append(s)
        x = x + g1 * out
        h = rmsnorm(x, P['norm_ffn_g'][i]) * (1 + sc2) + sh2
        if i % 2 == 0:
            ff = dense_swiglu(h, P['e_ffn_w_in'][j], P['e_ffn_w_out'][j])
        else:
            ff = moe_swiglu(h, P['o_router'][j], P['o_moe_w_in'][j], P['o_moe_w_out'][j])
        x = x + g2 * ff
    return rmsnorm(x, P['final_norm_g']), jnp.stack(rw_states, 1), jnp.stack(gd_states, 1)

def setup_inputs(seed: int = 0) -> dict:
    key = jax.random.key(seed)
    ks = iter(jax.random.split(key, 64))
    nrm = lambda shape, s: jax.random.normal(next(ks), shape, jnp.float32) * s
    uni = lambda shape, lo, hi: jax.random.uniform(next(ks), shape, jnp.float32, lo, hi)
    D = D_MODEL
    NE = N_EVEN
    NO = N_ODD
    inv = lambda n: n ** -0.5
    dt = jnp.exp(uni((NO, 2, GD_H), math.log(1e-3), math.log(1e-1)))
    return {
        'x_prompt': nrm((BATCH, SEQ, D), 1.0),
        'x_sample': nrm((DEC_BATCH, DEC_SEQ, D), 1.0),
        'state_rwkv': nrm((DEC_BATCH, NE, 2, RW_H, RW_N, RW_N), 0.1),
        'state_gdn': nrm((DEC_BATCH, NO, 2, GD_H, GD_DK, GD_DV), 0.1),
        'c': nrm((DEC_BATCH, D), 1.0),
        'c_ctx': nrm((D,), 1.0),
        'ada_w': nrm((DEPTH, D, N_MOD * D), 0.5 * inv(D)),
        'ada_b': nrm((DEPTH, N_MOD * D), 0.02),
        'norm_mix_g': 1.0 + nrm((DEPTH, D), 0.05),
        'norm_ffn_g': 1.0 + nrm((DEPTH, D), 0.05),
        'final_norm_g': 1.0 + nrm((D,), 0.05),
        'e_w_in': nrm((NE, D, P_EVEN), inv(D)),
        'e_hy_conv_w': nrm((NE, HY_SHORT, 3 * HY_W), 0.5),
        'e_hy_conv_b': nrm((NE, 3 * HY_W), 0.02),
        'e_hf_w1': nrm((NE, HY_EMB, HY_FFN), inv(HY_EMB)),
        'e_hf_b1': nrm((NE, HY_FFN), 0.1),
        'e_hf_freq1': 1.0 + nrm((NE, HY_FFN), 0.05),
        'e_hf_w2': nrm((NE, HY_FFN, HY_FFN), inv(HY_FFN)),
        'e_hf_b2': nrm((NE, HY_FFN), 0.1),
        'e_hf_freq2': 1.0 + nrm((NE, HY_FFN), 0.05),
        'e_hf_w3': nrm((NE, HY_FFN, 2 * HY_ORDER * HY_W), inv(HY_FFN)),
        'e_hy_bias': nrm((NE, HY_ORDER, HY_W), 0.5),
        'e_rw_mu': uni((NE, RW_PROJ), 0.0, 1.0),
        'e_rw_w0': uni((NE, 2, RW_W), -6.0, -1.0),
        'e_rw_w2': nrm((NE, 2, RW_WLORA, RW_W), 0.5 * inv(RW_WLORA)),
        'e_rw_a0': nrm((NE, 2, RW_W), 0.1),
        'e_rw_a2': nrm((NE, 2, RW_ALORA, RW_W), 0.5 * inv(RW_ALORA)),
        'e_rw_g2': nrm((NE, RW_GLORA, RW_W), inv(RW_GLORA)),
        'e_rw_kk': 0.85 + nrm((NE, RW_W), 0.05),
        'e_rw_ka': 1.0 + nrm((NE, RW_W), 0.05),
        'e_rw_rk': nrm((NE, RW_H, RW_N), 0.1),
        'e_rw_ln_w': 1.0 + nrm((NE, RW_W), 0.05),
        'e_rw_ln_b': nrm((NE, RW_W), 0.02),
        'e_w_out': nrm((NE, HY_W + RW_W, D), inv(HY_W + RW_W)),
        'e_ffn_w_in': nrm((NE, D, 2 * D_FF), inv(D)),
        'e_ffn_w_out': nrm((NE, D_FF, D), inv(D_FF)),
        'o_w_in': jnp.concatenate([nrm((NO, D, 2 * GD_QK + 2 * GD_W), inv(D)),
                                   nrm((NO, D, 2 * GD_H), 0.1 * inv(D)),
                                   nrm((NO, D, 2 * GD_H), inv(D))], -1),
        'o_conv_w': nrm((NO, GD_CONV, 2 * GD_QK + GD_W), 0.5),
        'o_A_log': jnp.log(uni((NO, 2, GD_H), 1.0, 16.0)),
        'o_dt_bias': dt + jnp.log(-jnp.expm1(-dt)),
        'o_norm_g': 1.0 + nrm((NO, GD_DV), 0.05),
        'o_w_out': nrm((NO, GD_W, D), inv(GD_W)),
        'o_router': nrm((NO, D, N_EXP), inv(D)),
        'o_moe_w_in': nrm((NO, N_EXP, D, 2 * E_FF), inv(D)),
        'o_moe_w_out': nrm((NO, N_EXP, E_FF, D), inv(E_FF)),
    }

def reference(x_prompt, x_sample, state_rwkv, state_gdn, c, c_ctx,
              ada_w, ada_b, norm_mix_g, norm_ffn_g, final_norm_g,
              e_w_in, e_hy_conv_w, e_hy_conv_b, e_hf_w1, e_hf_b1, e_hf_freq1, e_hf_w2, e_hf_b2, e_hf_freq2,
              e_hf_w3, e_hy_bias, e_rw_mu, e_rw_w0, e_rw_w2, e_rw_a0, e_rw_a2, e_rw_g2, e_rw_kk, e_rw_ka,
              e_rw_rk, e_rw_ln_w, e_rw_ln_b, e_w_out, e_ffn_w_in, e_ffn_w_out,
              o_w_in, o_conv_w, o_A_log, o_dt_bias, o_norm_g, o_w_out, o_router, o_moe_w_in, o_moe_w_out):
    P = {
        'ada_w': ada_w, 'ada_b': ada_b, 'norm_mix_g': norm_mix_g, 'norm_ffn_g': norm_ffn_g,
        'final_norm_g': final_norm_g,
        'e_w_in': e_w_in, 'e_hy_conv_w': e_hy_conv_w, 'e_hy_conv_b': e_hy_conv_b,
        'e_hf_w1': e_hf_w1, 'e_hf_b1': e_hf_b1, 'e_hf_freq1': e_hf_freq1,
        'e_hf_w2': e_hf_w2, 'e_hf_b2': e_hf_b2, 'e_hf_freq2': e_hf_freq2,
        'e_hf_w3': e_hf_w3, 'e_hy_bias': e_hy_bias,
        'e_rw_mu': e_rw_mu, 'e_rw_w0': e_rw_w0, 'e_rw_w2': e_rw_w2, 'e_rw_a0': e_rw_a0, 'e_rw_a2': e_rw_a2,
        'e_rw_g2': e_rw_g2, 'e_rw_kk': e_rw_kk, 'e_rw_ka': e_rw_ka, 'e_rw_rk': e_rw_rk,
        'e_rw_ln_w': e_rw_ln_w, 'e_rw_ln_b': e_rw_ln_b, 'e_w_out': e_w_out,
        'e_ffn_w_in': e_ffn_w_in, 'e_ffn_w_out': e_ffn_w_out,
        'o_w_in': o_w_in, 'o_conv_w': o_conv_w, 'o_A_log': o_A_log, 'o_dt_bias': o_dt_bias,
        'o_norm_g': o_norm_g, 'o_w_out': o_w_out, 'o_router': o_router,
        'o_moe_w_in': o_moe_w_in, 'o_moe_w_out': o_moe_w_out,
    }
    B = x_prompt.shape[0]
    rw0 = jnp.zeros((B, N_EVEN, 2, RW_H, RW_N, RW_N), jnp.float32)
    gd0 = jnp.zeros((B, N_ODD, 2, GD_H, GD_DK, GD_DV), jnp.float32)
    y_prompt, new_state_rwkv, new_state_gdn = trunk(x_prompt, c_ctx[None, :], rw0, gd0, P)
    x_lat = x_sample + grid_pos_embed(x_sample.shape[1]).astype(x_sample.dtype)[None]
    y_sample, _, _ = trunk(x_lat, c, state_rwkv, state_gdn, P)
    return (y_prompt, y_sample, new_state_rwkv, new_state_gdn)


_drawn_inputs = setup_inputs


def setup_inputs(seed=0):
    import zlib

    import numpy as np

    out = dict(_drawn_inputs(seed))
    spreads = {}
    factors = {'state_rwkv': 8.0,
     'e_hy_conv_b': 26.329,
     'e_hf_b1': 2.777,
     'e_hf_freq1': 7.813,
     'e_hf_b2': 3.825,
     'e_hf_freq2': 39.665,
     'e_rw_ln_w': 3.783,
     'e_rw_ln_b': 7.618,
     'o_norm_g': 3.815}
    for name, (base, spread) in spreads.items():
        noise = np.random.default_rng([zlib.crc32(name.encode()), seed]).standard_normal(out[name].shape)
        drawn = base * np.exp(spread * noise) if base else spread * noise
        out[name] = jnp.asarray(drawn.astype(out[name].dtype))
    for name, factor in factors.items():
        out[name] = (out[name] * factor).astype(out[name].dtype)
    return out
```

```python
import math
from contextlib import ExitStack

import numpy as np
import concourse.bass as bass
from concourse import mybir

F32 = mybir.dt.float32
U8 = mybir.dt.uint8
I32 = mybir.dt.int32
ALU = mybir.AluOpType
ACT = mybir.ActivationFunctionType
AX = mybir.AxisListType

P = 128
T = 128
NS = 2
TT = NS * T
D = 1024
DC = D // P
HYC = 4
RWC = 4
RWN = 64
KAPPA = math.exp(-0.5)
GH = 8
FF = 2816
NE = 8
EFF = 3584
RING = 7
TILE = 4096
LEVELS = 7
EVEN_IN_TILES = 7
FFN_IN_TILES = 11
FFN_OUT_TILES = 6
ODD_IN_TILES = 9
EXP_TILES = 21

STREAM = [("ada0a", 4), ("even_in", EVEN_IN_TILES), ("ada0b", 8), ("ada1", 12), ("even_out", 2), ("ffn", 17),
          ("odd_in", ODD_IN_TILES), ("odd_out", 2)]
FIRST = {}
_n = 0
for _name, _k in STREAM:
    FIRST[_name] = _n
    _n += _k
STREAM_TILES = _n

PARAM_SIZES = [("cond", 16), ("ada_b0", 48), ("ada_b1", 48), ("gmix0", 8), ("gmix1", 8), ("gffn0", 8), ("gffn1", 8),
               ("gfin", 8), ("hyw", 36), ("hyb", 12), ("mu", 14), ("w0", 8), ("a0", 8), ("kk", 4), ("ka", 4), ("rk", 4),
               ("lnw", 4), ("lnb", 4), ("gdw", 72), ("normg", 1), ("hfb1", 1), ("hff1", 1), ("hfb2", 1), ("hff2", 1)]
PCOL = {}
_n = 0
for _name, _k in PARAM_SIZES:
    PCOL[_name] = (_n, _k)
    _n += _k
NPARAM = _n

CONST_SIZES = [[("ident", 128), ("ones", 128), ("bones", 128), ("reset", 256), ("iota", 128),
                ("eps6", 1), ("lneps", 1), ("one", 1), ("tie", 64)],
               [("dft_c", 128), ("dft_s", 128), ("inv_c", 128), ("inv_s", 128)],
               [("tri_f", 128), ("tri_b", 128), ("tri_sf", 128), ("tri_sb", 128), ("incl_f", 128), ("incl_b", 128),
                ("strict_f", 128), ("strict_b", 128)]]
CCOL = {}
NCONST = []
for _g, _sizes in enumerate(CONST_SIZES):
    _n = 0
    for _name, _k in _sizes:
        CCOL[_name] = (_g, _n, _k)
        _n += _k
    NCONST.append(_n)


def constants():
    i = np.arange(P)
    row, col = i[:, None], i[None, :]
    f = {}
    f["ident"] = (row == col)
    f["ones"] = np.ones((P, P))
    f["bones"] = (row // 64 == col // 64)
    f["tri_f"] = (row <= col)
    f["tri_b"] = (row >= col)
    f["tri_sf"] = (row > col)
    f["tri_sb"] = (row < col)
    f["incl_f"] = (row <= col)
    f["incl_b"] = (row >= col)
    f["strict_f"] = (col < row)
    f["strict_b"] = (col > row)
    ang = 2 * np.pi * (row + 0.0) * (col + 0.5) / 256.0
    f["dft_c"] = np.cos(ang)
    f["dft_s"] = -np.sin(ang)
    f["inv_c"] = np.cos(ang.T) * (2 / 256.0)
    f["inv_s"] = -np.sin(ang.T) * (2 / 256.0)
    r = np.ones((P, 256))
    r[:, 0] = 0
    r[:, 128] = 0
    f["reset"] = r
    f["iota"] = np.broadcast_to(col, (P, P))
    f["eps6"] = np.full((P, 1), 1e-6)
    f["lneps"] = np.full((P, 1), 64e-5)
    f["one"] = np.ones((P, 1))
    e = np.arange(8)
    f["tie"] = np.broadcast_to((e[None, :] < e[:, None]).reshape(1, 64), (P, 64))
    table = [np.concatenate([np.asarray(f[n], np.float32).reshape(P, k) for n, k in g], 1) for g in CONST_SIZES]
    low = np.zeros((LEVELS, P, P), np.float32)
    for l in range(LEVELS):
        b = 1 << l
        low[l] = ((row // b) % 2 == 1) & (col // b == row // b - 1)
    lev = np.concatenate([low.transpose(1, 0, 2), low.transpose(2, 0, 1)], 1).reshape(P, -1)
    sel = np.concatenate([row < col, row <= col, row > col, row >= col, col < row, col > row], 1).astype(np.float32)
    masks = np.concatenate([lev, sel], 1)
    k = np.arange(T, dtype=np.float32)
    t = (k / np.float32(T - 1)).astype(np.float32)
    bands = np.linspace(1e-4, 15, 16, dtype=np.float32)
    an = (np.float32(2.0 * math.pi) * k / T)[:, None].astype(np.float32) * bands[None, :]
    feats = np.concatenate([t[:, None], np.cos(an), -np.sin(an)], -1).astype(np.float32).T.copy()
    deltas = np.abs(np.linspace(math.log(1e-2) / 0.3, math.log(1e-2) / 1.5, 512, dtype=np.float32))
    win = np.exp(-t[:, None] * deltas[None, :]).astype(np.float32)
    winb = win.copy()
    winb[0] = 0
    window = np.concatenate([win, winb], 1)
    q = D // 4
    omega = np.exp(-math.log(10000.0) * np.arange(q, dtype=np.float32) / q).astype(np.float32)
    tok = np.arange(T)
    rr, cc = (tok // 64).astype(np.float32), (tok % 64).astype(np.float32)
    enc = lambda z: np.concatenate([np.sin(z[:, None] * omega), np.cos(z[:, None] * omega)], -1)
    pos = np.concatenate([enc(rr), enc(cc)], -1).astype(np.float32)
    posT = pos.T.reshape(DC, P, T).transpose(1, 0, 2).copy()
    return table, masks, feats, window, posT


def program(nc, A, O):
    ctx = ExitStack()
    with ctx:
        def sb(name, shape, dt=F32, where=ctx):
            return where.enter_context(nc.sbuf_tensor(name, shape, dt))

        sems = {}

        def sem(name):
            if name not in sems:
                sems[name] = ctx.enter_context(nc.semaphore(name))
            return sems[name]

        class Link:
            def __init__(self, name):
                self.sem, self.n = sem(name), 0

            def __call__(self, eng, ins):
                self.n += 1
                ins.then_inc(self.sem, 1)
                eng.wait_ge(self.sem, self.n)

            def last(self, eng, ins):
                self.n += 1
                ins.then_inc(self.sem, 1)

            def sync(self, eng):
                eng.wait_ge(self.sem, self.n)

        ps = [ctx.enter_context(nc.psum_tensor(f"bank{i}", [P, 512], F32)) for i in range(8)]
        ring = sb("ring", [P, RING, TILE])
        xT = sb("xT", [P, DC, TT])
        par = sb("par", [P, NPARAM])
        con0 = sb("con0", [P, NCONST[0]])
        masks = sb("masks", [P, 2 * LEVELS * P + 6 * P], U8)
        mod = sb("mod", [P, 2, 48, 2])
        scl = sb("scl", [P, 4, DC, 2])
        rstd = sb("rstd", [P, TT])
        silc = sb("silc", [P, DC, 32])
        ARENA = (nc.SBUF_PARTITION_SIZE_BYTES - 16384 - 768 - 4 * (RING * TILE + DC * TT + NPARAM + NCONST[0] + 192 + 64 + TT + 256)
                 - 2 * LEVELS * P - 6 * P) // 4 // 8 * 8
        arena = sb("arena", [P, ARENA])
        floats = [0]

        def take(*shape, rows=P):
            n = 1
            for k in shape:
                n *= k
            assert floats[0] + n <= ARENA, (floats[0], n, ARENA)
            ap = arena[0:rows, floats[0]:floats[0] + n]
            floats[0] += n
            if len(shape) == 1:
                return ap
            names = "abcd"[:len(shape)]
            return ap.rearrange(f"p ({' '.join(names)}) -> p {' '.join(names)}", **{names[i]: shape[i] for i in range(len(shape))})

        def drop(to):
            floats[0] = to

        def pcol(name, i=0, n=None):
            o, k = PCOL[name]
            n = k - i if n is None else n
            return par[:, o + i:o + i + n]

        cons = {0: con0}

        def cc(name):
            g, o, k = CCOL[name]
            return cons[g][:, o:o + k]

        ident, ones, bones = cc("ident"), cc("ones"), cc("bones")
        lvl = masks[:, 0:2 * LEVELS * P].rearrange("p (u l t) -> p u l t", u=2, l=LEVELS)
        selm = masks[:, 2 * LEVELS * P:].rearrange("p (k t) -> p k t", k=6)

        s_const = sem("const_loaded")
        s_slot = [sem(f"slot{i}_loaded") for i in range(RING)]
        s_used = sem("tiles_used")
        dve_link, act_link, pool_link = Link("dve_link"), Link("act_link"), Link("pool_link")

        def slot(n):
            return ring[:, n % RING, :]

        def tile_in(n):
            return slot(n).rearrange("p (j c) -> p j c", j=8)

        def tile_out(n):
            return slot(n).rearrange("p (j c) -> p j c", j=4)

        def arrived(eng, n):
            eng.wait_ge(s_slot[n % RING], 16 * (n // RING + 1))

        def feed(sp, upto):
            while feed.n < min(upto + RING, STREAM_TILES + EXP_TILES * NE):
                n = feed.n
                if n >= RING:
                    sp.wait_ge(s_used, n - RING + 1)
                src = A["stream"][n] if n < STREAM_TILES else A["experts"][(n - STREAM_TILES) // EXP_TILES,
                                                                           (n - STREAM_TILES) % EXP_TILES]
                sp.dma_start(slot(n), src).then_inc(s_slot[n % RING], 16)
                feed.n += 1
        feed.n = 0

        norm_no = [0]
        s_sq, s_ss, s_rt, s_h = sem("squares_done"), sem("sumsq_done"), sem("root_done"), sem("h_ready")

        class Norm:
            def __init__(self, sub, sq):
                self.k, self.sub, self.sq = norm_no[0], sub, sq
                norm_no[0] += 1

            def act_squares(self, act):
                nc.scalar.activation(self.sq[:], xT[:], ACT.Square).then_inc(s_sq, 1)

            def pe(self, pe, bank):
                pe.wait_ge(s_sq, self.k + 1)
                for j in range(DC):
                    mm = nc.tensor.matmul(bank[:, 0:TT], ones, self.sq[:, j, :], start=(j == 0), stop=(j == DC - 1))
                mm.then_inc(s_ss, 1)

            def act_root(self, act, bank):
                act.wait_ge(s_ss, self.k + 1)
                nc.scalar.activation(rstd[:], bank[:, 0:TT], ACT.Sqrt, scale=1.0 / D, bias=cc("eps6")).then_inc(s_rt, 1)

            def dve(self, dve, out=None):
                dve.wait_ge(s_rt, self.k + 1)
                dve_link(dve, nc.vector.reciprocal(rstd[:], rstd[:]))
                for j in range(DC):
                    dve_link.last(dve, nc.vector.tensor_tensor(self.sq[:, j, :], xT[:, j, :], rstd[:], ALU.mult))
                dve_link.sync(dve)
                for j in range(DC):
                    if self.sub is None:
                        ins = nc.vector.tensor_scalar(out[:, j, :], self.sq[:, j, :], pcol("gfin", j, 1), None, ALU.mult)
                        ins.then_inc(s_h, 1)
                        continue
                    layer, second = divmod(self.sub, 2)
                    for s in range(NS):
                        sh = mod[:, layer, 24 * second + j, s:s + 1]
                        ins = nc.vector.tensor_scalar(hT[:, j, s * T:(s + 1) * T], self.sq[:, j, s * T:(s + 1) * T],
                                                      scl[:, self.sub, j, s:s + 1], sh, ALU.mult, ALU.add)
                    ins.then_inc(s_h, 1)

            def h_ready(self, eng, j=DC - 1):
                eng.wait_ge(s_h, self.k * DC + j + 1)

        rwp = take(14, TT)
        yT = take(DC, TT)
        m_rw = floats[0]
        hT = take(DC, TT)
        HA = take(2, 512)
        HB = take(2, 512)
        cons[1] = take(NCONST[1])
        m_hy = floats[0]
        drop(0)
        hfw = take(64 * 2 + 2048, rows=64)
        win = take(2, 512)
        hs = take(6, 128, rows=64)
        feats = take(128, rows=33)
        assert floats[0] <= m_rw
        drop(m_hy)
        sq0 = take(DC, TT)
        pos = take(DC, T)
        hbias = take(2, 512)
        filt = take(4, 512)
        fabs = hT.rearrange("p j t -> p (j t)").rearrange("p (k c) -> p k c", k=4)
        fsum = take(2, 2, 512)
        rn = pos.rearrange("p j t -> p (j t)").rearrange("p (o c) -> p o c", o=2)
        s_silc, s_ada, s_adat, s_mod = sem("silu_c_ready"), sem("ada_copied"), sem("ada_transposed"), sem("mod_ready")
        s_hf, s_hfa, s_hfs = sem("filter_mm_done"), sem("filter_arg_ready"), sem("filter_sin_ready")
        s_fw, s_fa, s_fs, s_fn, s_ft = (sem("filter_windowed"), sem("filter_abs_ready"), sem("filter_parts_ready"),
                                        sem("filter_norm_done"), sem("filter_dft_done"))
        s_par = sem("params_loaded")
        n0 = Norm(0, sq0)
        s_x = sem("x_ready")

        ADA_TILES = [FIRST["ada0a"] + k for k in range(4)] + [FIRST["ada0b"] + k for k in range(8)] + \
            [FIRST["ada1"] + k for k in range(12)]
        adac0 = take(TT)
        adac3 = rstd[:]

        def pe_ada(pe, G):
            if G:
                pe.wait_ge(s_mod, G)
            for t in range(2):
                n = ADA_TILES[2 * G + t]
                arrived(pe, n)
                for j in range(DC):
                    for f in range(4):
                        mm = nc.tensor.matmul(ps[7][32 * f:32 * f + 32, t * P:(t + 1) * P], silc[:, j, :],
                                              tile_in(n)[:, j, f * P:(f + 1) * P], start=(j == 0), stop=(j == DC - 1),
                                              tile_position=(0, 32 * f))
                mm.then_inc(s_used, 1)

        def act_ada(act, G, buf):
            used(act, ADA_TILES[2 * G + 1])
            nc.scalar.activation(buf, ps[7][:, 0:TT], ACT.Copy).then_inc(s_ada, 1)

        def pe_ada_t(pe, G, buf):
            pe.wait_ge(s_ada, G + 1)
            for t in range(2):
                mm = nc.tensor.transpose(ps[7][:, t * P:(t + 1) * P], buf[:, t * P:(t + 1) * P], ident)
            mm.then_inc(s_adat, 1)

        def dve_ada(dve, G):
            dve.wait_ge(s_adat, G + 1)
            layer, m = G // 6, 8 * (G % 6)
            nc.vector.tensor_tensor(mod[:, layer, m:m + 8, :],
                                    ps[7][:, 0:TT].rearrange("p (m r) -> p m r", r=32)[:, :, 0:NS],
                                    pcol(f"ada_b{layer}")[:, m:m + 8].unsqueeze(2).broadcast_to([P, 8, 2]), ALU.add)\
                .then_inc(s_mod, 1)

        def used(eng, n):
            eng.wait_ge(s_used, n + 1)

        def dve_scl(dve, sub):
            layer, second = divmod(sub, 2)
            dve.wait_ge(s_mod, 6 * layer + 3 * second + 2)
            g = pcol(["gmix", "gffn"][second] + str(layer)).unsqueeze(2).broadcast_to([P, DC, 2])
            m = 24 * second + 8
            dve_link(dve, nc.vector.tensor_scalar(scl[:, sub], mod[:, layer, m:m + 8, :], 1.0, None, ALU.add))
            dve_link(dve, nc.vector.tensor_tensor(scl[:, sub], scl[:, sub], g, ALU.mult))

        with nc.Block() as block:
            @block.sync
            def _(sp):
                for dst, src in ((par[:], A["par"]), (con0[:], A["con0"]), (xT[:], A["xT"]), (pos[:], A["pos"])):
                    sp.dma_start(dst, src).then_inc(s_par, 16)
                for dst, src in ((hfw[:], A["hfw"]), (feats[:], A["feats"]), (win[:].rearrange("p a c -> p (a c)"), A["window"]),
                                 (hbias[:].rearrange("p a c -> p (a c)"), A["hbias"].partition_broadcast(P)),
                                 (cons[1], A["con1"])):
                    sp.dma_start(dst, src).then_inc(s_const, 16)
                feed(sp, 0)

            @block.gpsimd
            def _(pool):
                nc.gpsimd.memset(silc[:], 0.0).then_inc(s_silc, 1)

            @block.scalar
            def _(act):
                act.wait_ge(s_par, 64)
                act.wait_ge(s_silc, 1)
                nc.scalar.activation(silc[:, :, 0:NS], pcol("cond").rearrange("p (j s) -> p j s", s=NS), ACT.Silu)\
                    .then_inc(s_silc, 1)
                act.wait_ge(s_x, 1)
                n0.act_squares(act)
                n0.act_root(act, ps[0])
                for k in range(2):
                    act.wait_ge(s_hfa, k + 1)
                    nc.scalar.activation(hs[:, 3 * k + 2, :], hs[:, 3 * k + 1, :], ACT.Sin).then_inc(s_hfs, 1)
                for k in range(4):
                    act.wait_ge(s_fw, k + 1)
                    nc.scalar.activation(fabs[:, k, :], filt[:, k, :], ACT.Abs).then_inc(s_fa, 1)
                for G in range(2):
                    act_ada(act, G, adac0)

            @block.tensor
            def _(pe):
                pe.wait_ge(s_par, 64)
                n0.pe(pe, ps[0])
                pe.wait_ge(s_const, 16 * 5)
                nc.tensor.matmul(ps[1][0:64, 0:128], hfw[0:33, 0:64], feats[:], start=True, stop=True).then_inc(s_hf, 1)
                pe.wait_ge(s_hfs, 1)
                nc.tensor.matmul(ps[1][0:64, 0:128], hfw[:, 64:128], hs[:, 2, :], start=True, stop=True).then_inc(s_hf, 1)
                pe.wait_ge(s_hfs, 2)
                for k in range(4):
                    nc.tensor.matmul(ps[2 + k][:], hs[:, 5, :], hfw[:, 128 + 512 * k:640 + 512 * k],
                                     start=True, stop=True).then_inc(s_hf, 1)
                pe.wait_ge(s_rt, 1)
                for o in range(2):
                    for dr in range(2):
                        pe.wait_ge(s_fa, 2 * dr + o + 1)
                        mm = nc.tensor.matmul(ps[o][:], ones, fabs[:, 2 * dr + o, :], start=(dr == 0), stop=(dr == 1))
                    mm.then_inc(s_fn, 1)
                pe.wait_ge(s_fs, 4)
                for o in range(2):
                    nc.tensor.matmul(ps[2 + o][:], cc("dft_c"), fsum[:, 0, o, :], start=True, stop=True).then_inc(s_ft, 1)
                    nc.tensor.matmul(ps[4 + o][:], cc("dft_s"), fsum[:, 1, o, :], start=True, stop=True).then_inc(s_ft, 1)
                pe.wait_ge(s_silc, 2)
                for G in range(2):
                    pe_ada(pe, G)
                    pe_ada_t(pe, G, adac0)

            @block.vector
            def _(dve):
                dve.wait_ge(s_par, 64)
                nc.vector.tensor_tensor(xT[:, :, T:TT], xT[:, :, T:TT], pos[:], ALU.add).then_inc(s_x, 1)

                def sine_arg(k, bank):
                    a, r = hs[:, 3 * k, :], hs[:, 3 * k + 1, :]
                    dve_link(dve, nc.vector.tensor_scalar(a, bank, pcol(f"hfb{k + 1}")[0:64], pcol(f"hff{k + 1}")[0:64],
                                                          ALU.add, ALU.mult))
                    magic = 1.5 * 2 ** 23
                    dve_link(dve, nc.vector.tensor_scalar(r, a, 1 / (2 * math.pi), magic, ALU.mult, ALU.add))
                    dve_link(dve, nc.vector.tensor_scalar(r, r, -magic, None, ALU.add))
                    c1 = 6.28125
                    c2 = 2 * math.pi - c1
                    dve_link(dve, nc.vector.scalar_tensor_tensor(a, r, -c1, a, ALU.mult, ALU.add))
                    dve_link(dve, nc.vector.scalar_tensor_tensor(a, r, -c2, a, ALU.mult, ALU.add))
                    nc.vector.tensor_scalar(r, a, math.pi * (1 - 1e-7), -math.pi * (1 - 1e-7), ALU.min, ALU.max)\
                        .then_inc(s_hfa, 1)

                dve.wait_ge(s_hf, 1)
                sine_arg(0, ps[1][0:64, 0:128])
                dve.wait_ge(s_hf, 2)
                sine_arg(1, ps[1][0:64, 0:128])
                dve.wait_ge(s_const, 16 * 5)
                for k in range(4):
                    dve.wait_ge(s_hf, 3 + k)
                    nc.vector.tensor_tensor(filt[:, k, :], ps[2 + k][:], win[:, k // 2, :], ALU.mult).then_inc(s_fw, 1)
                dve.wait_ge(s_fw, 4)
                for o in range(2):
                    nc.vector.tensor_tensor(fsum[:, 0, o, :], filt[:, o, :], filt[:, 2 + o, :], ALU.add).then_inc(s_fs, 1)
                    nc.vector.tensor_tensor(fsum[:, 1, o, :], filt[:, o, :], filt[:, 2 + o, :], ALU.subtract)\
                        .then_inc(s_fs, 1)
                for o in range(2):
                    dve.wait_ge(s_fn, o + 1)
                    dve_link.last(dve, nc.vector.reciprocal(rn[:, o, :], ps[o][:]))
                dve_link.sync(dve)
                for o in range(2):
                    dve.wait_ge(s_ft, 2 * o + 2)
                    dve_link(dve, nc.vector.tensor_tensor(HA[:, o, :], ps[2 + o][:], rn[:, o, :], ALU.mult))
                    dve_link.last(dve, nc.vector.tensor_tensor(HA[:, o, :], HA[:, o, :], hbias[:, o, :], ALU.add))
                    dve_link.last(dve, nc.vector.tensor_tensor(HB[:, o, :], ps[4 + o][:], rn[:, o, :], ALU.mult))
                dve_link.sync(dve)
                for G in range(2):
                    dve_ada(dve, G)
                dve_scl(dve, 0)
                n0.dve(dve)

        drop(m_hy)
        u = take(12, TT)
        m_u = floats[0]
        pad = take(4, NS, T + 2)
        tmp = take(2, NS, T)
        mus = take(2, 14)
        s_p, s_pad, s_pz, s_pc = sem("proj_done"), sem("proj_padded"), sem("pads_zeroed"), sem("pad_consumed")
        mask_f = take(2 * LEVELS * P + 6 * P)
        EC = 26

        with nc.Block() as block:
            @block.sync
            def _(sp):
                sp.dma_start(mask_f, A["masks"]).then_inc(s_par, 16)
                feed(sp, FIRST["even_in"] + EVEN_IN_TILES)

            @block.gpsimd
            def _(pool):
                nc.gpsimd.memset(pad[:], 0.0).then_inc(s_pz, 1)
                pool.wait_ge(s_par, 80)
                nc.gpsimd.tensor_copy(masks[:], mask_f)

            @block.scalar
            def _(act):
                act.wait_ge(s_pz, 1)
                for m in range(EC):
                    act.wait_ge(s_p, m + 1)
                    if m >= 4:
                        act.wait_ge(s_pc, m - 3)
                    rows = 96 if m == EC - 1 else P
                    src = ps[m % 4][0:rows, 0:TT].rearrange("p (s t) -> p s t", s=NS)
                    nc.scalar.activation(pad[0:rows, m % 4, :, 1:T + 1], src, ACT.Copy).then_inc(s_pad, 1)

            @block.tensor
            def _(pe):
                for m in range(EC):
                    n = FIRST["even_in"] + m // 4
                    if m % 4 == 0:
                        arrived(pe, n)
                    if m >= 4:
                        pe.wait_ge(s_pad, m - 3)
                    rows = 96 if m == EC - 1 else P
                    f = m % 4
                    for j in range(DC):
                        mm = nc.tensor.matmul(ps[m % 4][0:rows, 0:TT], tile_in(n)[:, j, f * P:f * P + rows], hT[:, j, :],
                                              start=(j == 0), stop=(j == DC - 1))
                    mm.then_inc(s_p, 1)
                    if f == 3 or m == EC - 1:
                        pe.wait_ge(s_p, m + 1)
                        pe.sem_inc(s_used, 1)

            @block.vector
            def _(dve):
                dve_link(dve, nc.vector.tensor_scalar(mus[:, 0, :], pcol("mu"), -1.0, 1.0, ALU.mult, ALU.add))
                dve_link(dve, nc.vector.tensor_scalar(mus[:, 1, :], pcol("mu"), 0.5, None, ALU.mult))
                for m in range(EC):
                    dve.wait_ge(s_pad, m + 1)
                    rows = 96 if m == EC - 1 else P
                    left, mid, right = (pad[0:rows, m % 4, :, k:k + T] for k in range(3))
                    a = tmp[0:rows, 0]
                    if m < 12:
                        out = u[:, m, :].rearrange("p (s t) -> p s t", s=NS)
                        w = pcol("hyw")
                        dve_link(dve, nc.vector.tensor_scalar(a, mid, w[:, 12 + m:13 + m], pcol("hyb", m, 1), ALU.mult, ALU.add))
                        dve_link(dve, nc.vector.scalar_tensor_tensor(out, left, w[:, m:m + 1], a, ALU.mult, ALU.add))
                        nc.vector.scalar_tensor_tensor(out, right, w[:, 24 + m:25 + m], out, ALU.mult, ALU.add)\
                            .then_inc(s_pc, 1)
                        dve.wait_ge(s_pc, m + 1)
                    else:
                        q = m - 12
                        out = rwp[0:rows, q, :].rearrange("p (s t) -> p s t", s=NS)
                        b = tmp[0:rows, 1]
                        dve_link.last(dve, nc.vector.tensor_tensor(a, left, right, ALU.add))
                        dve_link(dve, nc.vector.tensor_scalar(b, mid, mus[0:rows, 0, q:q + 1], None, ALU.mult))
                        nc.vector.scalar_tensor_tensor(out, a, mus[0:rows, 1, q:q + 1], b, ALU.mult, ALU.add)\
                            .then_inc(s_pc, 1)
                        dve.wait_ge(s_pc, m + 1)

        drop(m_u)
        vt = hT.rearrange("p j t -> p (j t)").rearrange("p (g s c) -> p g s c", g=2, s=NS)
        za = take(4, 512)
        sp_ab = take(2, 512)
        adac2 = take(TT)
        s_tr, s_vt, s_z, s_y, s_zt = (sem("hy_transposed"), sem("hy_token_major"), sem("hy_dft_done"),
                                      sem("hy_spectrum_ready"), sem("hy_time_done"))
        s_z1 = sem("hy_gated")

        with nc.Block() as block:
            @block.sync
            def _(sp):
                feed(sp, FIRST["ada0b"] + 8)

            @block.gpsimd
            def _(pool):
                pass

            @block.scalar
            def _(act):
                for k in range(4):
                    act.wait_ge(s_tr, k + 1)
                    nc.scalar.activation(vt[:, k // 2, k % 2, :], ps[k][:], ACT.Copy).then_inc(s_vt, 1)
                for k in range(4):
                    act_ada(act, 2 + k, adac2)

            @block.tensor
            def _(pe):
                for k in range(4):
                    g, s = divmod(k, 2)
                    for c in range(HYC):
                        mm = nc.tensor.transpose(ps[k][:, c * P:(c + 1) * P], u[:, 4 * g + c, s * T:(s + 1) * T], ident)
                    mm.then_inc(s_tr, 1)
                for o in range(2):
                    for s in range(NS):
                        k = 2 * o + s
                        if o == 0:
                            pe.wait_ge(s_vt, s + 1)
                        else:
                            pe.wait_ge(s_z1, s + 1)
                        if k >= 1:
                            pe.wait_ge(s_y, k)
                        if k == 0:
                            pe.wait_ge(s_vt, 2)
                        nc.tensor.matmul(ps[4][:], cc("dft_c"), vt[:, 0, s, :], start=True, stop=True)
                        nc.tensor.matmul(ps[5][:], cc("dft_s"), vt[:, 0, s, :], start=True, stop=True).then_inc(s_z, 1)
                        pe_ada(pe, 2 + k)
                        pe.wait_ge(s_y, k + 1)
                        if o == 0:
                            nc.tensor.matmul(ps[s][:], cc("inv_c"), sp_ab[:, 0, :], start=True, stop=False)
                            nc.tensor.matmul(ps[s][:], cc("inv_s"), sp_ab[:, 1, :], start=False, stop=True)\
                                .then_inc(s_zt, 1)
                        else:
                            for c in range(HYC):
                                out = ps[s][:, c * P:(c + 1) * P]
                                nc.tensor.matmul(out, sp_ab[:, 0, c * P:(c + 1) * P], cc("inv_c"), start=True, stop=False)
                                mm = nc.tensor.matmul(out, sp_ab[:, 1, c * P:(c + 1) * P], cc("inv_s"),
                                                      start=False, stop=True)
                            mm.then_inc(s_zt, 1)
                        pe_ada_t(pe, 2 + k, adac2)

            @block.vector
            def _(dve):
                for o in range(2):
                    for s in range(NS):
                        k = 2 * o + s
                        dve.wait_ge(s_z, k + 1)
                        for i, (bank, h) in enumerate(((ps[4], HA), (ps[5], HB), (ps[4], HB), (ps[5], HA))):
                            dve_link.last(dve, nc.vector.tensor_tensor(za[:, i, :], bank[:], h[:, o, :], ALU.mult))
                        dve_link.sync(dve)
                        if k >= 1:
                            dve.wait_ge(s_zt, k)
                        dve_link(dve, nc.vector.tensor_tensor(sp_ab[:, 0, :], za[:, 0, :], za[:, 1, :], ALU.subtract))
                        nc.vector.tensor_tensor(sp_ab[:, 1, :], za[:, 2, :], za[:, 3, :], ALU.add).then_inc(s_y, 1)
                        dve.wait_ge(s_zt, k + 1)
                        if o == 0:
                            dve.wait_ge(s_vt, 4)
                            nc.vector.tensor_tensor(vt[:, 0, s, :], ps[s][:], vt[:, 1, s, :], ALU.mult).then_inc(s_z1, 1)
                        else:
                            dve_link(dve, nc.vector.tensor_tensor(
                                yT[:, 0:4, s * T:(s + 1) * T], ps[s][:].rearrange("p (c t) -> p c t", c=4),
                                u[:, 8:12, s * T:(s + 1) * T], ALU.mult))
                        dve_ada(dve, 2 + k)
                dve_scl(dve, 1)
        s_id, s_T, s_U = ([sem(f"{n}{g}") for g in range(2)] for n in ("identity_set", "T_level_done", "U_level_done"))
        s_X, s_Xs, s_TX, s_XU = ([sem(f"{n}{g}") for g in range(2)] for n in ("AT_done", "AT_copied", "TAT_done", "TATt_done"))
        NT, NU = (LEVELS - 1, LEVELS), (LEVELS, LEVELS - 1)
        NTX, NXU = (LEVELS - 2, LEVELS - 1), (LEVELS - 1, LEVELS - 2)

        class Inversion:
            def __init__(self):
                self.T = [take(4, T) for _ in range(2)]
                self.U = [take(4, T) for _ in range(2)]
                self.X = [take(4, T) for _ in range(2)]
                self.final = [self.U[0], self.T[1]]

            def pool_reset(self, pool, g):
                eye = ident.unsqueeze(1).broadcast_to([P, 4, T])
                nc.gpsimd.tensor_copy(self.T[g], eye).then_inc(s_id[g], 1)
                nc.gpsimd.tensor_copy(self.U[g], eye).then_inc(s_id[g], 1)

            def level_mask(self, upper, l):
                return lvl[:, upper, l, :].unsqueeze(1).broadcast_to([P, 4, T])

            def dve_first(self, dve, r, g, low, up):
                dve.wait_ge(s_id[g], 2 * (r + 1))
                nc.vector.copy_predicated(self.T[g], self.level_mask(0, 0), low).then_inc(s_T[g], 1)
                nc.vector.copy_predicated(self.U[g], self.level_mask(1, 0), up).then_inc(s_U[g], 1)

            def pe_level(self, pe, r, l, up):
                for g in range(2):
                    pe.wait_ge(s_T[g], r * NT[g] + l)
                    for q in range(4):
                        mm = nc.tensor.matmul(ps[g][:, q * T:(q + 1) * T], up[g][:, q], self.T[g][:, q], start=True, stop=True)
                    mm.then_inc(s_X[g], 1)
                for g in range(2):
                    pe.wait_ge(s_U[g], r * NU[g] + l)
                    pe.wait_ge(s_Xs[g], r * (LEVELS - 1) + l)
                    if l < LEVELS - 1 or g == 1:
                        for q in range(4):
                            mm = nc.tensor.matmul(ps[2 + g][:, q * T:(q + 1) * T], self.U[g][:, q], self.X[g][:, q],
                                                  start=True, stop=True)
                        mm.then_inc(s_TX[g], 1)
                    if l < LEVELS - 1 or g == 0:
                        for q in range(4):
                            mm = nc.tensor.matmul(ps[4 + g][:, q * T:(q + 1) * T], self.X[g][:, q], self.U[g][:, q],
                                                  start=True, stop=True)
                        mm.then_inc(s_XU[g], 1)

            def act_level(self, act, r, l):
                for g in range(2):
                    act.wait_ge(s_X[g], r * (LEVELS - 1) + l)
                    nc.scalar.activation(self.X[g].rearrange("p q t -> p (q t)"), ps[g][:], ACT.Copy).then_inc(s_Xs[g], 1)

            def dve_level(self, dve, r, l):
                for g in range(2):
                    if l < LEVELS - 1 or g == 1:
                        dve.wait_ge(s_TX[g], r * NTX[g] + l)
                        dve.wait_ge(s_T[g], r * NT[g] + l)
                        nc.vector.copy_predicated(self.T[g], self.level_mask(0, l),
                                                  ps[2 + g][:].rearrange("p (q t) -> p q t", q=4)).then_inc(s_T[g], 1)
                    if l < LEVELS - 1 or g == 0:
                        dve.wait_ge(s_XU[g], r * NXU[g] + l)
                        dve.wait_ge(s_U[g], r * NU[g] + l)
                        nc.vector.copy_predicated(self.U[g], self.level_mask(1, l),
                                                  ps[4 + g][:].rearrange("p (q t) -> p q t", q=4)).then_inc(s_U[g], 1)

            def pe_final(self, pe, r, g):
                pe.wait_ge(s_U[0] if g == 0 else s_T[1], (r + 1) * LEVELS)

        drop(m_rw)
        lora = take(512)
        g2 = take(512, rows=96)
        s0 = take(2, 4, 64)
        m_keep = floats[0]
        inv = Inversion()
        AT = [take(4, 4, T) for _ in range(2)]
        Ab = [take(4, T) for _ in range(2)]
        ar = [take(2, TT) for _ in range(2)]
        bk = take(2, TT)
        bkt = [take(2, T) for _ in range(2)]
        vtok = take(NS, T)
        Q, W = take(TT), take(TT)
        sg, av, kd = take(TT), take(TT), take(TT)
        kk, ksq, knm = take(TT), Q, W
        bon = take(TT)
        Gs = [inv.X[g][:, 0:2, :].rearrange("p a (b v) -> p (a b) v", b=2) for g in range(2)]
        Zs = [inv.X[g][:, 2:4, :].rearrange("p a (b v) -> p (a b) v", b=2) for g in range(2)]
        s0s = [take(2, RWN) for _ in range(2)]
        hp = [take(NS) for _ in range(2)]
        eh = [take(NS) for _ in range(2)]
        sst = s0
        y4 = yT[:, 4:8, :].rearrange("p c t -> p (c t)")
        std = AT[0].rearrange("p q k t -> p (q k t)")[:, 0:1024]
        ybuf = AT[0].rearrange("p q k t -> p (q k t)")[:, 1024:2048]
        s_rwc = sem("rwkv_params_loaded")
        s_zero = sem("scores_zeroed")
        s_kr, s_ksq, s_kss, s_krt = sem("kk_raw_ready"), sem("kk_squared"), sem("kk_sumsq_done"), sem("kk_root_done")
        s_tanh, s_sigg = sem("lora_tanh_done"), sem("lora_gate_done")
        s_lor, s_sg, s_Q, s_exp, s_unit = (sem("lora_done"), sem("sigmoids_done"), sem("decay_sums_ready"),
                                           sem("decays_ready"), sem("unit_ready"))
        s_gen, s_sel, s_tk, s_tks = sem("scores_done"), sem("scores_masked"), sem("tok_major_done"), sem("tok_major_copied")
        s_G, s_Gs, s_Z, s_Zs = sem("rhs_done"), sem("rhs_copied"), sem("solved"), sem("solution_copied")
        s_Y, s_Ys, s_S, s_Ss = sem("rw_out_done"), sem("rw_out_copied"), sem("rw_state_done"), sem("rw_state_copied")
        s_s0, s_bon, s_bss, s_bons = sem("s0_scaled"), sem("bonus_arg_ready"), sem("bonus_sum_done"), sem("bonus_ready")
        s_mn, s_yc, s_ysq, s_vr, s_std = (sem("ln_mean_done"), sem("ln_centred"), sem("ln_squared"), sem("ln_var_done"),
                                          sem("ln_root_done"))
        s_gg, s_stored = sem("gate_lora_done"), sem("state_stored")
        v3 = lambda ap: ap.rearrange("p (s t) -> p s t", s=NS)

        def ada_groups(c, g):
            k = {(0, 0): 0, (0, 1): 1, (1, 0): 2, (1, 1): 3, (2, 0): 4, (3, 0): 5}.get((c, g))
            return [] if k is None else [6 + k]

        with nc.Block() as block:
            @block.sync
            def _(sp):
                for dst, src in ((lora, A["lora"]), (g2, A["g2"]), (s0, A["s0rw"])):
                    sp.dma_start(dst, src).then_inc(s_rwc, 16)
                feed(sp, FIRST["ada1"] + 12)
                sp.wait_ge(s_Ss, 8)
                sp.dma_start(O["srw"], sst).then_inc(s_stored, 16)
                sp.wait_ge(s_stored, 16)

            @block.gpsimd
            def _(pool):
                for g in range(2):
                    nc.gpsimd.memset(AT[g], 0.0).then_inc(s_zero, 1)
                    nc.gpsimd.memset(Ab[g], 0.0).then_inc(s_zero, 1)
                    nc.gpsimd.memset(s0s[g], 0.0).then_inc(s_zero, 1)
                for c in range(RWC):
                    for g in range(2):
                        if c:
                            pool.wait_ge(s_Z, 2 * c)
                        inv.pool_reset(pool, g)

            @block.scalar
            def _(act):
                nc.scalar.activation(rwp[0:64, 12, :], rwp[0:64, 12, :], ACT.Tanh).then_inc(s_tanh, 1)
                nc.scalar.activation(rwp[0:96, 13, :], rwp[0:96, 13, :], ACT.Sigmoid).then_inc(s_sigg, 1)
                for c in range(RWC):
                    act.wait_ge(s_kr, c + 1)
                    nc.scalar.activation(ksq, kk, ACT.Square).then_inc(s_ksq, 1)
                    act.wait_ge(s_kss, c + 1)
                    nc.scalar.activation(knm, ps[7][:, 256:512], ACT.Sqrt).then_inc(s_krt, 1)
                    act.wait_ge(s_tk, 3 * c + 1)
                    if c:
                        act.wait_ge(s_S, 2 * c)
                    nc.scalar.activation(vtok.rearrange("p s t -> p (s t)"), ps[7][:, 256:512], ACT.Copy).then_inc(s_tks, 1)
                    for g in range(2):
                        k = 2 * c + g
                        act.wait_ge(s_lor, k + 1)
                        if k:
                            act.wait_ge(s_unit, k)
                        nc.scalar.activation(sg, ps[6][:, 0:TT], ACT.Sigmoid, bias=pcol("w0", 4 * g + c, 1)).then_inc(s_sg, 1)
                        nc.scalar.activation(av, ps[5][:, TT:2 * TT], ACT.Sigmoid, bias=pcol("a0", 4 * g + c, 1))\
                            .then_inc(s_sg, 1)
                        for G in ada_groups(c, g):
                            act_ada(act, G, adac3)
                        act.wait_ge(s_Q, k + 1)
                        if k:
                            act.wait_ge(s_gen, k)
                        if c:
                            act.wait_ge(s_Y, c)
                        fwd = g == 0
                        nc.scalar.activation(ar[g][:, 0, :], W if fwd else Q, ACT.Exp, scale=-KAPPA if fwd else KAPPA)\
                            .then_inc(s_exp, 1)
                        nc.scalar.activation(ar[g][:, 1, :], Q if fwd else W, ACT.Exp, scale=-KAPPA if fwd else KAPPA)\
                            .then_inc(s_exp, 1)
                        nc.scalar.activation(bk[:, 1, :], Q if fwd else W, ACT.Exp, scale=KAPPA if fwd else -KAPPA)\
                            .then_inc(s_exp, 1)
                        nc.scalar.activation(eh[g], hp[g], ACT.Exp, scale=-KAPPA).then_inc(s_exp, 1)
                        act.wait_ge(s_tk, 3 * c + 2 + g)
                        nc.scalar.activation(bkt[g].rearrange("p a t -> p (a t)"), ps[6][:, TT:2 * TT], ACT.Copy).then_inc(s_tks, 1)
                    for l in range(1, LEVELS):
                        inv.act_level(act, c, l)
                    for g in range(2):
                        act.wait_ge(s_G, 2 * c + g + 1)
                        nc.scalar.activation(Gs[g].rearrange("p q v -> p (q v)"), ps[g][:, 0:TT], ACT.Copy).then_inc(s_Gs, 1)
                act.wait_ge(s_yc, 1)
                nc.scalar.activation(ybuf, y4, ACT.Square).then_inc(s_ysq, 1)
                for h in range(2):
                    act.wait_ge(s_vr, h + 1)
                    nc.scalar.activation(std[:, 512 * h:512 * h + 512], ps[2 + h][:], ACT.Sqrt, scale=1 / 64.0,
                                         bias=cc("lneps")).then_inc(s_std, 1)

            @block.tensor
            def _(pe):
                pe.wait_ge(s_rwc, 48)
                pe.wait_ge(s_tanh, 1)
                for c in range(RWC):
                    pe.wait_ge(s_ksq, c + 1)
                    pe.wait_ge(s_mod, 6 + (2 * c if c < 3 else 5))
                    nc.tensor.matmul(ps[7][:, 256:512], bones, ksq, start=True, stop=True).then_inc(s_kss, 1)
                    if c:
                        pe.wait_ge(s_U[1], c * NU[1])
                        pe.wait_ge(s_Ys, c)
                        pe.wait_ge(s_bons, c)
                    pe.wait_ge(s_krt, c + 1)
                    for s in range(NS):
                        mm = nc.tensor.transpose(ps[7][:, TT + s * T:TT + (s + 1) * T], rwp[:, 8 + c, s * T:(s + 1) * T], ident)
                    mm.then_inc(s_tk, 1)
                    for g in range(2):
                        k = 2 * c + g
                        if g:
                            pe.wait_ge(s_sel, 6 * k)
                            pe.wait_ge(s_tks, 3 * c + 2)
                        for i in range(2):
                            b = 64 * i + 32 * g
                            mm = nc.tensor.matmul(ps[6 - i][:, i * TT:(i + 1) * TT], lora[b:b + 32, c * P:(c + 1) * P],
                                                  rwp[b:b + 32, 12, :], start=True, stop=True, tile_position=(b, 0))
                        mm.then_inc(s_lor, 1)
                        if g == 0:
                            pe.wait_ge(s_tks, 3 * c + 1)
                        for G in ada_groups(c, g):
                            pe_ada(pe, G)
                        pe.wait_ge(s_unit, k + 1)
                        if k:
                            pe.wait_ge(s_sel, 6 * k)
                        if c and g == 0:
                            pe.wait_ge(s_Zs, 2 * c)
                            pe.wait_ge(s_Ss, 2 * c)
                        for q in range(4):
                            s, hh = divmod(q, 2)
                            rows, tok = slice(64 * hh, 64 * hh + 64), slice(s * T, (s + 1) * T)
                            for i in range(2):
                                nc.tensor.matmul(ps[q][:, i * TT:(i + 1) * TT].rearrange("p (a t) -> p a t", a=2),
                                                 bk[rows, i, tok], ar[g][rows, :, tok], start=True, stop=True)
                            mm = nc.tensor.matmul(ps[4 + hh][:, s * T:(s + 1) * T], ar[g][rows, 0, tok], bk[rows, 0, tok],
                                                  start=True, stop=True)
                        mm.then_inc(s_gen, 1)
                        for G in ada_groups(c, g):
                            pe_ada_t(pe, G, adac3)
                        pe.wait_ge(s_tks, 3 * c + 1 + g)
                        for i in range(2):
                            mm = nc.tensor.transpose(ps[6][:, TT + i * T:TT + (i + 1) * T], bk[:, i, 0:T], ident)
                        mm.then_inc(s_tk, 1)
                    pe.wait_ge(s_tks, 3 * c + 3)
                    pe.wait_ge(s_sel, 6 * (2 * c + 2))
                    up = [AT[0][:, :, 0, :], Ab[1]]
                    for l in range(1, LEVELS):
                        inv.pe_level(pe, c, l, up)
                    for g in range(2):
                        if g == 0:
                            pe.wait_ge(s_s0, 4 * c + 4)
                        for s in range(NS):
                            if s:
                                nc.tensor.matmul(ps[g][:, T:2 * T].rearrange("p (h v) -> p h v", h=2), ar[g][:, 0, T:TT],
                                                 s0s[g], start=True, stop=False)
                            for hh in range(2):
                                q = 2 * s + hh
                                mm = nc.tensor.matmul(ps[g][:, q * RWN:(q + 1) * RWN], AT[g][:, q, 2, :],
                                                      vtok[:, s, 64 * hh:64 * hh + 64], start=(s == 0), stop=(s == 0 or hh == 1))
                        mm.then_inc(s_G, 1)
                    for g in range(2):
                        inv.pe_final(pe, c, g)
                        pe.wait_ge(s_Gs, 2 * c + g + 1)
                        for q in range(4):
                            mm = nc.tensor.matmul(ps[g][:, TT + q * RWN:TT + (q + 1) * RWN], inv.final[g][:, q], Gs[g][:, q, :],
                                                  start=True, stop=True)
                        mm.then_inc(s_Z, 1)
                    pe.wait_ge(s_Zs, 2 * c + 2)
                    for q in range(4):
                        s, hh = divmod(q, 2)
                        rows, tok = slice(64 * hh, 64 * hh + 64), slice(s * T, (s + 1) * T)
                        out = ps[6][rows, tok]
                        for g in range(2):
                            nc.tensor.matmul(out, Zs[g][:, q, :], AT[g][:, q, 1, :], start=(g == 0), stop=False)
                            if s:
                                nc.tensor.matmul(out, s0s[g][:, hh, :], ar[g][:, 1, tok], start=False, stop=False)
                            mm = nc.tensor.matmul(out, vtok[:, s, rows], AT[g][:, q, 3, :], start=False, stop=(g == 1))
                    mm.then_inc(s_Y, 1)
                    for g in range(2):
                        nc.tensor.matmul(ps[2 + g][:, 0:T], bkt[g][:, 0, :], Zs[g][:, 0:2, :].rearrange("p q v -> p (q v)"),
                                         start=True, stop=False)
                        nc.tensor.matmul(ps[2 + g][:, 0:T], bkt[g][:, 1, :], vtok[:, 0, :], start=False, stop=True)\
                            .then_inc(s_S, 1)
                    pe.wait_ge(s_bon, c + 1)
                    pe.wait_ge(s_Ys, c + 1)
                    nc.tensor.matmul(ps[6][:, TT:2 * TT], bones, bon, start=True, stop=True).then_inc(s_bss, 1)
                pe.wait_ge(s_Ys, RWC)
                pe.wait_ge(s_Ss, 2 * RWC)
                for h in range(2):
                    nc.tensor.matmul(ps[h][:], bones, y4[:, 512 * h:512 * h + 512], start=True, stop=True).then_inc(s_mn, 1)
                pe.wait_ge(s_sigg, 1)
                for c in range(RWC):
                    mm = nc.tensor.matmul(ps[4 + c // 2][:, (c % 2) * TT:(c % 2 + 1) * TT], g2[:, c * P:(c + 1) * P],
                                          rwp[0:96, 13, :], start=True, stop=True)
                mm.then_inc(s_gg, 1)
                pe.wait_ge(s_ysq, 1)
                for h in range(2):
                    nc.tensor.matmul(ps[2 + h][:], bones, ybuf[:, 512 * h:512 * h + 512], start=True, stop=True)\
                        .then_inc(s_vr, 1)

            @block.vector
            def _(dve):
                V = nc.vector
                dve.wait_ge(s_rwc, 48)
                dve.wait_ge(s_zero, 6)
                for c in range(RWC):
                    r, kc, vc = (rwp[:, i + c, :] for i in (0, 4, 8))
                    if c:
                        dve.wait_ge(s_kss, c)
                    V.tensor_scalar(kk, kc, pcol("kk", c, 1), None, ALU.mult).then_inc(s_kr, 1)
                    dve.wait_ge(s_krt, c + 1)
                    dve_link(dve, V.tensor_scalar(knm, knm, 1e-12, None, ALU.max))
                    dve_link(dve, V.reciprocal(knm, knm))
                    dve_link(dve, V.tensor_tensor(kk, kk, knm, ALU.mult))
                    for g in range(2):
                        k = 2 * c + g
                        dve.wait_ge(s_sg, 2 * (k + 1))
                        if c:
                            dve.wait_ge(s_exp, 4 * k)
                        dve_link(dve, V.tensor_tensor_scan(Q, cc("reset"), sg, 0.0, ALU.mult, ALU.add))
                        dve_link(dve, V.tensor_scalar(hp[g], v3(Q)[:, :, T - 1], 0.5, None, ALU.mult))
                        dve_link(dve, V.tensor_tensor(v3(Q), v3(Q), hp[g].unsqueeze(2).broadcast_to([P, NS, T]), ALU.subtract))
                        V.tensor_tensor(W, Q, sg, ALU.subtract).then_inc(s_Q, 1)
                        dve_link(dve, V.tensor_scalar(kd, av, -1.0, pcol("ka", c, 1), ALU.add, ALU.mult))
                        dve_link(dve, V.scalar_tensor_tensor(kd, kd, 1.0, kc, ALU.add, ALU.mult))
                        if g == 0:
                            if c:
                                dve.wait_ge(s_bss, c)
                            dve_link.last(dve, V.tensor_copy(bon, kd))
                        else:
                            dve_link(dve, V.tensor_tensor(bon, bon, kd, ALU.add))
                        dve_link(dve, V.tensor_tensor(av, av, kk, ALU.mult))
                        dve.wait_ge(s_exp, 4 * (k + 1))
                        if k:
                            dve.wait_ge(s_tk, 3 * ((k - 1) // 2) + 2 + (k - 1) % 2)
                        dve_link.last(dve, V.scalar_tensor_tensor(ar[g][:, 0, :], ar[g][:, 0, :], -1.0, kk, ALU.mult, ALU.mult))
                        dve_link.last(dve, V.tensor_tensor(ar[g][:, 1, :], ar[g][:, 1, :], r, ALU.mult))
                        dve_link(dve, V.tensor_tensor(bk[:, 0, :], bk[:, 1, :], av, ALU.mult))
                        dve_link.sync(dve)
                        V.tensor_tensor(bk[:, 1, :], bk[:, 1, :], kd, ALU.mult).then_inc(s_unit, 1)
                        if c:
                            dve.wait_ge(s_Y, c)
                        for hh in range(2):
                            rows = slice(64 * hh, 64 * hh + 64)
                            V.tensor_scalar(s0s[g][rows, hh, :], s0[rows, g, c, :], eh[g][rows, 1:2], None, ALU.mult)\
                                .then_inc(s_s0, 1)
                        dve.wait_ge(s_gen, k + 1)
                        if c:
                            dve.wait_ge(s_Y, c)
                        for q in range(4):
                            V.copy_predicated(AT[g][:, q].rearrange("p (i a) t -> p i a t", i=2),
                                              selm[:, 2 * g:2 * g + 2, :].unsqueeze(1).broadcast_to([P, 2, 2, T]),
                                              ps[q][:].rearrange("p (i a t) -> p i a t", i=2, a=2)).then_inc(s_sel, 1)
                        for hh in range(2):
                            V.copy_predicated(Ab[g][:, hh:4:2, :], selm[:, 4 + g, :].unsqueeze(1).broadcast_to([P, 2, T]),
                                              v3(ps[4 + hh][:, 0:TT])).then_inc(s_sel, 1)
                        dve.wait_ge(s_sel, 6 * (k + 1))
                        low, up = (Ab[0], AT[0][:, :, 0, :]) if g == 0 else (AT[1][:, :, 0, :], Ab[1])
                        inv.dve_first(dve, c, g, low, up)
                        for G in ada_groups(c, g):
                            dve_ada(dve, G)
                    dve_link(dve, V.scalar_tensor_tensor(bon, bon, pcol("rk", c, 1), r, ALU.mult, ALU.mult))
                    V.tensor_copy(bon, bon).then_inc(s_bon, 1)
                    for l in range(1, LEVELS):
                        inv.dve_level(dve, c, l)
                    for g in range(2):
                        dve.wait_ge(s_Z, 2 * c + g + 1)
                        V.tensor_copy(Zs[g].rearrange("p q v -> p (q v)"), ps[g][:, TT:2 * TT]).then_inc(s_Zs, 1)
                    dve.wait_ge(s_Y, c + 1)
                    V.tensor_copy(yT[:, 4 + c, :], ps[6][:, 0:TT]).then_inc(s_Ys, 1)
                    for g in range(2):
                        dve.wait_ge(s_S, 2 * c + g + 1)
                        for hh in range(2):
                            rows = slice(64 * hh, 64 * hh + 64)
                            ins = V.tensor_scalar(sst[rows, g, c, :], ps[2 + g][rows, 64 * hh:64 * hh + 64],
                                                  eh[g][rows, 0:1], None, ALU.mult)
                        ins.then_inc(s_Ss, 1)
                    dve.wait_ge(s_bss, c + 1)
                    V.tensor_tensor(r, ps[6][:, TT:2 * TT], vc, ALU.mult).then_inc(s_bons, 1)
                dve.wait_ge(s_mn, 2)
                for h in range(2):
                    ins = V.scalar_tensor_tensor(y4[:, 512 * h:512 * h + 512], ps[h][:], -1 / 64.0, y4[:, 512 * h:512 * h + 512],
                                                 ALU.mult, ALU.add)
                    if h == 0:
                        dve_link.last(dve, ins)
                dve_link.sync(dve)
                ins.then_inc(s_yc, 1)
                dve.wait_ge(s_yc, 1)
                for h in range(2):
                    dve.wait_ge(s_std, h + 1)
                    dve_link.last(dve, V.reciprocal(std[:, 512 * h:512 * h + 512], std[:, 512 * h:512 * h + 512]))
                dve_link.sync(dve)
                dve_link(dve, V.tensor_tensor(y4, y4, std, ALU.mult))
                for c in range(RWC):
                    dve_link.last(dve, V.tensor_scalar(yT[:, 4 + c, :], yT[:, 4 + c, :], pcol("lnw", c, 1), pcol("lnb", c, 1),
                                                       ALU.mult, ALU.add))
                dve_link.sync(dve)
                dve.wait_ge(s_bons, RWC)
                dve_link(dve, V.tensor_tensor(yT[:, 4:8, :], yT[:, 4:8, :], rwp[:, 0:4, :], ALU.add))
                dve.wait_ge(s_gg, 1)
                for h in range(2):
                    dve_link.last(dve, V.tensor_tensor(y4[:, 512 * h:512 * h + 512], y4[:, 512 * h:512 * h + 512], ps[4 + h][:],
                                                       ALU.mult))
                dve_link.sync(dve)
                dve_scl(dve, 2)
                dve_scl(dve, 3)
        def pe_out_proj(pe, first, src, sig):
            for d in range(DC):
                if d == 0:
                    arrived(pe, first)
                    arrived(pe, first + 1)
                for j in range(DC):
                    mm = nc.tensor.matmul(ps[d // 2][:, (d % 2) * TT:(d % 2 + 1) * TT],
                                          tile_out(first + j // 4)[:, j % 4, d * P:(d + 1) * P], src[:, j, :],
                                          start=(j == 0), stop=(j == DC - 1))
                if d % 2:
                    mm.then_inc(sig, 1)

        def dve_residual(dve, sig, count, layer, m):
            for b in range(4):
                if count is not None:
                    dve.wait_ge(sig, count + b + 1)
                for d in (2 * b, 2 * b + 1):
                    for s in range(NS):
                        x = xT[:, d, s * T:(s + 1) * T]
                        ins = nc.vector.scalar_tensor_tensor(x, ps[b][:, (d % 2) * TT + s * T:(d % 2) * TT + (s + 1) * T],
                                                             mod[:, layer, m + d, s:s + 1], x, ALU.mult, ALU.add)
                        if d < DC - 1 or s == 0:
                            dve_link.last(dve, ins)
            dve_link.sync(dve)
            ins.then_inc(s_x, 1)

        drop(m_rw)
        hT = take(DC, TT)
        sq1 = take(DC, TT)
        act4 = take(2, 4, TT)
        sgt = take(2, TT)
        n1 = Norm(1, sq1)
        s_op, s_gu, s_sil, s_act, s_ffn = (sem("out_proj_done"), sem("gate_up_done"), sem("silu_done"), sem("act_ready"),
                                           sem("ffn_done"))
        FC = FF // P
        with nc.Block() as block:
            @block.sync
            def _(sp):
                feed(sp, FIRST["ffn"] + 17)

            @block.gpsimd
            def _(pool):
                pass

            @block.scalar
            def _(act):
                act.wait_ge(s_x, 2)
                n1.act_squares(act)
                n1.act_root(act, ps[4])
                for m in range(FC):
                    act.wait_ge(s_gu, m + 1)
                    if m >= 2:
                        act.wait_ge(s_act, m - 1)
                    nc.scalar.activation(sgt[:, m % 2, :], ps[4 + m % 4][:, 0:TT], ACT.Silu).then_inc(s_sil, 1)

            @block.tensor
            def _(pe):
                pe_out_proj(pe, FIRST["even_out"], yT, s_op)
                pe.wait_ge(s_op, 4)
                pe.sem_inc(s_used, 2)
                n1.pe(pe, ps[4])
                n1.h_ready(pe)
                m = 0
                for k in range(FFN_OUT_TILES):
                    for n in range(2):
                        if 2 * k + n == FFN_IN_TILES:
                            continue
                        tile = FIRST["ffn"] + 3 * k + n
                        arrived(pe, tile)
                        w = tile_in(tile)
                        for _ in range(2):
                            if m >= 4:
                                pe.wait_ge(s_act, m - 3)
                            f = (m % 2) * P
                            for half in range(2):
                                for j in range(DC):
                                    mm = nc.tensor.matmul(ps[4 + m % 4][:, half * TT:(half + 1) * TT],
                                                          w[:, j, half * 256 + f:half * 256 + f + P], hT[:, j, :],
                                                          start=(j == 0), stop=(j == DC - 1))
                            mm.then_inc(s_gu, 1)
                            m += 1
                        pe.wait_ge(s_gu, m)
                        pe.sem_inc(s_used, 1)
                    tile = FIRST["ffn"] + (3 * k + 2 if k < 5 else 16)
                    arrived(pe, tile)
                    for f in range(4 * k, m):
                        pe.wait_ge(s_act, f + 1)
                        for d in range(DC):
                            mm = nc.tensor.matmul(ps[d // 2][:, (d % 2) * TT:(d % 2 + 1) * TT],
                                                  tile_out(tile)[:, f % 4, d * P:(d + 1) * P], act4[:, k % 2, f % 4, :],
                                                  start=(f == 0 and d % 2 == 0), stop=(f == FC - 1), skip_group_check=True)
                    mm.then_inc(s_ffn, 1)
                    pe.wait_ge(s_ffn, k + 1)
                    pe.sem_inc(s_used, 1)

            @block.vector
            def _(dve):
                dve_residual(dve, s_op, 0, 0, 16)
                dve.wait_ge(s_sq, n1.k + 1)
                n1.dve(dve)
                for m in range(FC):
                    dve.wait_ge(s_sil, m + 1)
                    if m >= 8 and m % 4 == 0:
                        dve.wait_ge(s_ffn, m // 4 - 1)
                    nc.vector.tensor_tensor(act4[:, (m // 4) % 2, m % 4, :], ps[4 + m % 4][:, TT:2 * TT], sgt[:, m % 2, :],
                                            ALU.mult).then_inc(s_act, 1)
                dve.wait_ge(s_ffn, FFN_OUT_TILES)
                dve_residual(dve, s_ffn, None, 0, 40)
        drop(0)
        cons[2] = take(NCONST[2])
        qkv = take(3 * GH, TT)
        sz = take(GH, TT)
        gg = take(NS, 16)
        beta = take(NS, 16)
        Gp = take(NS, 16)
        eG = take(NS, 16)
        nbe = take(NS, 16)
        eE = take(16)
        m_gd = floats[0]
        hT = take(DC, TT)
        sq2 = take(DC, TT)
        pad = take(4, NS, T + 2)
        tmp = take(2, NS, T)
        gdrow = take(2, 16)
        xa, xn = take(NS, 16), take(NS, 16)
        nrm4 = take(2, 4, TT)
        n2 = Norm(2, sq2)
        s_s5 = sem("silu5_done")
        P1 = EC
        s_q5, s_ss5, s_rt5 = sem("qk_squared"), sem("qk_sumsq_done"), sem("qk_root_done")
        s_ab, s_xn, s_e5, s_l5, s_g5, s_cum, s_eg = (sem("ab_done"), sem("gate_arg_ready"), sem("gate_exp_done"),
                                                     sem("gate_log_done"), sem("log_decay_ready"), sem("decay_sums_done"),
                                                     sem("decay_exps_done"))
        s_b5 = sem("beta_done")
        s_c5, s_nq = sem("odd_params_loaded"), sem("qk_normed")
        OC = 32
        with nc.Block() as block:
            @block.sync
            def _(sp):
                sp.dma_start(cons[2], A["con2"]).then_inc(s_c5, 16)
                sp.dma_start(gdrow.rearrange("p a c -> p (a c)"), A["gdrow"].partition_broadcast(P)).then_inc(s_c5, 16)
                feed(sp, FIRST["odd_in"] + ODD_IN_TILES)

            @block.gpsimd
            def _(pool):
                nc.gpsimd.memset(pad, 0.0).then_inc(s_pz, 1)

            @block.scalar
            def _(act):
                n2.act_squares(act)
                n2.act_root(act, ps[4])
                act.wait_ge(s_pz, 2)
                for m in range(OC):
                    act.wait_ge(s_p, P1 + m + 1)
                    src = v3(ps[m % 4][:, 0:TT])
                    if m < 24:
                        if m >= 4:
                            act.wait_ge(s_pc, P1 + m - 3)
                        nc.scalar.activation(pad[:, m % 4, :, 1:T + 1], src, ACT.Copy).then_inc(s_pad, 1)
                        act.wait_ge(s_pc, P1 + m + 1)
                        nc.scalar.activation(qkv[:, m, :], qkv[:, m, :], ACT.Silu).then_inc(s_s5, 1)
                        if m < 16 and m % 4 == 3:
                            act.wait_ge(s_s5, m + 1)
                            if m >= 4:
                                act.wait_ge(s_ss5, m // 4)
                            nc.scalar.activation(nrm4[:, 0], qkv[:, m - 3:m + 1, :], ACT.Square).then_inc(s_q5, 1)
                        if m % 4 == 1 and 4 < m < 20:
                            g4 = m // 4 - 1
                            act.wait_ge(s_ss5, g4 + 1)
                            if g4:
                                act.wait_ge(s_nq, g4)
                            for h in range(2):
                                nc.scalar.activation(nrm4[:, 1, 2 * h:2 * h + 2, :].rearrange("p c t -> p (c t)"), ps[5 + h][:],
                                                     ACT.Sqrt, bias=cc("eps6")).then_inc(s_rt5, 1)
                    else:
                        nc.scalar.activation(v3(sz[:, m - 24, :]), src, ACT.Silu).then_inc(s_pad, 1)
                nc.scalar.activation(gdrow[:, 0, :], gdrow[:, 0, :], ACT.Exp).then_inc(s_e5, 1)
                act.wait_ge(s_ab, 1)
                nc.scalar.activation(beta, ps[7][:, 0:64].rearrange("p (s c) -> p s c", s=2)[:, :, 16:32], ACT.Sigmoid)\
                    .then_inc(s_b5, 1)
                act.wait_ge(s_xn, 1)
                nc.scalar.activation(xn, xn, ACT.Exp).then_inc(s_e5, 1)
                act.wait_ge(s_e5, 2)
                nc.scalar.activation(xn, xn, ACT.Ln, bias=cc("one")).then_inc(s_l5, 1)
                act.wait_ge(s_cum, 1)
                nc.scalar.activation(eG, ps[5][:, 0:32].rearrange("p (d s h) -> p s d h", d=2, s=2), ACT.Exp).then_inc(s_eg, 1)
                nc.scalar.activation(eE, ps[5][:, 32:48], ACT.Exp).then_inc(s_eg, 1)

            @block.tensor
            def _(pe):
                n2.pe(pe, ps[4])
                n2.h_ready(pe)
                for m in range(OC):
                    n = FIRST["odd_in"] + m // 4
                    if m % 4 == 0:
                        arrived(pe, n)
                    if m >= 4:
                        pe.wait_ge(s_pad, P1 + m - 3)
                    f = m % 4
                    for j in range(DC):
                        mm = nc.tensor.matmul(ps[m % 4][:, 0:TT], tile_in(n)[:, j, f * P:(f + 1) * P], hT[:, j, :],
                                              start=(j == 0), stop=(j == DC - 1))
                    mm.then_inc(s_p, 1)
                    if f == 3:
                        pe.wait_ge(s_p, P1 + m + 1)
                        pe.sem_inc(s_used, 1)
                    if m % 4 == 0 and 4 <= m <= 16:
                        g4 = m // 4 - 1
                        pe.wait_ge(s_q5, g4 + 1)
                        if g4:
                            pe.wait_ge(s_rt5, 2 * g4)
                        for h in range(2):
                            mm = nc.tensor.matmul(ps[5 + h][:], ones, nrm4[:, 0, 2 * h:2 * h + 2, :]
                                                  .rearrange("p c t -> p (c t)"), start=True, stop=True)
                        mm.then_inc(s_ss5, 1)
                n = FIRST["odd_in"] + 8
                arrived(pe, n)
                for s in range(NS):
                    for j in range(DC):
                        mm = nc.tensor.matmul(ps[7][:, 32 * s:32 * s + 32], hT[:, j, s * T:(s + 1) * T], tile_in(n)[:, j, 0:32],
                                              start=(j == 0), stop=(j == DC - 1))
                mm.then_inc(s_ab, 1)
                pe.wait_ge(s_ab, 1)
                pe.sem_inc(s_used, 1)
                pe.wait_ge(s_g5, 1)
                pe.wait_ge(s_c5, 32)
                pe.wait_ge(s_rt5, 8)
                for d in range(2):
                    nc.tensor.matmul(ps[5][:, 16 * d:16 * d + 16], cc("tri_f" if d == 0 else "tri_b"),
                                     gg[:, :, 8 * d:8 * d + 8], start=True, stop=True)
                for d in range(2):
                    mm = nc.tensor.matmul(ps[5][:, 32 + 8 * d:40 + 8 * d], cc("tri_sf" if d == 0 else "tri_sb"),
                                          gg[:, 0, 8 * d:8 * d + 8], start=True, stop=True)
                mm.then_inc(s_cum, 1)

            @block.vector
            def _(dve):
                V = nc.vector
                n2.dve(dve)
                w = pcol("gdw")

                def scale_qk(g4):
                    dve.wait_ge(s_rt5, 2 * (g4 + 1))
                    b = nrm4[:, 1]
                    dve_link(dve, V.reciprocal(b, b))
                    dve.wait_ge(s_s5, 4 * g4 + 4)
                    seg = qkv[:, 4 * g4:4 * g4 + 4, :]
                    V.scalar_tensor_tensor(seg.rearrange("p c t -> p (c t)"), seg.rearrange("p c t -> p (c t)"),
                                           P ** -0.5 if g4 < 2 else 1.0, b.rearrange("p c t -> p (c t)"), ALU.mult, ALU.mult)\
                        .then_inc(s_nq, 1)

                for m in range(24):
                    dve.wait_ge(s_pad, P1 + m + 1)
                    left, mid, right = (pad[:, m % 4, :, k:k + T] for k in range(3))
                    out = v3(qkv[:, m, :])
                    a = tmp[:, 0]
                    dve_link(dve, V.tensor_scalar(a, mid, w[:, 24 + m:25 + m], None, ALU.mult))
                    dve_link(dve, V.scalar_tensor_tensor(out, left, w[:, m:m + 1], a, ALU.mult, ALU.add))
                    V.scalar_tensor_tensor(out, right, w[:, 48 + m:49 + m], out, ALU.mult, ALU.add).then_inc(s_pc, 1)
                    dve.wait_ge(s_pc, P1 + m + 1)
                    if m % 4 == 2 and 6 <= m <= 18:
                        scale_qk(m // 4 - 1)
                dve.wait_ge(s_c5, 32)
                dve.wait_ge(s_ab, 1)
                dve.wait_ge(s_b5, 1)
                bcast = lambda i: gdrow[:, i, :].unsqueeze(1).broadcast_to([P, NS, 16])
                dve_link(dve, V.tensor_tensor(xa, ps[7][:, 0:64].rearrange("p (s c) -> p s c", s=2)[:, :, 0:16], bcast(1), ALU.add))
                fl = lambda ap: ap.rearrange("p s c -> p (s c)")
                V.scalar_tensor_tensor(fl(xn), fl(xa), -1.0, fl(xa), ALU.mult, ALU.min).then_inc(s_xn, 1)
                dve.wait_ge(s_l5, 1)
                dve_link(dve, V.scalar_tensor_tensor(fl(xa), fl(xa), 0.0, fl(xn), ALU.max, ALU.add))
                dve.wait_ge(s_e5, 1)
                dve_link(dve, V.tensor_tensor(xa, xa, bcast(0), ALU.mult))
                V.tensor_scalar(gg, xa, -1.0, None, ALU.mult).then_inc(s_g5, 1)
                V.tensor_scalar(nbe, beta, -1.0, None, ALU.mult)
                dve.wait_ge(s_eg, 2)
                dve_link(dve, V.tensor_copy(Gp, ps[5][:, 0:32].rearrange("p (d s h) -> p s d h", d=2, s=2)))
                dve_link(dve, V.tensor_scalar(eG, eG, -1.0, None, ALU.mult))
        drop(m_gd)
        m_inv = floats[0]
        inv = Inversion()
        m_qk = floats[0]
        QK = [take(4, T) for _ in range(2)]
        Am = [take(4, T) for _ in range(2)]
        Dg = [take(4, T) for _ in range(2)]
        Rh = [take(4, T) for _ in range(2)]
        kend = [take(2, T) for _ in range(2)]
        S0 = take(2, 2, P)
        qd = [take(2, T) for _ in range(2)]
        flat = lambda lo, n: arena[:, lo:lo + n]
        sto = Am[0].rearrange("p (h d) t -> p h d t", h=2)
        yg = qkv[:, 0:GH, :]
        ygf = yg.rearrange("p h t -> p (h t)")
        sqg, rsg = flat(m_inv, 2048), flat(m_qk + 2048, 2048)
        s_s05, s_kq, s_row, s_vk, s_vt5, s_ks = (sem("s0_loaded"), sem("kq_done"), sem("decay_rows_done"),
                                                 sem("vk_tok_major"), sem("v_copied"), sem("ks0_done"))
        s_df, s_gam, s_er, s_gm, s_qd = (sem("decay_args_ready"), sem("decays5_done"), sem("row_exps_done"),
                                         sem("decays_masked"), sem("q_decayed"))
        s_bt, s_btt, s_A, s_At, s_ats = (sem("kk_scores_ready"), sem("kk_transposed"), sem("A_ready"), sem("A_transposed"),
                                         sem("At_copied"))
        s_ke, s_R, s_V, s_Vs, s_O5, s_Os, s_S5, s_sts = (
            sem("k_end_ready"), sem("rhs5_ready"), sem("values_done"), sem("values_copied"), sem("out5_done"),
            sem("out5_copied"), sem("state5_done"), sem("state5_copied"))
        s_sq6, s_ss6, s_rt6 = sem("o_squared"), sem("o_sumsq_done"), sem("o_root_done")
        PAIRS = GH // 2
        with nc.Block() as block:
            @block.sync
            def _(sp):
                for i in range(PAIRS):
                    if i:
                        sp.wait_ge(s_O5, i)
                    sp.dma_start(S0, A["s0gd"][:, 2 * i:2 * i + 2]).then_inc(s_s05, 16)
                    sp.wait_ge(s_sts, i + 1)
                    sp.dma_start(O["sgd"][:, 2 * i:2 * i + 2], sto).then_inc(s_stored, 16)
                sp.wait_ge(s_stored, 16 * (PAIRS + 1))
                feed(sp, FIRST["odd_out"])

            @block.gpsimd
            def _(pool):
                for i in range(PAIRS):
                    for g in range(2):
                        if i:
                            pool.wait_ge(s_V, 2 * i)
                            pool.wait_ge(s_Z, 2 * RWC)
                        inv.pool_reset(pool, g)
                    for g in range(2):
                        k = 2 * i + g
                        pool.wait_ge(s_gam, k + 1)
                        nc.gpsimd.affine_select(out=Dg[g], in_=Dg[g], pattern=[[0, 4], [1 if g == 0 else -1, T]],
                                                compare_op=ALU.is_ge, fill=0.0, base=0,
                                                channel_multiplier=-1 if g == 0 else 1).then_inc(s_gm, 1)
                        pool.wait_ge(s_er, k + 1)
                        nc.gpsimd.tensor_tensor(qd[g], qd[g], qkv[:, 2 * i:2 * i + 2, T:TT], ALU.mult).then_inc(s_qd, 1)

            @block.scalar
            def _(act):
                for i in range(PAIRS):
                    act.wait_ge(s_vk, 2 * i + 1)
                    if i:
                        act.wait_ge(s_V, 2 * i)
                    nc.scalar.activation(Rh[1].rearrange("p q v -> p (q v)"), ps[4][:], ACT.Copy).then_inc(s_vt5, 1)
                    for g in range(2):
                        k = 2 * i + g
                        act.wait_ge(s_df, k + 1)
                        nc.scalar.activation(Dg[g], Dg[g], ACT.Exp).then_inc(s_gam, 1)
                        act.wait_ge(s_row, k + 1)
                        if i:
                            act.wait_ge(s_O5, i)
                        nc.scalar.activation(qd[g].rearrange("p h t -> p (h t)"), ps[2 + g][:, TT:2 * TT], ACT.Exp)\
                            .then_inc(s_er, 1)
                    for g in range(2):
                        act.wait_ge(s_At, 2 * i + g + 1)
                        nc.scalar.activation(Dg[g].rearrange("p q t -> p (q t)"), ps[7][:], ACT.Copy).then_inc(s_ats, 1)
                    for l in range(1, LEVELS):
                        inv.act_level(act, RWC + i, l)
                    for g in range(2):
                        act.wait_ge(s_V, 2 * i + g + 1)
                        nc.scalar.activation(inv.X[g].rearrange("p q v -> p (q v)"), ps[g][:], ACT.Copy).then_inc(s_Vs, 1)
                    act.wait_ge(s_O5, i + 1)
                    nc.scalar.activation(qkv[:, 2 * i:2 * i + 2, :].rearrange("p h t -> p (h t)"), ps[6][:], ACT.Copy)\
                        .then_inc(s_Os, 1)
                act.wait_ge(s_Os, PAIRS)
                nc.scalar.activation(sqg, ygf, ACT.Square).then_inc(s_sq6, 1)
                act.wait_ge(s_ss6, 1)
                for b in range(4):
                    nc.scalar.activation(rsg[:, 512 * b:512 * b + 512], ps[b][:], ACT.Sqrt, scale=1.0 / P, bias=cc("eps6"))\
                        .then_inc(s_rt6, 1)

            @block.tensor
            def _(pe):
                tri = [cc("tri_f"), cc("tri_b")]
                for i in range(PAIRS):
                    if i:
                        pe.wait_ge(s_Vs, 2 * i)
                        pe.wait_ge(s_U[1], (RWC + i) * NU[1])
                        pe.wait_ge(s_T[1], (RWC + i) * NT[1])
                        pe.wait_ge(s_U[0], (RWC + i) * NU[0])
                    for hh in range(2):
                        h = 2 * i + hh
                        for s in range(NS):
                            tok = slice(s * T, (s + 1) * T)
                            mm = nc.tensor.matmul(ps[hh][:, s * TT:(s + 1) * TT].rearrange("p (a t) -> p a t", a=2),
                                                  qkv[:, GH + h, tok], qkv[:, h:h + GH + 1:GH, tok], start=True, stop=True)
                    mm.then_inc(s_kq, 1)
                    for g in range(2):
                        for q in range(4):
                            s, hh = divmod(q, 2)
                            col = gg[:, s, 8 * g + 2 * i + hh:8 * g + 2 * i + hh + 1].broadcast_to([P, P])
                            mm = nc.tensor.matmul(ps[2 + g][:, q * T:(q + 1) * T], col, tri[g], start=True, stop=True)
                        mm.then_inc(s_row, 1)
                    for q in range(4):
                        s, hh = divmod(q, 2)
                        mm = nc.tensor.transpose(ps[4][:, q * T:(q + 1) * T], qkv[:, 2 * GH + 2 * i + hh, s * T:(s + 1) * T], ident)
                    mm.then_inc(s_vk, 1)
                    for hh in range(2):
                        mm = nc.tensor.transpose(ps[5][:, hh * T:(hh + 1) * T], qkv[:, GH + 2 * i + hh, 0:T], ident)
                    mm.then_inc(s_vk, 1)
                    pe.wait_ge(s_s05, 16 * (i + 1))
                    pe.wait_ge(s_vt5, i + 1)
                    for hh in range(2):
                        mm = nc.tensor.matmul(ps[4][:, hh * TT:(hh + 1) * TT], qkv[:, GH + 2 * i + hh, T:TT],
                                              S0[:, hh].rearrange("p d v -> p (d v)"), start=True, stop=True)
                    mm.then_inc(s_ks, 1)
                    if i:
                        pe.wait_ge(s_Os, i)
                        pe.wait_ge(s_sts, i)
                    for g in range(2):
                        k = 2 * i + g
                        pe.wait_ge(s_bt, k + 1)
                        if g:
                            pe.wait_ge(s_A, k)
                        for q in range(4):
                            mm = nc.tensor.transpose(ps[6][:, q * T:(q + 1) * T], Dg[g][:, q], ident)
                        mm.then_inc(s_btt, 1)
                        pe.wait_ge(s_A, k + 1)
                        if g:
                            pe.wait_ge(s_ats, k)
                        for q in range(4):
                            mm = nc.tensor.transpose(ps[7][:, q * T:(q + 1) * T], Am[g][:, q], ident)
                        mm.then_inc(s_At, 1)
                    pe.wait_ge(s_ats, 2 * i + 2)
                    pe.wait_ge(s_R, 2 * i + 2)
                    pe.wait_ge(s_er, 2 * i + 2)
                    pe.wait_ge(s_ke, i + 1)
                    up = [Dg[0], Am[1]]
                    for l in range(1, LEVELS):
                        inv.pe_level(pe, RWC + i, l, up)
                    for g in range(2):
                        inv.pe_final(pe, RWC + i, g)
                        for q in range(4):
                            mm = nc.tensor.matmul(ps[g][:, q * T:(q + 1) * T], inv.final[g][:, q], Rh[g][:, q], start=True, stop=True)
                        mm.then_inc(s_V, 1)
                    pe.wait_ge(s_Vs, 2 * i + 2)
                    pe.wait_ge(s_qd, 2 * i + 2)
                    for hh in range(2):
                        for s in range(NS):
                            q = 2 * s + hh
                            out = ps[6][:, hh * TT + s * T:hh * TT + (s + 1) * T]
                            for g in range(2):
                                if s:
                                    nc.tensor.matmul(out, S0[:, hh, g], qd[g][:, hh], start=(g == 0), stop=False)
                                mm = nc.tensor.matmul(out, inv.X[g][:, q], QK[g][:, q], start=(g == 0 and s == 0), stop=(g == 1))
                    mm.then_inc(s_O5, 1)
                    for hh in range(2):
                        for g in range(2):
                            mm = nc.tensor.matmul(ps[7][:, (2 * hh + g) * T:(2 * hh + g + 1) * T], kend[g][:, hh],
                                                  inv.X[g][:, hh], start=True, stop=True)
                    mm.then_inc(s_S5, 1)
                pe.wait_ge(s_sq6, 1)
                for b in range(4):
                    mm = nc.tensor.matmul(ps[b][:], ones, sqg[:, 512 * b:512 * b + 512], start=True, stop=True)
                mm.then_inc(s_ss6, 1)

            @block.vector
            def _(dve):
                V = nc.vector
                for i in range(PAIRS):
                    h0 = 2 * i
                    for g in range(2):
                        k = 2 * i + g
                        dve.wait_ge(s_row, k + 1)
                        for q in range(4):
                            s, hh = divmod(q, 2)
                            ins = V.tensor_scalar(Dg[g][:, q], ps[2 + g][:, q * T:(q + 1) * T],
                                                  Gp[:, s, 8 * g + h0 + hh:8 * g + h0 + hh + 1], 0.0, ALU.subtract, ALU.min)
                        ins.then_inc(s_df, 1)
                    dve.wait_ge(s_vk, 2 * i + 2)
                    for g in range(2):
                        for hh in range(2):
                            c = 8 * g + h0 + hh
                            ins = V.tensor_scalar(kend[g][:, hh], ps[5][:, hh * T:(hh + 1) * T], eE[:, c:c + 1], None, ALU.mult)
                    ins.then_inc(s_ke, 1)
                    dve.wait_ge(s_vt5, i + 1)
                    dve.wait_ge(s_ks, i + 1)
                    for g in range(2):
                        for hh in range(2):
                            c = 8 * g + h0 + hh
                            dve_link(dve, V.scalar_tensor_tensor(Rh[g][:, 2 + hh], ps[4][:, hh * TT + g * T:hh * TT + (g + 1) * T],
                                                                 eG[:, 1, c:c + 1], Rh[1][:, 2 + hh], ALU.mult, ALU.add))
                        for q in range(4):
                            s, hh = divmod(q, 2)
                            c = 8 * g + h0 + hh
                            ins = V.tensor_scalar(Rh[g][:, q], Rh[1][:, q] if s == 0 else Rh[g][:, q], beta[:, s, c:c + 1],
                                                  None, ALU.mult)
                        ins.then_inc(s_R, 1)
                    dve.wait_ge(s_kq, i + 1)
                    if i:
                        dve.wait_ge(s_stored, 16 * (i + 1))
                    for g in range(2):
                        k = 2 * i + g
                        dve.wait_ge(s_gm, k + 1)
                        for hh in range(2):
                            kq = ps[hh][:].rearrange("p (s a t) -> p s a t", s=2, a=2)
                            d = Dg[g][:, hh:4:2]
                            dve_link.last(dve, V.tensor_tensor(QK[g][:, hh:4:2], kq[:, :, 0], d, ALU.mult))
                        dve_link.sync(dve)
                        for hh in range(2):
                            kq = ps[hh][:].rearrange("p (s a t) -> p s a t", s=2, a=2)
                            d = Dg[g][:, hh:4:2]
                            ins = V.tensor_tensor(d, kq[:, :, 1], d, ALU.mult)
                        ins.then_inc(s_bt, 1)
                        dve.wait_ge(s_btt, k + 1)
                        for q in range(4):
                            s, hh = divmod(q, 2)
                            c = 8 * g + h0 + hh
                            ins = V.scalar_tensor_tensor(Am[g][:, q], ps[6][:, q * T:(q + 1) * T], nbe[:, s, c:c + 1],
                                                         selm[:, 4 + g, :], ALU.mult, ALU.mult)
                        ins.then_inc(s_A, 1)
                    dve.wait_ge(s_A, 2 * i + 2)
                    for g in range(2):
                        dve.wait_ge(s_ats, 2 * i + g + 1)
                        low, up = (Am[0], Dg[0]) if g == 0 else (Dg[1], Am[1])
                        inv.dve_first(dve, RWC + i, g, low, up)
                    for l in range(1, LEVELS):
                        inv.dve_level(dve, RWC + i, l)
                    dve.wait_ge(s_S5, i + 1)
                    V.tensor_copy(sto.rearrange("p h d t -> p (h d t)"), ps[7][:]).then_inc(s_sts, 1)
                for b in range(4):
                    dve.wait_ge(s_rt6, b + 1)
                    r = rsg[:, 512 * b:512 * b + 512]
                    y = ygf[:, 512 * b:512 * b + 512]
                    z = sz.rearrange("p h t -> p (h t)")[:, 512 * b:512 * b + 512]
                    dve_link(dve, V.reciprocal(r, r))
                    dve_link(dve, V.tensor_tensor(y, y, r, ALU.mult))
                    dve_link(dve, V.scalar_tensor_tensor(y, y, pcol("normg"), z, ALU.mult, ALU.mult))
        drop(NCONST[2])
        yg7 = take(GH, TT)
        hT = take(DC, TT)
        htok = take(NS, D)
        hA = take(DC, T)
        hB = take(DC, T)
        moe = take(DC, TT)
        m_route = floats[0]
        rows16 = NE * 2 + 1
        pos = take(NS, rows16)
        wgt = take(NS, 2 * NE)
        Psel = take(NS, T)
        Pw = take(NS, T)
        flag = take(2)
        sq3 = take(DC, TT)
        router = take(DC, NE)
        L, cnt, wd, sel = take(NS, NE), take(NS, NE), take(NS, NE), take(NS, NE)
        cg, ce = take(NS, NE, NE), take(NS, NE, NE)
        s1 = take(2, NS, NE)
        top = take(NS, NE)
        lv = take(4, NS)
        n3 = Norm(3, sq3)
        s_lg, s_cnt7, s_e7, s_rk, s_P, s_Pw, s_flag = (
            sem("logits_done"), sem("selection_ready"), sem("route_exp_done"), sem("ranks_done"),
            sem("slots_ready"), sem("slot_weights_ready"), sem("overflow_known"))
        s_ht, s_htc, s_gat, s_hB, s_hA = (sem("h_tok_major"), sem("h_tok_copied"), sem("gathered"), sem("gather_copied"),
                                                 sem("expert_h_ready"))
        s_dl = sem("gate_diff_ready")
        s_tr8, s_aT, s_ye, s_Ct, s_C, s_sc, s_acc = (
            sem("act_transposed"), sem("act_t_copied"), sem("y_copied"),
            sem("weights_transposed"), sem("weights_copied"), sem("scattered"), sem("accumulated"))
        over = flag.bitcast(I32)[:, 0:1]

        def dve_slots(dve, out, it, weights):
            for s in range(NS):
                p = pos[:, s, bass.ds(it, 1)]
                if weights:
                    ins = nc.vector.tensor_scalar(out[:, s, :], cc("iota"), p, wgt[:, s, bass.ds(it, 1)], ALU.is_equal, ALU.mult)
                else:
                    ins = nc.vector.tensor_scalar(out[:, s, :], cc("iota"), p, None, ALU.is_equal)
            return ins

        def pe_gather(pe, half):
            for j in range(4 * half, 4 * half + 4):
                for s in range(NS):
                    mm = nc.tensor.matmul(ps[5][:, (j % 4) * T:(j % 4 + 1) * T], htok[:, s, j * P:(j + 1) * P], Psel[:, s, :],
                                          start=(s == 0), stop=(s == 1))
            mm.then_inc(s_gat, 1)

        def act_gather(act, half):
            nc.scalar.activation(hB[:, 4 * half:4 * half + 4, :].rearrange("p j t -> p (j t)"), ps[5][:], ACT.Copy)\
                .then_inc(s_hB, 1)

        with nc.Block() as block:
            @block.sync
            def _(sp):
                sp.dma_start(router, A["router"]).then_inc(s_c5, 16)
                feed(sp, STREAM_TILES)

            @block.gpsimd
            def _(pool):
                nc.gpsimd.memset(moe, 0.0)
                for s in (s_tr8, s_aT, s_Ct, s_acc):
                    pool.sem_inc(s, 1)

            @block.scalar
            def _(act):
                act.wait_ge(s_x, 4)
                n3.act_squares(act)
                n3.act_root(act, ps[4])
                for k in range(4):
                    act.wait_ge(s_ht, k + 1)
                    nc.scalar.activation(htok[:, k // 2, 512 * (k % 2):512 * (k % 2) + 512], ps[k][:], ACT.Copy).then_inc(s_htc, 1)
                act.wait_ge(s_dl, 1)
                nc.scalar.activation(lv[:, 2], lv[:, 1], ACT.Exp).then_inc(s_e7, 1)
                for half in range(2):
                    act.wait_ge(s_gat, half + 1)
                    act_gather(act, half)

            @block.tensor
            def _(pe):
                pe_out_proj(pe, FIRST["odd_out"], yg7, s_op)
                pe.wait_ge(s_op, 8)
                pe.sem_inc(s_used, 2)
                n3.pe(pe, ps[4])
                n3.h_ready(pe)
                pe.wait_ge(s_c5, 48)
                for s in range(NS):
                    for j in range(DC):
                        mm = nc.tensor.matmul(ps[6][:, 8 * s:8 * s + 8], hT[:, j, s * T:(s + 1) * T], router[:, j, :],
                                              start=(j == 0), stop=(j == DC - 1))
                mm.then_inc(s_lg, 1)
                for k in range(4):
                    for j in range(4):
                        mm = nc.tensor.transpose(ps[k][:, j * P:(j + 1) * P],
                                                 hT[:, 4 * (k % 2) + j, (k // 2) * T:(k // 2 + 1) * T], ident)
                    mm.then_inc(s_ht, 1)
                pe.wait_ge(s_cnt7, 1)
                nc.tensor.matmul(ps[7][:, 0:8], cc("tri_sb"), sel[:, 0, :], start=True, stop=True)
                nc.tensor.matmul(ps[7][:, 8:16], cc("tri_sb"), sel[:, 1, :], start=True, stop=False)
                nc.tensor.matmul(ps[7][:, 8:16], ones, sel[:, 0, :], start=False, stop=True)
                nc.tensor.matmul(ps[7][:, 16:24], ones, sel[:, 0, :], start=True, stop=False)
                nc.tensor.matmul(ps[7][:, 16:24], ones, sel[:, 1, :], start=False, stop=True).then_inc(s_rk, 1)
                pe.wait_ge(s_htc, 4)
                pe.wait_ge(s_P, 1)
                pe_gather(pe, 0)
                pe.wait_ge(s_hB, 1)
                pe_gather(pe, 1)

            @block.vector
            def _(dve):
                V = nc.vector
                dve_residual(dve, s_op, 4, 1, 16)
                n3.dve(dve)
                dve.wait_ge(s_lg, 1)
                dve_link(dve, V.tensor_copy(L.rearrange("p s e -> p (s e)"), ps[6][:, 0:16]))
                for s in range(NS):
                    other = L[:, s, :].unsqueeze(1).broadcast_to([P, NE, NE])
                    own = L[:, s, :].unsqueeze(2).broadcast_to([P, NE, NE])
                    tie = cc("tie").rearrange("p (a b) -> p a b", a=NE)
                    dve_link.last(dve, V.tensor_tensor(cg[:, s], other, own, ALU.is_gt))
                    dve_link(dve, V.tensor_tensor(ce[:, s], other, own, ALU.is_equal))
                    dve_link(dve, V.tensor_tensor(ce[:, s], ce[:, s], tie, ALU.mult))
                dve_link(dve, V.tensor_tensor(cg.rearrange("p s a b -> p (s a b)"), cg.rearrange("p s a b -> p (s a b)"),
                                              ce.rearrange("p s a b -> p (s a b)"), ALU.add))
                dve_link(dve, V.tensor_reduce(cnt, cg, AX.X, ALU.add))
                dve_link.last(dve, V.tensor_scalar(s1[:, 0], cnt, 0.0, None, ALU.is_equal))
                dve_link.last(dve, V.tensor_scalar(s1[:, 1], cnt, 1.0, None, ALU.is_equal))
                dve_link.sync(dve)
                V.tensor_scalar(sel, cnt, 1.5, None, ALU.is_lt).then_inc(s_cnt7, 1)
                dve_link.last(dve, V.tensor_tensor(top, s1[:, 0], L, ALU.mult))
                dve_link.last(dve, V.tensor_tensor(wd, s1[:, 1], L, ALU.mult))
                dve_link.sync(dve)
                dve_link.last(dve, V.tensor_reduce(lv[:, 0], top, AX.X, ALU.add))
                dve_link.last(dve, V.tensor_reduce(lv[:, 1], wd, AX.X, ALU.add))
                dve_link.sync(dve)
                V.tensor_tensor(lv[:, 1], lv[:, 1], lv[:, 0], ALU.subtract).then_inc(s_dl, 1)
                dve.wait_ge(s_e7, 1)
                dve_link(dve, V.tensor_scalar(lv[:, 3], lv[:, 2], 1.0, None, ALU.add))
                dve_link(dve, V.reciprocal(lv[:, 3], lv[:, 3]))
                dve_link(dve, V.tensor_tensor(lv[:, 2], lv[:, 2], lv[:, 3], ALU.mult))
                for s in range(NS):
                    dve_link(dve, V.tensor_scalar(wd[:, s], s1[:, 0, s], lv[:, 3, s:s + 1], None, ALU.mult))
                    for r in range(2):
                        dve_link.last(dve, V.scalar_tensor_tensor(wgt[:, s, 8 * r:8 * r + 8], s1[:, 1, s], lv[:, 2, s:s + 1], wd[:, s],
                                                                  ALU.mult, ALU.add))
                dve_link.sync(dve)
                dve.wait_ge(s_rk, 1)
                dve_link(dve, V.tensor_scalar(pos[:, :, 0:8], sel, -4096.0, 4096.0, ALU.mult, ALU.add))
                dve_link(dve, V.tensor_tensor(pos[:, :, 0:8], pos[:, :, 0:8], ps[7][:, 0:16].rearrange("p (s e) -> p s e", s=2),
                                              ALU.add))
                dve_link.last(dve, V.tensor_scalar(pos[:, :, 8:16], pos[:, :, 0:8], -float(T), None, ALU.add))
                dve_link.last(dve, V.memset(pos[:, :, 16:17], 4096.0))
                dve_link(dve, V.tensor_reduce(flag[:, 1:2], ps[7][:, 16:24], AX.X, ALU.max))
                V.tensor_scalar(over, flag[:, 1:2], float(T), None, ALU.is_gt).then_inc(s_flag, 1)
                dve_link.sync(dve)
                dve_slots(dve, Psel, 0, False).then_inc(s_P, 1)
                dve.wait_ge(s_hB, 2)
                V.tensor_copy(hA, hB).then_inc(s_hA, 1)

        drop(m_route)
        floats[0] += 2 * rows16 + 2 * 16 + 4 * T + 2 + 64
        sgl = take(2, 512)
        actb = take(2, 512)
        actT = take(2, 4, T)
        ye = take(D)
        Cw = take(TT)
        sq4 = take(DC, TT)
        n4 = Norm(None, sq4)
        KC = EFF // 512
        TG = [0] + [2 + 3 * (k - 1) for k in range(1, KC)]
        TU = [t + 1 for t in TG]
        TO = [TG[k + 1] + 2 for k in range(KC - 1)] + [EXP_TILES - 1]
        BANKS = [2, 3, 4, 5]

        def used8(eng, it, t):
            eng.wait_ge(s_used, it * EXP_TILES + (STREAM_TILES + t + 1))

        def arrived8(eng, it, t):
            n = STREAM_TILES + t
            eng.wait_ge(s_slot[n % RING], it * (16 * EXP_TILES // RING) + 16 * (n // RING + 1))

        def rounds(eng, body):
            with eng.Fori(0, NE) as it:
                body(it)
            eng.wait_ge(s_flag, 1)
            more = eng.value_load(over[0:1, 0:1], min_val=0, max_val=1)
            with eng.If(more > 0):
                with eng.Fori(NE, 2 * NE) as it:
                    body(it)

        with nc.Block() as block:
            @block.sync
            def _(sp):
                def load(it, e, t):
                    n = STREAM_TILES + t
                    sp.dma_start(slot(n), A["experts"][bass.ds(e, 1), t % EXP_TILES].rearrange("a p c -> (a p) c"))\
                        .then_inc(s_slot[n % RING], 16)

                def tail_tiles(it, e):
                    for t in range(RING, EXP_TILES):
                        used8(sp, it, t - RING)
                        load(it, e, t)

                def next_tiles(it, e):
                    for t in range(EXP_TILES, EXP_TILES + RING):
                        used8(sp, it, t - RING)
                        load(it, e + 1, t)

                with sp.Fori(0, NE - 1) as e:
                    tail_tiles(e, e)
                    next_tiles(e, e)
                tail_tiles(NE - 1, NE - 1)
                sp.wait_ge(s_flag, 1)
                more = sp.value_load(over[0:1, 0:1], min_val=0, max_val=1)
                with sp.If(more > 0):
                    next_tiles(NE - 1, -1)
                    with sp.Fori(0, NE - 1) as e:
                        tail_tiles(e + NE, e)
                        next_tiles(e + NE, e)
                    tail_tiles(2 * NE - 1, NE - 1)
                sp.wait_ge(s_h, (n4.k + 1) * DC)
                sp.dma_start(O["y"], sq4).then_inc(s_stored, 16)
                sp.wait_ge(s_stored, 16 * (PAIRS + 2))

            @block.gpsimd
            def _(pool):
                pass

            @block.scalar
            def _(act):
                def body(it):
                    g0 = it * KC
                    for k in range(KC):
                        used8(act, it, TG[k])
                        act.wait_ge(s_act, g0 + (FC + max(k - 1, 0)))
                        nc.scalar.activation(sgl[:, k % 2], ps[2 * (k % 2)][:], ACT.Silu).then_inc(s_sil, 1)
                        if k:
                            act.wait_ge(s_tr8, g0 + k + 1)
                            if k >= 2:
                                used8(act, it, TO[k - 2])
                            nc.scalar.activation(actT[:, (k - 1) % 2].rearrange("p f t -> p (f t)"), ps[4][:], ACT.Copy)\
                                .then_inc(s_aT, 1)
                        if k in (2, 3):
                            act.wait_ge(s_hA, it + 1)
                            act.wait_ge(s_gat, 2 * it + (k + 1))
                            act_gather(act, k - 2)
                        if k == 4:
                            act.wait_ge(s_Ct, it + 2)
                            nc.scalar.activation(Cw, ps[5][:, 0:TT], ACT.Copy).then_inc(s_C, 1)
                    act.wait_ge(s_tr8, g0 + KC + 1)
                    nc.scalar.activation(actT[:, (KC - 1) % 2].rearrange("p f t -> p (f t)"), ps[4][:], ACT.Copy).then_inc(s_aT, 1)
                    used8(act, it, TO[KC - 1])
                    for h in range(2):
                        nc.scalar.activation(ye[:, 512 * h:512 * h + 512], ps[6 + h][:], ACT.Copy).then_inc(s_ye, 1)
                rounds(act, body)
                act.wait_ge(s_x, 5)
                n4.act_squares(act)
                n4.act_root(act, ps[0])

            @block.tensor
            def _(pe):
                def transposes(it, k):
                    pe.wait_ge(s_act, it * KC + (FC + k + 1))
                    pe.wait_ge(s_aT, it * KC + (k + 1))
                    for f in range(4):
                        mm = nc.tensor.transpose(ps[4][:, f * T:(f + 1) * T], actb[:, k % 2, f * P:(f + 1) * P], ident)
                    mm.then_inc(s_tr8, 1)

                def project(it, k):
                    n = STREAM_TILES + TO[k]
                    pe.wait_ge(s_aT, it * KC + (k + 2))
                    arrived8(pe, it, TO[k])
                    for f in range(4):
                        for h in range(2):
                            mm = nc.tensor.matmul(ps[6 + h][:], actT[:, k % 2, f, :], tile_out(n)[:, f, 512 * h:512 * h + 512],
                                                  start=(k == 0 and f == 0), stop=(k == KC - 1 and f == 3))
                    mm.then_inc(s_used, 1)

                def body(it):
                    pe.wait_ge(s_hA, it + 1)
                    for k in range(KC):
                        pe.wait_ge(s_act, it * KC + (FC + max(k - 1, 0)))
                        if k == 1:
                            pe.wait_ge(s_acc, it * 4 + 1)
                        for half, t in enumerate((TG[k], TU[k])):
                            arrived8(pe, it, t)
                            if half and k:
                                transposes(it, k - 1)
                            for j in range(DC):
                                mm = nc.tensor.matmul(ps[2 * (k % 2) + half][:], hA[:, j, :], tile_in(STREAM_TILES + t)[:, j, :],
                                                      start=(j == 0), stop=(j == DC - 1))
                            mm.then_inc(s_used, 1)
                        if k:
                            project(it, k - 1)
                        if k == 2:
                            pe.wait_ge(s_P, it + 2)
                            pe_gather(pe, 0)
                        if k == 3:
                            pe.wait_ge(s_hB, 2 * it + 3)
                            pe_gather(pe, 1)
                        if k == 4:
                            pe.wait_ge(s_hB, 2 * it + 4)
                            pe.wait_ge(s_Pw, it + 1)
                            for s in range(NS):
                                mm = nc.tensor.transpose(ps[5][:, s * T:(s + 1) * T], Pw[:, s, :], ident)
                            mm.then_inc(s_Ct, 1)
                    transposes(it, KC - 1)
                    project(it, KC - 1)
                    pe.wait_ge(s_C, it + 1)
                    pe.wait_ge(s_ye, 2 * it + 2)
                    for b in range(4):
                        for d in (2 * b, 2 * b + 1):
                            mm = nc.tensor.matmul(ps[BANKS[b]][:, (d % 2) * TT:(d % 2 + 1) * TT], ye[:, d * P:(d + 1) * P], Cw,
                                                  start=True, stop=True)
                        mm.then_inc(s_sc, 1)
                rounds(pe, body)
                n4.pe(pe, ps[0])

            @block.vector
            def _(dve):
                V = nc.vector

                def body(it):
                    dve.wait_ge(s_Ct, it + 1)
                    dve_slots(dve, Pw, it, True).then_inc(s_Pw, 1)
                    dve.wait_ge(s_gat, 2 * it + 2)
                    dve_slots(dve, Psel, it + 1, False).then_inc(s_P, 1)
                    for k in range(KC):
                        dve.wait_ge(s_sil, it * KC + (FC + k + 1))
                        used8(dve, it, TU[k])
                        dve.wait_ge(s_tr8, it * KC + (max(k - 1, 0) + 1))
                        V.tensor_tensor(actb[:, k % 2], ps[2 * (k % 2) + 1][:], sgl[:, k % 2], ALU.mult).then_inc(s_act, 1)
                    dve.wait_ge(s_hB, 2 * it + 4)
                    V.tensor_copy(hA, hB).then_inc(s_hA, 1)
                    for b in range(4):
                        dve.wait_ge(s_sc, 4 * it + (b + 1))
                        m = moe[:, 2 * b:2 * b + 2, :].rearrange("p d t -> p (d t)")
                        V.tensor_tensor(m, m, ps[BANKS[b]][:], ALU.add).then_inc(s_acc, 1)
                    dve.wait_ge(s_acc, 4 * it + 5)
                rounds(dve, body)
                for d in range(DC):
                    for s in range(NS):
                        x = xT[:, d, s * T:(s + 1) * T]
                        ins = V.scalar_tensor_tensor(x, moe[:, d, s * T:(s + 1) * T], mod[:, 1, 40 + d, s:s + 1], x, ALU.mult, ALU.add)
                        if d < DC - 1 or s == 0:
                            dve_link.last(dve, ins)
                dve_link.sync(dve)
                ins.then_inc(s_x, 1)
                n4.dve(dve, sq4)


def _cols(v, chunks):
    v = np.asarray(v, np.float32).reshape(-1)
    out = np.zeros((chunks * P,), np.float32)
    out[:v.size] = v
    return out.reshape(chunks, P).T


def _in_tiles(w, groups):
    out = np.zeros((len(groups), P, 8, 512), np.float32)
    wj = w.reshape(8, P, w.shape[1])
    for t, ranges in enumerate(groups):
        at = 0
        for a, b in ranges:
            out[t, :, :, at:at + b - a] = wj[:, :, a:b].transpose(1, 0, 2)
            at += b - a
    return out.reshape(len(groups), P, TILE)


def _out_tiles(w):
    k = -(-w.shape[0] // 512)
    full = np.zeros((k * 512, 1024), np.float32)
    full[:w.shape[0]] = w
    return full.reshape(k, 4, P, 1024).transpose(0, 2, 1, 3).reshape(k, P, TILE)


def _by(n, step=512):
    return [[(a, min(a + step, n))] for a in range(0, n, step)]


def pack(i):
    i = {k: np.asarray(v) for k, v in i.items()}
    table, masks, feats, window, posT = constants()
    par = {}
    c0 = i["c_ctx"].reshape(8, P)
    c1 = i["c"].reshape(8, P)
    par["cond"] = np.stack([c0, c1], -1).transpose(1, 0, 2).reshape(P, 16)
    for l in range(2):
        par[f"ada_b{l}"] = _cols(i["ada_b"][l], 48)
        par[f"gmix{l}"] = _cols(i["norm_mix_g"][l], 8)
        par[f"gffn{l}"] = _cols(i["norm_ffn_g"][l], 8)
    par["gfin"] = _cols(i["final_norm_g"], 8)
    par["hyw"] = np.concatenate([_cols(i["e_hy_conv_w"][0, k], 12) for k in range(3)], 1)
    par["hyb"] = _cols(i["e_hy_conv_b"], 12)
    par["mu"] = _cols(i["e_rw_mu"], 14)
    par["w0"] = np.concatenate([_cols(i["e_rw_w0"][0, d], 4) for d in range(2)], 1)
    par["a0"] = np.concatenate([_cols(i["e_rw_a0"][0, d], 4) for d in range(2)], 1)
    par["kk"], par["ka"], par["rk"] = (_cols(i[n], 4) for n in ("e_rw_kk", "e_rw_ka", "e_rw_rk"))
    par["lnw"], par["lnb"] = _cols(i["e_rw_ln_w"], 4), _cols(i["e_rw_ln_b"], 4)
    par["gdw"] = np.concatenate([_cols(i["o_conv_w"][0, k], 24) for k in range(3)], 1)
    par["normg"] = _cols(i["o_norm_g"], 1)
    for k in (1, 2):
        par[f"hfb{k}"] = _cols(i[f"e_hf_b{k}"], 1)
        par[f"hff{k}"] = _cols(i[f"e_hf_freq{k}"], 1)
    x = np.concatenate([i["x_prompt"][0], i["x_sample"][0]], 0)
    hfw = np.zeros((64, 128 + 2048), np.float32)
    hfw[:33, :64] = i["e_hf_w1"][0]
    hfw[:, 64:128] = i["e_hf_w2"][0]
    hfw[:, 128:] = i["e_hf_w3"][0]
    ada = [_in_tiles(i["ada_w"][l], _by(6144)) for l in range(2)]
    ffn_in = _in_tiles(i["e_ffn_w_in"][0], [[(a, a + 256), (FF + a, FF + a + 256)] for a in range(0, FF, 256)])
    ffn_out = _out_tiles(i["e_ffn_w_out"][0])
    ffn = []
    for k in range(FFN_OUT_TILES):
        ffn += [ffn_in[2 * k:2 * k + 2], ffn_out[k:k + 1]]
    parts = {"ada0a": ada[0][:4], "ada0b": ada[0][4:], "ada1": ada[1],
             "even_in": _in_tiles(i["e_w_in"][0], _by(3296)), "even_out": _out_tiles(i["e_w_out"][0]),
             "ffn": np.concatenate(ffn), "odd_in": _in_tiles(i["o_w_in"][0], _by(4128)),
             "odd_out": _out_tiles(i["o_w_out"][0])}
    stream = np.concatenate([parts[n] for n, _ in STREAM])
    experts = np.empty((NE, EXP_TILES, P, TILE), np.float32)
    for e in range(NE):
        gu = _in_tiles(i["o_moe_w_in"][0, e], [[(a + g, a + g + 512)] for a in range(0, EFF, 512) for g in (0, EFF)])
        wo = _out_tiles(i["o_moe_w_out"][0, e])
        for k in range(7):
            at = 3 * k - 1 if k else 0
            experts[e, at:at + 2] = gu[2 * k:2 * k + 2]
            experts[e, 3 * k + 4 if k < 6 else 20] = wo[k]
    f = lambda a: np.ascontiguousarray(a, dtype=a.dtype)
    out = {
        "par": f(np.concatenate([par[n].reshape(P, k) for n, k in PARAM_SIZES], 1)),
        "con0": table[0], "con1": table[1], "con2": table[2], "masks": masks, "feats": feats, "window": window, "pos": posT,
        "xT": f(x.T.reshape(8, P, TT).transpose(1, 0, 2)),
        "hfw": hfw, "hbias": f(i["e_hy_bias"].reshape(1024)),
        "stream": stream, "experts": experts,
        "lora": f(np.concatenate([i["e_rw_w2"].reshape(64, 512), i["e_rw_a2"].reshape(64, 512)], 0)),
        "g2": f(i["e_rw_g2"][0]),
        "s0rw": f(i["state_rwkv"][0, 0].reshape(2, 4, 2, 64, 64).transpose(2, 4, 0, 1, 3).reshape(P, 2, 4, 64)),
        "s0gd": f(i["state_gdn"][0, 0].transpose(2, 1, 0, 3)),
        "gdrow": f(np.concatenate([i["o_A_log"].reshape(16), i["o_dt_bias"].reshape(16)])),
        "router": f(i["o_router"][0].reshape(8, P, 8).transpose(1, 0, 2)),
    }
    return out


OUTS = {"y": (P, DC, TT), "srw": (P, 2, 4, 64), "sgd": (P, GH, 2, P)}


def unpack(r):
    y = r["y"].transpose(2, 1, 0).reshape(TT, D)
    srw = r["srw"].reshape(2, 64, 2, 4, 64).transpose(2, 3, 0, 4, 1).reshape(1, 1, 2, 8, 64, 64)
    sgd = r["sgd"].transpose(2, 1, 0, 3).reshape(1, 1, 2, GH, P, P)
    c = np.ascontiguousarray
    return c(y[:T].reshape(1, T, D)), c(y[T:].reshape(1, T, D)), c(srw), c(sgd)


def kernel(**inputs):
    import concourse.bacc as bacc
    from concourse.bass_utils import run_bass_kernel_spmd

    nc = bacc.Bacc("TRN2", target_bir_lowering=False, num_devices=1)
    arrays, A = {}, {}
    for name, a in pack(inputs).items():
        arrays["in_" + name] = a
        A[name] = nc.dram_tensor("in_" + name, a.shape, mybir.dt.from_np(a.dtype), kind="ExternalInput").ap()
    O = {n: nc.dram_tensor("out_" + n, s, F32, kind="ExternalOutput").ap() for n, s in OUTS.items()}
    program(nc, A, O)
    r = run_bass_kernel_spmd(nc, [arrays], core_ids=[0])
    return unpack({n: np.asarray(r.results[0]["out_" + n]) for n in OUTS})
```

```python
import math
from contextlib import ExitStack

import numpy as np
import concourse.bass as bass
from concourse import mybir

F32 = mybir.dt.float32
U8 = mybir.dt.uint8
I32 = mybir.dt.int32
ALU = mybir.AluOpType
ACT = mybir.ActivationFunctionType
AX = mybir.AxisListType

P = 128
T = 128
NS = 2
TT = NS * T
D = 1024
DC = D // P
HYC = 4
RWC = 4
RWN = 64
KAPPA = math.exp(-0.5)
GH = 8
FF = 2816
NE = 8
EFF = 3584
RING = 7
TILE = 4096
LEVELS = 7
EVEN_IN_TILES = 7
FFN_IN_TILES = 11
FFN_OUT_TILES = 6
ODD_IN_TILES = 9
EXP_TILES = 21

STREAM = [("ada0a", 4), ("even_in", EVEN_IN_TILES), ("ada0b", 8), ("ada1", 12), ("even_out", 2), ("ffn", 17),
          ("odd_in", ODD_IN_TILES), ("odd_out", 2)]
FIRST = {}
_n = 0
for _name, _k in STREAM:
    FIRST[_name] = _n
    _n += _k
STREAM_TILES = _n

PARAM_SIZES = [("cond", 16), ("ada_b0", 48), ("ada_b1", 48), ("gmix0", 8), ("gmix1", 8), ("gffn0", 8), ("gffn1", 8),
               ("gfin", 8), ("hyw", 36), ("hyb", 12), ("mu", 14), ("w0", 8), ("a0", 8), ("kk", 4), ("ka", 4), ("rk", 4),
               ("lnw", 4), ("lnb", 4), ("gdw", 72), ("normg", 1), ("hfb1", 1), ("hff1", 1), ("hfb2", 1), ("hff2", 1)]
PCOL = {}
_n = 0
for _name, _k in PARAM_SIZES:
    PCOL[_name] = (_n, _k)
    _n += _k
NPARAM = _n

CONST_SIZES = [[("ident", 128), ("ones", 128), ("bones", 128), ("reset", 256), ("iota", 128),
                ("eps6", 1), ("lneps", 1), ("one", 1), ("tie", 64)],
               [("dft_c", 128), ("dft_s", 128), ("inv_c", 128), ("inv_s", 128)],
               [("tri_f", 128), ("tri_b", 128), ("tri_sf", 128), ("tri_sb", 128), ("incl_f", 128), ("incl_b", 128),
                ("strict_f", 128), ("strict_b", 128)]]
CCOL = {}
NCONST = []
for _g, _sizes in enumerate(CONST_SIZES):
    _n = 0
    for _name, _k in _sizes:
        CCOL[_name] = (_g, _n, _k)
        _n += _k
    NCONST.append(_n)


def constants():
    i = np.arange(P)
    row, col = i[:, None], i[None, :]
    f = {}
    f["ident"] = (row == col)
    f["ones"] = np.ones((P, P))
    f["bones"] = (row // 64 == col // 64)
    f["tri_f"] = (row <= col)
    f["tri_b"] = (row >= col)
    f["tri_sf"] = (row > col)
    f["tri_sb"] = (row < col)
    f["incl_f"] = (row <= col)
    f["incl_b"] = (row >= col)
    f["strict_f"] = (col < row)
    f["strict_b"] = (col > row)
    ang = 2 * np.pi * (row + 0.0) * (col + 0.5) / 256.0
    f["dft_c"] = np.cos(ang)
    f["dft_s"] = -np.sin(ang)
    f["inv_c"] = np.cos(ang.T) * (2 / 256.0)
    f["inv_s"] = -np.sin(ang.T) * (2 / 256.0)
    r = np.ones((P, 256))
    r[:, 0] = 0
    r[:, 128] = 0
    f["reset"] = r
    f["iota"] = np.broadcast_to(col, (P, P))
    f["eps6"] = np.full((P, 1), 1e-6)
    f["lneps"] = np.full((P, 1), 64e-5)
    f["one"] = np.ones((P, 1))
    e = np.arange(8)
    f["tie"] = np.broadcast_to((e[None, :] < e[:, None]).reshape(1, 64), (P, 64))
    table = [np.concatenate([np.asarray(f[n], np.float32).reshape(P, k) for n, k in g], 1) for g in CONST_SIZES]
    low = np.zeros((LEVELS, P, P), np.float32)
    for l in range(LEVELS):
        b = 1 << l
        low[l] = ((row // b) % 2 == 1) & (col // b == row // b - 1)
    lev = np.concatenate([low.transpose(1, 0, 2), low.transpose(2, 0, 1)], 1).reshape(P, -1)
    sel = np.concatenate([row < col, row <= col, row > col, row >= col, col < row, col > row], 1).astype(np.float32)
    masks = np.concatenate([lev, sel], 1)
    k = np.arange(T, dtype=np.float32)
    t = (k / np.float32(T - 1)).astype(np.float32)
    bands = np.linspace(1e-4, 15, 16, dtype=np.float32)
    an = (np.float32(2.0 * math.pi) * k / T)[:, None].astype(np.float32) * bands[None, :]
    feats = np.concatenate([t[:, None], np.cos(an), -np.sin(an)], -1).astype(np.float32).T.copy()
    deltas = np.abs(np.linspace(math.log(1e-2) / 0.3, math.log(1e-2) / 1.5, 512, dtype=np.float32))
    win = np.exp(-t[:, None] * deltas[None, :]).astype(np.float32)
    winb = win.copy()
    winb[0] = 0
    window = np.concatenate([win, winb], 1)
    q = D // 4
    omega = np.exp(-math.log(10000.0) * np.arange(q, dtype=np.float32) / q).astype(np.float32)
    tok = np.arange(T)
    rr, cc = (tok // 64).astype(np.float32), (tok % 64).astype(np.float32)
    enc = lambda z: np.concatenate([np.sin(z[:, None] * omega), np.cos(z[:, None] * omega)], -1)
    pos = np.concatenate([enc(rr), enc(cc)], -1).astype(np.float32)
    posT = pos.T.reshape(DC, P, T).transpose(1, 0, 2).copy()
    return table, masks, feats, window, posT


def program(nc, A, O):
    ctx = ExitStack()
    with ctx:
        def sb(name, shape, dt=F32, where=ctx):
            return where.enter_context(nc.sbuf_tensor(name, shape, dt))

        sems = {}

        def sem(name):
            if name not in sems:
                sems[name] = ctx.enter_context(nc.semaphore(name))
            return sems[name]

        class Link:
            def __init__(self, name):
                self.sem, self.n = sem(name), 0

            def __call__(self, eng, ins):
                self.n += 1
                ins.then_inc(self.sem, 1)
                eng.wait_ge(self.sem, self.n)

            def last(self, eng, ins):
                self.n += 1
                ins.then_inc(self.sem, 1)

            def sync(self, eng):
                eng.wait_ge(self.sem, self.n)

        ps = [ctx.enter_context(nc.psum_tensor(f"bank{i}", [P, 512], F32)) for i in range(8)]
        ring = sb("ring", [P, RING, TILE])
        xT = sb("xT", [P, DC, TT])
        par = sb("par", [P, NPARAM])
        con0 = sb("con0", [P, NCONST[0]])
        masks = sb("masks", [P, 2 * LEVELS * P + 6 * P], U8)
        mod = sb("mod", [P, 2, 48, 2])
        scl = sb("scl", [P, 4, DC, 2])
        rstd = sb("rstd", [P, TT])
        silc = sb("silc", [P, DC, 32])
        ARENA = (nc.SBUF_PARTITION_SIZE_BYTES - 16384 - 768 - 4 * (RING * TILE + DC * TT + NPARAM + NCONST[0] + 192 + 64 + TT + 256)
                 - 2 * LEVELS * P - 6 * P) // 4 // 8 * 8
        arena = sb("arena", [P, ARENA])
        floats = [0]

        def take(*shape, rows=P):
            n = 1
            for k in shape:
                n *= k
            assert floats[0] + n <= ARENA, (floats[0], n, ARENA)
            ap = arena[0:rows, floats[0]:floats[0] + n]
            floats[0] += n
            if len(shape) == 1:
                return ap
            names = "abcd"[:len(shape)]
            return ap.rearrange(f"p ({' '.join(names)}) -> p {' '.join(names)}", **{names[i]: shape[i] for i in range(len(shape))})

        def drop(to):
            floats[0] = to

        def pcol(name, i=0, n=None):
            o, k = PCOL[name]
            n = k - i if n is None else n
            return par[:, o + i:o + i + n]

        cons = {0: con0}

        def cc(name):
            g, o, k = CCOL[name]
            return cons[g][:, o:o + k]

        ident, ones, bones = cc("ident"), cc("ones"), cc("bones")
        lvl = masks[:, 0:2 * LEVELS * P].rearrange("p (u l t) -> p u l t", u=2, l=LEVELS)
        selm = masks[:, 2 * LEVELS * P:].rearrange("p (k t) -> p k t", k=6)

        s_const = sem("const_loaded")
        s_slot = [sem(f"slot{i}_loaded") for i in range(RING)]
        s_used = sem("tiles_used")
        dve_link, act_link, pool_link = Link("dve_link"), Link("act_link"), Link("pool_link")

        def slot(n):
            return ring[:, n % RING, :]

        def tile_in(n):
            return slot(n).rearrange("p (j c) -> p j c", j=8)

        def tile_out(n):
            return slot(n).rearrange("p (j c) -> p j c", j=4)

        def arrived(eng, n):
            eng.wait_ge(s_slot[n % RING], 16 * (n // RING + 1))

        def feed(sp, upto):
            while feed.n < min(upto + RING, STREAM_TILES + EXP_TILES * NE):
                n = feed.n
                if n >= RING:
                    sp.wait_ge(s_used, n - RING + 1)
                src = A["stream"][n] if n < STREAM_TILES else A["experts"][(n - STREAM_TILES) // EXP_TILES,
                                                                           (n - STREAM_TILES) % EXP_TILES]
                sp.dma_start(slot(n), src).then_inc(s_slot[n % RING], 16)
                feed.n += 1
        feed.n = 0

        norm_no = [0]
        s_sq, s_ss, s_rt, s_h = sem("squares_done"), sem("sumsq_done"), sem("root_done"), sem("h_ready")

        class Norm:
            def __init__(self, sub, sq):
                self.k, self.sub, self.sq = norm_no[0], sub, sq
                norm_no[0] += 1

            def act_squares(self, act, x_done, each=True):
                for b in range(4):
                    if b == 0 or each:
                        act.wait_ge(s_x, x_done + (b + 1 if each else 1))
                    nc.scalar.activation(self.sq[:, 2 * b:2 * b + 2], xT[:, 2 * b:2 * b + 2], ACT.Square).then_inc(s_sq, 1)

            def pe(self, pe, bank):
                for j in range(DC):
                    if j % 2 == 0:
                        pe.wait_ge(s_sq, 4 * self.k + j // 2 + 1)
                    mm = nc.tensor.matmul(bank[:, 0:TT], ones, self.sq[:, j, :], start=(j == 0), stop=(j == DC - 1))
                mm.then_inc(s_ss, 1)

            def act_root(self, act, bank):
                act.wait_ge(s_ss, self.k + 1)
                nc.scalar.activation(rstd[:], bank[:, 0:TT], ACT.Sqrt, scale=1.0 / D, bias=cc("eps6")).then_inc(s_rt, 1)

            def dve(self, dve, out=None):
                dve.wait_ge(s_rt, self.k + 1)
                dve_link(dve, nc.vector.reciprocal(rstd[:], rstd[:]))
                scaled = []
                for j in range(DC + 1):
                    if j < DC:
                        dve_link.last(dve, nc.vector.tensor_tensor(self.sq[:, j, :], xT[:, j, :], rstd[:], ALU.mult))
                        scaled.append(dve_link.n)
                    if j == 0:
                        continue
                    i = j - 1
                    dve.wait_ge(dve_link.sem, scaled[i])
                    if self.sub is None:
                        nc.vector.tensor_scalar(out[:, i, :], self.sq[:, i, :], pcol("gfin", i, 1), None, ALU.mult)\
                            .then_inc(s_h, 1)
                        continue
                    layer, second = divmod(self.sub, 2)
                    for s in range(NS):
                        sh = mod[:, layer, 24 * second + i, s:s + 1]
                        ins = nc.vector.tensor_scalar(hT[:, i, s * T:(s + 1) * T], self.sq[:, i, s * T:(s + 1) * T],
                                                      scl[:, self.sub, i, s:s + 1], sh, ALU.mult, ALU.add)
                    ins.then_inc(s_h, 1)

            def h_ready(self, eng, j=DC - 1):
                eng.wait_ge(s_h, self.k * DC + j + 1)

        rwp = take(14, TT)
        yT = take(DC, TT)
        m_rw = floats[0]
        hT = take(DC, TT)
        HA = take(2, 512)
        HB = take(2, 512)
        cons[1] = take(NCONST[1])
        m_hy = floats[0]
        drop(0)
        hfw = take(64 * 2 + 2048, rows=64)
        win = take(2, 512)
        hs = take(6, 128, rows=64)
        feats = take(128, rows=33)
        assert floats[0] <= m_rw
        drop(m_hy)
        sq0 = take(DC, TT)
        pos = take(DC, T)
        hbias = take(2, 512)
        filt = take(4, 512)
        fabs = hT.rearrange("p j t -> p (j t)").rearrange("p (k c) -> p k c", k=4)
        fsum = take(2, 2, 512)
        rn = pos.rearrange("p j t -> p (j t)").rearrange("p (o c) -> p o c", o=2)
        s_silc, s_ada, s_adat, s_mod = sem("silu_c_ready"), sem("ada_copied"), sem("ada_transposed"), sem("mod_ready")
        s_hf, s_hfa, s_hfs = sem("filter_mm_done"), sem("filter_arg_ready"), sem("filter_sin_ready")
        s_fw, s_fa, s_fs, s_fn, s_ft = (sem("filter_windowed"), sem("filter_abs_ready"), sem("filter_parts_ready"),
                                        sem("filter_norm_done"), sem("filter_dft_done"))
        s_par = sem("params_loaded")
        n0 = Norm(0, sq0)
        s_x = sem("x_ready")

        ADA_TILES = [FIRST["ada0a"] + k for k in range(4)] + [FIRST["ada0b"] + k for k in range(8)] + \
            [FIRST["ada1"] + k for k in range(12)]
        adac0 = take(TT)
        adac3 = rstd[:]

        def pe_ada(pe, G):
            if G:
                pe.wait_ge(s_mod, G)
            for t in range(2):
                n = ADA_TILES[2 * G + t]
                arrived(pe, n)
                for j in range(DC):
                    for f in range(4):
                        mm = nc.tensor.matmul(ps[7][32 * f:32 * f + 32, t * P:(t + 1) * P], silc[:, j, :],
                                              tile_in(n)[:, j, f * P:(f + 1) * P], start=(j == 0), stop=(j == DC - 1),
                                              tile_position=(0, 32 * f))
                mm.then_inc(s_used, 1)

        def act_ada(act, G, buf):
            used(act, ADA_TILES[2 * G + 1])
            nc.scalar.activation(buf, ps[7][:, 0:TT], ACT.Copy).then_inc(s_ada, 1)

        def pe_ada_t(pe, G, buf):
            pe.wait_ge(s_ada, G + 1)
            for t in range(2):
                mm = nc.tensor.transpose(ps[7][:, t * P:(t + 1) * P], buf[:, t * P:(t + 1) * P], ident)
            mm.then_inc(s_adat, 1)

        def dve_ada(dve, G):
            dve.wait_ge(s_adat, G + 1)
            layer, m = G // 6, 8 * (G % 6)
            nc.vector.tensor_tensor(mod[:, layer, m:m + 8, :],
                                    ps[7][:, 0:TT].rearrange("p (m r) -> p m r", r=32)[:, :, 0:NS],
                                    pcol(f"ada_b{layer}")[:, m:m + 8].unsqueeze(2).broadcast_to([P, 8, 2]), ALU.add)\
                .then_inc(s_mod, 1)

        def used(eng, n):
            eng.wait_ge(s_used, n + 1)

        def dve_scl(dve, sub):
            layer, second = divmod(sub, 2)
            dve.wait_ge(s_mod, 6 * layer + 3 * second + 2)
            g = pcol(["gmix", "gffn"][second] + str(layer)).unsqueeze(2).broadcast_to([P, DC, 2])
            m = 24 * second + 8
            dve_link(dve, nc.vector.tensor_scalar(scl[:, sub], mod[:, layer, m:m + 8, :], 1.0, None, ALU.add))
            dve_link(dve, nc.vector.tensor_tensor(scl[:, sub], scl[:, sub], g, ALU.mult))

        with nc.Block() as block:
            @block.sync
            def _(sp):
                for dst, src in ((par[:], A["par"]), (con0[:], A["con0"]), (xT[:], A["xT"]), (pos[:], A["pos"])):
                    sp.dma_start(dst, src).then_inc(s_par, 16)
                for dst, src in ((hfw[:], A["hfw"]), (feats[:], A["feats"]), (win[:].rearrange("p a c -> p (a c)"), A["window"]),
                                 (hbias[:].rearrange("p a c -> p (a c)"), A["hbias"].partition_broadcast(P)),
                                 (cons[1], A["con1"])):
                    sp.dma_start(dst, src).then_inc(s_const, 16)
                feed(sp, 0)

            @block.gpsimd
            def _(pool):
                nc.gpsimd.memset(silc[:], 0.0).then_inc(s_silc, 1)

            @block.scalar
            def _(act):
                act.wait_ge(s_par, 64)
                act.wait_ge(s_silc, 1)
                nc.scalar.activation(silc[:, :, 0:NS], pcol("cond").rearrange("p (j s) -> p j s", s=NS), ACT.Silu)\
                    .then_inc(s_silc, 1)
                n0.act_squares(act, 0, False)
                n0.act_root(act, ps[0])
                for k in range(2):
                    act.wait_ge(s_hfa, k + 1)
                    nc.scalar.activation(hs[:, 3 * k + 2, :], hs[:, 3 * k + 1, :], ACT.Sin).then_inc(s_hfs, 1)
                for k in range(4):
                    act.wait_ge(s_fw, k + 1)
                    nc.scalar.activation(fabs[:, k, :], filt[:, k, :], ACT.Abs).then_inc(s_fa, 1)
                for G in range(2):
                    act_ada(act, G, adac0)

            @block.tensor
            def _(pe):
                pe.wait_ge(s_par, 64)
                n0.pe(pe, ps[0])
                pe.wait_ge(s_const, 16 * 5)
                nc.tensor.matmul(ps[1][0:64, 0:128], hfw[0:33, 0:64], feats[:], start=True, stop=True).then_inc(s_hf, 1)
                pe.wait_ge(s_hfs, 1)
                nc.tensor.matmul(ps[1][0:64, 0:128], hfw[:, 64:128], hs[:, 2, :], start=True, stop=True).then_inc(s_hf, 1)
                pe.wait_ge(s_hfs, 2)
                for k in range(4):
                    nc.tensor.matmul(ps[2 + k][:], hs[:, 5, :], hfw[:, 128 + 512 * k:640 + 512 * k],
                                     start=True, stop=True).then_inc(s_hf, 1)
                pe.wait_ge(s_rt, 1)
                for o in range(2):
                    for dr in range(2):
                        pe.wait_ge(s_fa, 2 * dr + o + 1)
                        mm = nc.tensor.matmul(ps[o][:], ones, fabs[:, 2 * dr + o, :], start=(dr == 0), stop=(dr == 1))
                    mm.then_inc(s_fn, 1)
                pe.wait_ge(s_fs, 4)
                for o in range(2):
                    nc.tensor.matmul(ps[2 + o][:], cc("dft_c"), fsum[:, 0, o, :], start=True, stop=True).then_inc(s_ft, 1)
                    nc.tensor.matmul(ps[4 + o][:], cc("dft_s"), fsum[:, 1, o, :], start=True, stop=True).then_inc(s_ft, 1)
                pe.wait_ge(s_silc, 2)
                for G in range(2):
                    pe_ada(pe, G)
                    pe_ada_t(pe, G, adac0)

            @block.vector
            def _(dve):
                dve.wait_ge(s_par, 64)
                nc.vector.tensor_tensor(xT[:, :, T:TT], xT[:, :, T:TT], pos[:], ALU.add).then_inc(s_x, 1)

                def sine_arg(k, bank):
                    a, r = hs[:, 3 * k, :], hs[:, 3 * k + 1, :]
                    dve_link(dve, nc.vector.tensor_scalar(a, bank, pcol(f"hfb{k + 1}")[0:64], pcol(f"hff{k + 1}")[0:64],
                                                          ALU.add, ALU.mult))
                    magic = 1.5 * 2 ** 23
                    dve_link(dve, nc.vector.tensor_scalar(r, a, 1 / (2 * math.pi), magic, ALU.mult, ALU.add))
                    dve_link(dve, nc.vector.tensor_scalar(r, r, -magic, None, ALU.add))
                    c1 = 6.28125
                    c2 = 2 * math.pi - c1
                    dve_link(dve, nc.vector.scalar_tensor_tensor(a, r, -c1, a, ALU.mult, ALU.add))
                    dve_link(dve, nc.vector.scalar_tensor_tensor(a, r, -c2, a, ALU.mult, ALU.add))
                    nc.vector.tensor_scalar(r, a, math.pi * (1 - 1e-7), -math.pi * (1 - 1e-7), ALU.min, ALU.max)\
                        .then_inc(s_hfa, 1)

                dve.wait_ge(s_hf, 1)
                sine_arg(0, ps[1][0:64, 0:128])
                dve.wait_ge(s_hf, 2)
                sine_arg(1, ps[1][0:64, 0:128])
                dve.wait_ge(s_const, 16 * 5)
                for k in range(4):
                    dve.wait_ge(s_hf, 3 + k)
                    nc.vector.tensor_tensor(filt[:, k, :], ps[2 + k][:], win[:, k // 2, :], ALU.mult).then_inc(s_fw, 1)
                dve.wait_ge(s_fw, 4)
                for o in range(2):
                    nc.vector.tensor_tensor(fsum[:, 0, o, :], filt[:, o, :], filt[:, 2 + o, :], ALU.add).then_inc(s_fs, 1)
                    nc.vector.tensor_tensor(fsum[:, 1, o, :], filt[:, o, :], filt[:, 2 + o, :], ALU.subtract)\
                        .then_inc(s_fs, 1)
                for o in range(2):
                    dve.wait_ge(s_fn, o + 1)
                    dve_link.last(dve, nc.vector.reciprocal(rn[:, o, :], ps[o][:]))
                dve_link.sync(dve)
                for o in range(2):
                    dve.wait_ge(s_ft, 2 * o + 2)
                    dve_link(dve, nc.vector.tensor_tensor(HA[:, o, :], ps[2 + o][:], rn[:, o, :], ALU.mult))
                    dve_link.last(dve, nc.vector.tensor_tensor(HA[:, o, :], HA[:, o, :], hbias[:, o, :], ALU.add))
                    dve_link.last(dve, nc.vector.tensor_tensor(HB[:, o, :], ps[4 + o][:], rn[:, o, :], ALU.mult))
                dve_link.sync(dve)
                for G in range(2):
                    dve_ada(dve, G)
                dve_scl(dve, 0)
                n0.dve(dve)

        drop(m_hy)
        u = take(12, TT)
        m_u = floats[0]
        pad = take(4, NS, T + 2)
        tmp = take(2, NS, T)
        mus = take(2, 14)
        s_p, s_pad, s_pz, s_pc = sem("proj_done"), sem("proj_padded"), sem("pads_zeroed"), sem("pad_consumed")
        mask_f = take(2 * LEVELS * P + 6 * P)
        lora = arena[:, ARENA - 1024:ARENA - 512]
        s0 = arena[:, ARENA - 512:].rearrange("p (g c v) -> p g c v", g=2, c=4)
        assert floats[0] <= ARENA - 1024
        s_rwc = sem("rwkv_params_loaded")
        EC = 26

        def projected(eng, m, last, first, before=0):
            if m % 4 == 3 or m == last:
                used(eng, first + m // 4)
            else:
                eng.wait_ge(s_p, before + m - m // 4 + 1)

        with nc.Block() as block:
            @block.sync
            def _(sp):
                sp.dma_start(mask_f, A["masks"]).then_inc(s_par, 16)
                for dst, src in ((lora, A["lora"]), (s0, A["s0rw"])):
                    sp.dma_start(dst, src).then_inc(s_rwc, 16)
                feed(sp, FIRST["even_in"] + EVEN_IN_TILES - 4)

            @block.gpsimd
            def _(pool):
                nc.gpsimd.memset(pad[:], 0.0).then_inc(s_pz, 1)
                pool.wait_ge(s_par, 80)
                nc.gpsimd.tensor_copy(masks[:], mask_f)

            @block.scalar
            def _(act):
                act.wait_ge(s_pz, 1)
                for m in range(EC):
                    projected(act, m, EC - 1, FIRST["even_in"])
                    if m >= 4:
                        act.wait_ge(s_pc, m - 3)
                    rows = 96 if m == EC - 1 else P
                    src = ps[m % 4][0:rows, 0:TT].rearrange("p (s t) -> p s t", s=NS)
                    nc.scalar.activation(pad[0:rows, m % 4, :, 1:T + 1], src, ACT.Copy).then_inc(s_pad, 1)

            @block.tensor
            def _(pe):
                for m in range(EC):
                    n = FIRST["even_in"] + m // 4
                    if m % 4 == 0:
                        arrived(pe, n)
                    if m >= 4:
                        pe.wait_ge(s_pad, m - 3)
                    rows = 96 if m == EC - 1 else P
                    f = m % 4
                    for j in range(DC):
                        mm = nc.tensor.matmul(ps[m % 4][0:rows, 0:TT], tile_in(n)[:, j, f * P:f * P + rows], hT[:, j, :],
                                              start=(j == 0), stop=(j == DC - 1))
                    mm.then_inc(s_used if f == 3 or m == EC - 1 else s_p, 1)

            @block.vector
            def _(dve):
                dve_link(dve, nc.vector.tensor_scalar(mus[:, 0, :], pcol("mu"), -1.0, 1.0, ALU.mult, ALU.add))
                dve_link(dve, nc.vector.tensor_scalar(mus[:, 1, :], pcol("mu"), 0.5, None, ALU.mult))
                for m in range(EC):
                    dve.wait_ge(s_pad, m + 1)
                    rows = 96 if m == EC - 1 else P
                    left, mid, right = (pad[0:rows, m % 4, :, k:k + T] for k in range(3))
                    a = tmp[0:rows, 0]
                    if m < 12:
                        out = u[:, m, :].rearrange("p (s t) -> p s t", s=NS)
                        w = pcol("hyw")
                        dve_link(dve, nc.vector.tensor_scalar(a, mid, w[:, 12 + m:13 + m], pcol("hyb", m, 1), ALU.mult, ALU.add))
                        dve_link(dve, nc.vector.scalar_tensor_tensor(out, left, w[:, m:m + 1], a, ALU.mult, ALU.add))
                        nc.vector.scalar_tensor_tensor(out, right, w[:, 24 + m:25 + m], out, ALU.mult, ALU.add)\
                            .then_inc(s_pc, 1)
                        dve.wait_ge(s_pc, m + 1)
                    else:
                        q = m - 12
                        out = rwp[0:rows, q, :].rearrange("p (s t) -> p s t", s=NS)
                        b = tmp[0:rows, 1]
                        dve_link.last(dve, nc.vector.tensor_tensor(a, left, right, ALU.add))
                        dve_link(dve, nc.vector.tensor_scalar(b, mid, mus[0:rows, 0, q:q + 1], None, ALU.mult))
                        nc.vector.scalar_tensor_tensor(out, a, mus[0:rows, 1, q:q + 1], b, ALU.mult, ALU.add)\
                            .then_inc(s_pc, 1)
                        dve.wait_ge(s_pc, m + 1)

        drop(m_u)
        vt = hT.rearrange("p j t -> p (j t)").rearrange("p (g s c) -> p g s c", g=2, s=NS)
        za = take(4, 512)
        sp_ab = take(2, 512)
        adac2 = take(TT)
        s_tr, s_vt, s_z, s_y, s_zt = (sem("hy_transposed"), sem("hy_token_major"), sem("hy_dft_done"),
                                      sem("hy_spectrum_ready"), sem("hy_time_done"))
        s_z1 = sem("hy_gated")

        with nc.Block() as block:
            @block.sync
            def _(sp):
                feed(sp, FIRST["ada0b"] + 8 - 4)

            @block.gpsimd
            def _(pool):
                pass

            @block.scalar
            def _(act):
                for k in range(4):
                    act.wait_ge(s_tr, k + 1)
                    nc.scalar.activation(vt[:, k // 2, k % 2, :], ps[k][:], ACT.Copy).then_inc(s_vt, 1)
                for k in range(4):
                    act_ada(act, 2 + k, adac2)

            @block.tensor
            def _(pe):
                for k in range(4):
                    g, s = divmod(k, 2)
                    for c in range(HYC):
                        mm = nc.tensor.transpose(ps[k][:, c * P:(c + 1) * P], u[:, 4 * g + c, s * T:(s + 1) * T], ident)
                    mm.then_inc(s_tr, 1)
                for o in range(2):
                    for s in range(NS):
                        k = 2 * o + s
                        if o == 0:
                            pe.wait_ge(s_vt, s + 1)
                        else:
                            pe.wait_ge(s_z1, s + 1)
                        if k >= 1:
                            pe.wait_ge(s_y, k)
                        if k == 0:
                            pe.wait_ge(s_vt, 2)
                        nc.tensor.matmul(ps[4][:], cc("dft_c"), vt[:, 0, s, :], start=True, stop=True)
                        nc.tensor.matmul(ps[5][:], cc("dft_s"), vt[:, 0, s, :], start=True, stop=True).then_inc(s_z, 1)
                        pe_ada(pe, 2 + k)
                        pe.wait_ge(s_y, k + 1)
                        if o == 0:
                            nc.tensor.matmul(ps[s][:], cc("inv_c"), sp_ab[:, 0, :], start=True, stop=False)
                            nc.tensor.matmul(ps[s][:], cc("inv_s"), sp_ab[:, 1, :], start=False, stop=True)\
                                .then_inc(s_zt, 1)
                        else:
                            for c in range(HYC):
                                out = ps[s][:, c * P:(c + 1) * P]
                                nc.tensor.matmul(out, sp_ab[:, 0, c * P:(c + 1) * P], cc("inv_c"), start=True, stop=False)
                                mm = nc.tensor.matmul(out, sp_ab[:, 1, c * P:(c + 1) * P], cc("inv_s"),
                                                      start=False, stop=True)
                            mm.then_inc(s_zt, 1)
                        pe_ada_t(pe, 2 + k, adac2)

            @block.vector
            def _(dve):
                for o in range(2):
                    for s in range(NS):
                        k = 2 * o + s
                        dve.wait_ge(s_z, k + 1)
                        for i, (bank, h) in enumerate(((ps[4], HA), (ps[5], HB), (ps[4], HB), (ps[5], HA))):
                            dve_link.last(dve, nc.vector.tensor_tensor(za[:, i, :], bank[:], h[:, o, :], ALU.mult))
                        dve_link.sync(dve)
                        if k >= 1:
                            dve.wait_ge(s_zt, k)
                        dve_link(dve, nc.vector.tensor_tensor(sp_ab[:, 0, :], za[:, 0, :], za[:, 1, :], ALU.subtract))
                        nc.vector.tensor_tensor(sp_ab[:, 1, :], za[:, 2, :], za[:, 3, :], ALU.add).then_inc(s_y, 1)
                        dve.wait_ge(s_zt, k + 1)
                        if o == 0:
                            dve.wait_ge(s_vt, 4)
                            nc.vector.tensor_tensor(vt[:, 0, s, :], ps[s][:], vt[:, 1, s, :], ALU.mult).then_inc(s_z1, 1)
                        else:
                            dve_link(dve, nc.vector.tensor_tensor(
                                yT[:, 0:4, s * T:(s + 1) * T], ps[s][:].rearrange("p (c t) -> p c t", c=4),
                                u[:, 8:12, s * T:(s + 1) * T], ALU.mult))
                        dve_ada(dve, 2 + k)
                dve_scl(dve, 1)
        s_id, s_T, s_U = ([sem(f"{n}{g}") for g in range(2)] for n in ("identity_set", "T_level_done", "U_level_done"))
        s_X, s_Xs, s_TX, s_XU = ([sem(f"{n}{g}") for g in range(2)] for n in ("AT_done", "AT_copied", "TAT_done", "TATt_done"))
        NT, NU = (LEVELS - 1, LEVELS), (LEVELS, LEVELS - 1)
        NTX, NXU = (LEVELS - 2, LEVELS - 1), (LEVELS - 1, LEVELS - 2)

        class Inversion:
            def __init__(self):
                self.T = [take(4, T) for _ in range(2)]
                self.U = [take(4, T) for _ in range(2)]
                self.X = [take(4, T) for _ in range(2)]
                self.final = [self.U[0], self.T[1]]

            def pool_reset(self, pool, g):
                eye = ident.unsqueeze(1).broadcast_to([P, 4, T])
                nc.gpsimd.tensor_copy(self.T[g], eye).then_inc(s_id[g], 1)
                nc.gpsimd.tensor_copy(self.U[g], eye).then_inc(s_id[g], 1)

            def level_mask(self, upper, l):
                return lvl[:, upper, l, :].unsqueeze(1).broadcast_to([P, 4, T])

            def dve_first(self, dve, r, g, low, up):
                dve.wait_ge(s_id[g], 2 * (r + 1))
                nc.vector.copy_predicated(self.T[g], self.level_mask(0, 0), low).then_inc(s_T[g], 1)
                nc.vector.copy_predicated(self.U[g], self.level_mask(1, 0), up).then_inc(s_U[g], 1)

            def pe_level(self, pe, r, l, up):
                for g in range(2):
                    pe.wait_ge(s_T[g], r * NT[g] + l)
                    for q in range(4):
                        mm = nc.tensor.matmul(ps[g][:, q * T:(q + 1) * T], up[g][:, q], self.T[g][:, q], start=True, stop=True)
                    mm.then_inc(s_X[g], 1)
                for g in range(2):
                    pe.wait_ge(s_U[g], r * NU[g] + l)
                    pe.wait_ge(s_Xs[g], r * (LEVELS - 1) + l)
                    if l < LEVELS - 1 or g == 1:
                        for q in range(4):
                            mm = nc.tensor.matmul(ps[2 + g][:, q * T:(q + 1) * T], self.U[g][:, q], self.X[g][:, q],
                                                  start=True, stop=True)
                        mm.then_inc(s_TX[g], 1)
                    if l < LEVELS - 1 or g == 0:
                        for q in range(4):
                            mm = nc.tensor.matmul(ps[4 + g][:, q * T:(q + 1) * T], self.X[g][:, q], self.U[g][:, q],
                                                  start=True, stop=True)
                        mm.then_inc(s_XU[g], 1)

            def act_level(self, act, r, l):
                for g in range(2):
                    act.wait_ge(s_X[g], r * (LEVELS - 1) + l)
                    nc.scalar.activation(self.X[g].rearrange("p q t -> p (q t)"), ps[g][:], ACT.Copy).then_inc(s_Xs[g], 1)

            def dve_level(self, dve, r, l):
                for g in range(2):
                    if l < LEVELS - 1 or g == 1:
                        dve.wait_ge(s_TX[g], r * NTX[g] + l)
                        dve.wait_ge(s_T[g], r * NT[g] + l)
                        nc.vector.copy_predicated(self.T[g], self.level_mask(0, l),
                                                  ps[2 + g][:].rearrange("p (q t) -> p q t", q=4)).then_inc(s_T[g], 1)
                    if l < LEVELS - 1 or g == 0:
                        dve.wait_ge(s_XU[g], r * NXU[g] + l)
                        dve.wait_ge(s_U[g], r * NU[g] + l)
                        nc.vector.copy_predicated(self.U[g], self.level_mask(1, l),
                                                  ps[4 + g][:].rearrange("p (q t) -> p q t", q=4)).then_inc(s_U[g], 1)

            def pe_final(self, pe, r, g):
                pe.wait_ge(s_U[0] if g == 0 else s_T[1], (r + 1) * LEVELS)

        drop(m_rw)
        m_keep = floats[0]
        inv = Inversion()
        AT = [take(4, 4, T) for _ in range(2)]
        Ab = [take(4, T) for _ in range(2)]
        ar = [take(2, TT) for _ in range(2)]
        bk = [take(2, TT) for _ in range(2)]
        bkt = [take(2, T) for _ in range(2)]
        vtok = take(NS, T)
        Q, W = take(TT), take(TT)
        sg, av, kd = take(TT), take(TT), take(TT)
        kk, ksq, knm = take(TT), Q, W
        bon = take(TT)
        Gs = [inv.X[g][:, 0:2, :].rearrange("p a (b v) -> p (a b) v", b=2) for g in range(2)]
        Zs = [inv.X[g][:, 2:4, :].rearrange("p a (b v) -> p (a b) v", b=2) for g in range(2)]
        half = lambda x, i: x[:, 2 * i:2 * i + 2, :].rearrange("p a t -> p (a t)")
        sgs, avs, Qs, Ws = ([sg, half(inv.X[0], 0)], [av, half(inv.X[0], 1)], [Q, half(inv.X[1], 0)], [W, half(inv.X[1], 1)])
        LORA_BANK = [[(6, 0), (4, TT)], [(5, TT), (0, 0)]]
        s0s = [take(2, RWN) for _ in range(2)]
        hp = [take(NS) for _ in range(2)]
        eh = [take(NS) for _ in range(2)]
        sst = s0
        y4 = yT[:, 4:8, :].rearrange("p c t -> p (c t)")
        g2 = AT[1].rearrange("p q k t -> p (q k t)")[0:96, 0:512]
        ybuf, std = Q, W
        s_zero = sem("scores_zeroed")
        s_kr, s_ksq, s_kss, s_krt = sem("kk_raw_ready"), sem("kk_squared"), sem("kk_sumsq_done"), sem("kk_root_done")
        s_tanh, s_sigg = sem("lora_tanh_done"), sem("lora_gate_done")
        s_lor, s_sg, s_Q, s_exp, s_unit = (sem("lora_done"), sem("sigmoids_done"), sem("decay_sums_ready"),
                                           sem("decays_ready"), sem("unit_ready"))
        s_gen, s_sel, s_tk, s_tks = sem("scores_done"), sem("scores_masked"), sem("tok_major_done"), sem("tok_major_copied")
        s_G, s_Gs, s_Z, s_Zs = sem("rhs_done"), sem("rhs_copied"), sem("solved"), sem("solution_copied")
        s_Y, s_Ys, s_S, s_Ss = sem("rw_out_done"), sem("rw_out_copied"), sem("rw_state_done"), sem("rw_state_copied")
        s_s0, s_bon, s_bss, s_bons = sem("s0_scaled"), sem("bonus_arg_ready"), sem("bonus_sum_done"), sem("bonus_ready")
        s_mn, s_yc, s_ysq, s_vr, s_std = (sem("ln_mean_done"), sem("ln_centred"), sem("ln_squared"), sem("ln_var_done"),
                                          sem("ln_root_done"))
        s_gg, s_stored = sem("gate_lora_done"), sem("state_stored")
        v3 = lambda ap: ap.rearrange("p (s t) -> p s t", s=NS)

        def ada_groups(c, g):
            k = {(0, 0): 0, (0, 1): 1, (1, 0): 2, (1, 1): 3, (2, 0): 4, (3, 0): 5}.get((c, g))
            return [] if k is None else [6 + k]

        with nc.Block() as block:
            @block.sync
            def _(sp):
                feed(sp, FIRST["ada1"] + 12)
                sp.wait_ge(s_Y, RWC)
                sp.dma_start(g2, A["g2"]).then_inc(s_rwc, 16)
                sp.wait_ge(s_Ss, 8)
                sp.dma_start(O["srw"], sst).then_inc(s_stored, 16)
                sp.wait_ge(s_stored, 16)

            @block.gpsimd
            def _(pool):
                for part in (*bk, s0s[0], AT[0], Ab[0], s0s[1], AT[1], Ab[1]):
                    nc.gpsimd.memset(part, 0.0).then_inc(s_zero, 1)
                for c in range(RWC):
                    for g in range(2):
                        if c:
                            pool.wait_ge(s_Z, 2 * c)
                        inv.pool_reset(pool, g)

            @block.scalar
            def _(act):
                nc.scalar.activation(rwp[0:64, 12, :], rwp[0:64, 12, :], ACT.Tanh).then_inc(s_tanh, 1)
                nc.scalar.activation(rwp[0:96, 13, :], rwp[0:96, 13, :], ACT.Sigmoid).then_inc(s_sigg, 1)

                def key_squares(c):
                    act.wait_ge(s_kr, c + 1)
                    nc.scalar.activation(ksq, kk, ACT.Square).then_inc(s_ksq, 1)

                def key_norm(c):
                    act.wait_ge(s_kss, c + 1)
                    nc.scalar.activation(knm, ps[7][:, 256:512], ACT.Sqrt).then_inc(s_krt, 1)

                def square(c):
                    act.wait_ge(s_yc, c + 1)
                    nc.scalar.activation(ybuf, yT[:, 4 + c, :], ACT.Square).then_inc(s_ysq, 1)

                def deviation(c):
                    act.wait_ge(s_vr, c + 1)
                    nc.scalar.activation(std, ps[6][:, TT:2 * TT], ACT.Sqrt, scale=1 / 64.0, bias=cc("lneps")).then_inc(s_std, 1)

                key_squares(0)
                key_norm(0)
                for c in range(RWC):
                    act.wait_ge(s_tk, 3 * c + 1)
                    if c:
                        act.wait_ge(s_S, 2 * c)
                    nc.scalar.activation(vtok.rearrange("p s t -> p (s t)"), ps[7][:, 256:512], ACT.Copy).then_inc(s_tks, 1)
                    act.wait_ge(s_lor, c + 1)
                    if c:
                        act.wait_ge(s_unit, 2 * c)
                    for g in range(2):
                        for i, (dst, bias) in enumerate(((sgs, "w0"), (avs, "a0"))):
                            bank, o = LORA_BANK[i][g]
                            nc.scalar.activation(dst[g], ps[bank][:, o:o + TT], ACT.Sigmoid, bias=pcol(bias, 4 * g + c, 1))\
                                .then_inc(s_sg, 1)
                    if c:
                        act.wait_ge(s_Y, c)
                    for g in range(2):
                        act.wait_ge(s_Q, 2 * c + g + 1)
                        incl, excl, sign = (Qs[0], Ws[0], -KAPPA) if g == 0 else (Ws[1], Qs[1], KAPPA)
                        nc.scalar.activation(ar[g][:, 0, :], excl, ACT.Exp, scale=sign).then_inc(s_exp, 1)
                        nc.scalar.activation(ar[g][:, 1, :], incl, ACT.Exp, scale=sign).then_inc(s_exp, 1)
                        nc.scalar.activation(sgs[g], incl, ACT.Exp, scale=-sign).then_inc(s_exp, 1)
                        nc.scalar.activation(eh[g], hp[g], ACT.Exp, scale=-KAPPA).then_inc(s_exp, 1)
                    for g in range(2):
                        for G in ada_groups(c, g):
                            act_ada(act, G, adac3)
                        act.wait_ge(s_tk, 3 * c + 2 + g)
                        nc.scalar.activation(bkt[g].rearrange("p a t -> p (a t)"), ps[6][:, TT:2 * TT], ACT.Copy).then_inc(s_tks, 1)
                    if c < RWC - 1:
                        key_squares(c + 1)
                    for l in range(1, LEVELS):
                        inv.act_level(act, c, l)
                        if l == 1 and c < RWC - 1:
                            key_norm(c + 1)
                        if l == 3 and c:
                            square(c - 1)
                        if l == 4 and c:
                            deviation(c - 1)
                    for g in range(2):
                        act.wait_ge(s_G, 2 * c + g + 1)
                        nc.scalar.activation(Gs[g].rearrange("p q v -> p (q v)"), ps[g][:, 0:TT], ACT.Copy).then_inc(s_Gs, 1)
                square(RWC - 1)
                deviation(RWC - 1)

            @block.tensor
            def _(pe):
                pe.wait_ge(s_rwc, 32)
                pe.wait_ge(s_tanh, 1)

                def unit_key(c):
                    pe.wait_ge(s_ksq, c + 1)
                    pe.wait_ge(s_mod, 6 + (2 * c if c < 3 else 5))
                    nc.tensor.matmul(ps[7][:, 256:512], bones, ksq, start=True, stop=True).then_inc(s_kss, 1)

                def mean(c):
                    pe.wait_ge(s_Ys, c + 1)
                    pe.wait_ge(s_bons, c + 1)
                    nc.tensor.matmul(ps[6][:, 0:TT], bones, yT[:, 4 + c, :], start=True, stop=True).then_inc(s_mn, 1)

                def variance(c):
                    pe.wait_ge(s_ysq, c + 1)
                    nc.tensor.matmul(ps[6][:, TT:2 * TT], bones, ybuf, start=True, stop=True).then_inc(s_vr, 1)

                unit_key(0)
                for c in range(RWC):
                    if c:
                        pe.wait_ge(s_U[1], c * NU[1])
                        pe.wait_ge(s_Ys, c)
                        pe.wait_ge(s_bons, c)
                    pe.wait_ge(s_krt, c + 1)
                    for s in range(NS):
                        mm = nc.tensor.transpose(ps[7][:, TT + s * T:TT + (s + 1) * T], rwp[:, 8 + c, s * T:(s + 1) * T], ident)
                    mm.then_inc(s_tk, 1)
                    for g in range(2):
                        for i in range(2):
                            b = 64 * i + 32 * g
                            bank, o = LORA_BANK[i][g]
                            mm = nc.tensor.matmul(ps[bank][:, o:o + TT], lora[b:b + 32, c * P:(c + 1) * P],
                                                  rwp[b:b + 32, 12, :], start=True, stop=True, tile_position=(b, 0))
                    mm.then_inc(s_lor, 1)
                    for g in range(2):
                        k = 2 * c + g
                        if g == 0:
                            pe.wait_ge(s_tks, 3 * c + 1)
                        for G in ada_groups(c, g):
                            pe_ada(pe, G)
                        pe.wait_ge(s_unit, k + 1)
                        pe.wait_ge(s_sg, 4 * (c + 1))
                        if k:
                            pe.wait_ge(s_sel, 6 * k)
                        if c and g == 0:
                            pe.wait_ge(s_Zs, 2 * c)
                            pe.wait_ge(s_Ss, 2 * c)
                        for q in range(4):
                            s, hh = divmod(q, 2)
                            tok = slice(s * T, (s + 1) * T)
                            for i in range(2):
                                nc.tensor.matmul(ps[q][:, i * TT:(i + 1) * TT].rearrange("p (a t) -> p a t", a=2),
                                                 bk[hh][:, i, tok], ar[g][:, :, tok], start=True, stop=True)
                            mm = nc.tensor.matmul(ps[4 + hh][:, s * T:(s + 1) * T], ar[g][:, 0, tok], bk[hh][:, 0, tok],
                                                  start=True, stop=True)
                        mm.then_inc(s_gen, 1)
                        for G in ada_groups(c, g):
                            pe_ada_t(pe, G, adac3)
                        pe.wait_ge(s_tks, 3 * c + 1 + g)
                        for i in range(2):
                            for hh in range(2):
                                mm = nc.tensor.matmul(ps[6][:, TT + i * T:TT + (i + 1) * T], bk[hh][:, i, 0:T], ident,
                                                      start=(hh == 0), stop=(hh == 1))
                        mm.then_inc(s_tk, 1)
                    pe.wait_ge(s_tks, 3 * c + 3)
                    pe.wait_ge(s_sel, 6 * (2 * c + 2))
                    up = [AT[0][:, :, 0, :], Ab[1]]
                    for l in range(1, LEVELS):
                        inv.pe_level(pe, c, l, up)
                        if l == 1 and c < RWC - 1:
                            unit_key(c + 1)
                        if l == 2 and c:
                            mean(c - 1)
                        if l == 3 and c:
                            variance(c - 1)
                    for g in range(2):
                        if g == 0:
                            pe.wait_ge(s_s0, 4 * c + 4)
                        for s in range(NS):
                            if s:
                                nc.tensor.matmul(ps[g][:, T:2 * T].rearrange("p (h v) -> p h v", h=2), ar[g][:, 0, T:TT],
                                                 s0s[g], start=True, stop=False)
                            for hh in range(2):
                                q = 2 * s + hh
                                mm = nc.tensor.matmul(ps[g][:, q * RWN:(q + 1) * RWN], AT[g][:, q, 2, :],
                                                      vtok[:, s, 64 * hh:64 * hh + 64], start=(s == 0), stop=(s == 0 or hh == 1))
                        mm.then_inc(s_G, 1)
                    for g in range(2):
                        inv.pe_final(pe, c, g)
                        pe.wait_ge(s_Gs, 2 * c + g + 1)
                        for q in range(4):
                            mm = nc.tensor.matmul(ps[g][:, TT + q * RWN:TT + (q + 1) * RWN], inv.final[g][:, q], Gs[g][:, q, :],
                                                  start=True, stop=True)
                        mm.then_inc(s_Z, 1)
                    pe.wait_ge(s_Zs, 2 * c + 2)
                    if c:
                        pe.wait_ge(s_std, c)
                    for q in range(4):
                        s, hh = divmod(q, 2)
                        rows, tok = slice(64 * hh, 64 * hh + 64), slice(s * T, (s + 1) * T)
                        out = ps[6][rows, tok]
                        for g in range(2):
                            nc.tensor.matmul(out, Zs[g][:, q, :], AT[g][:, q, 1, :], start=(g == 0), stop=False)
                            if s:
                                nc.tensor.matmul(out, s0s[g][:, hh, :], ar[g][:, 1, tok], start=False, stop=False)
                            mm = nc.tensor.matmul(out, vtok[:, s, rows], AT[g][:, q, 3, :], start=False, stop=(g == 1))
                    mm.then_inc(s_Y, 1)
                    for g in range(2):
                        nc.tensor.matmul(ps[2 + g][:, 0:T], bkt[g][:, 0, :], Zs[g][:, 0:2, :].rearrange("p q v -> p (q v)"),
                                         start=True, stop=False)
                        nc.tensor.matmul(ps[2 + g][:, 0:T], bkt[g][:, 1, :], vtok[:, 0, :], start=False, stop=True)\
                            .then_inc(s_S, 1)
                    pe.wait_ge(s_bon, c + 1)
                    pe.wait_ge(s_Ys, c + 1)
                    nc.tensor.matmul(ps[6][:, TT:2 * TT], bones, bon, start=True, stop=True).then_inc(s_bss, 1)
                mean(RWC - 1)
                pe.wait_ge(s_sigg, 1)
                pe.wait_ge(s_rwc, 48)
                for c in range(RWC):
                    mm = nc.tensor.matmul(ps[4 + c // 2][:, (c % 2) * TT:(c % 2 + 1) * TT], g2[:, c * P:(c + 1) * P],
                                          rwp[0:96, 13, :], start=True, stop=True)
                mm.then_inc(s_gg, 1)
                variance(RWC - 1)

            @block.vector
            def _(dve):
                V = nc.vector

                def raw_key(c):
                    V.tensor_scalar(kk, rwp[:, 4 + c, :], pcol("kk", c, 1), None, ALU.mult).then_inc(s_kr, 1)

                def unit_key(c):
                    dve.wait_ge(s_krt, c + 1)
                    dve_link(dve, V.tensor_scalar(knm, knm, 1e-12, None, ALU.max))
                    dve_link(dve, V.reciprocal(knm, knm))
                    dve_link(dve, V.tensor_tensor(kk, kk, knm, ALU.mult))

                def centre(c):
                    y = yT[:, 4 + c, :]
                    dve.wait_ge(s_mn, c + 1)
                    V.scalar_tensor_tensor(y, ps[6][:, 0:TT], -1 / 64.0, y, ALU.mult, ALU.add).then_inc(s_yc, 1)

                def norm(c):
                    y = yT[:, 4 + c, :]
                    dve.wait_ge(s_std, c + 1)
                    dve_link(dve, V.reciprocal(std, std))
                    dve_link(dve, V.tensor_tensor(y, y, std, ALU.mult))
                    dve_link(dve, V.tensor_scalar(y, y, pcol("lnw", c, 1), pcol("lnb", c, 1), ALU.mult, ALU.add))
                    dve_link.last(dve, V.tensor_tensor(y, y, rwp[:, c, :], ALU.add))

                raw_key(0)
                unit_key(0)
                for c in range(RWC):
                    r, kc, vc = (rwp[:, i + c, :] for i in (0, 4, 8))

                    def sums(g):
                        k = 2 * c + g
                        Q, W, sg, av = Qs[g], Ws[g], sgs[g], avs[g]
                        dve.wait_ge(s_sg, 2 * (k + 1))
                        if c:
                            dve.wait_ge(s_exp, 4 * k)
                            dve.wait_ge(s_S, 2 * c)
                        dve_link(dve, V.tensor_tensor_scan(Q, cc("reset"), sg, 0.0, ALU.mult, ALU.add))
                        dve_link(dve, V.tensor_scalar(hp[g], v3(Q)[:, :, T - 1], 0.5, None, ALU.mult))
                        dve_link(dve, V.tensor_tensor(v3(Q), v3(Q), hp[g].unsqueeze(2).broadcast_to([P, NS, T]), ALU.subtract))
                        V.tensor_tensor(W, Q, sg, ALU.subtract).then_inc(s_Q, 1)
                        dve_link(dve, V.tensor_scalar(kd, av, -1.0, pcol("ka", c, 1), ALU.add, ALU.mult))
                        dve_link(dve, V.scalar_tensor_tensor(kd, kd, 1.0, kc, ALU.add, ALU.mult))
                        if g == 0:
                            if c:
                                dve.wait_ge(s_bss, c)
                            dve_link.last(dve, V.tensor_copy(bon, kd))
                        else:
                            dve_link.last(dve, V.tensor_tensor(bon, bon, kd, ALU.add))
                        dve_link(dve, V.tensor_tensor(av, av, kk, ALU.mult))

                    def unit(g):
                        k = 2 * c + g
                        dve.wait_ge(s_exp, 4 * (k + 1))
                        if k:
                            dve.wait_ge(s_tk, 3 * ((k - 1) // 2) + 2 + (k - 1) % 2)
                        else:
                            dve.wait_ge(s_zero, 3)
                            dve.wait_ge(s_rwc, 32)
                        if k == 1:
                            dve.wait_ge(s_zero, 6)
                        dve_link.last(dve, V.scalar_tensor_tensor(ar[g][:, 0, :], ar[g][:, 0, :], -1.0, kk, ALU.mult, ALU.mult))
                        dve_link.last(dve, V.tensor_tensor(ar[g][:, 1, :], ar[g][:, 1, :], r, ALU.mult))
                        for i, f in enumerate((avs[g], kd)):
                            for hh in range(2):
                                rows = slice(64 * hh, 64 * hh + 64)
                                ins = V.tensor_tensor(bk[hh][rows, i, :], sgs[g][rows], f[rows], ALU.mult)
                                if (i, hh) != (1, 1):
                                    dve_link.last(dve, ins)
                        ins.then_inc(s_unit, 1)
                        if c:
                            dve.wait_ge(s_Y, c)
                        for hh in range(2):
                            rows = slice(64 * hh, 64 * hh + 64)
                            V.tensor_scalar(s0s[g][rows, hh, :], s0[rows, g, c, :], eh[g][rows, 1:2], None, ALU.mult)\
                                .then_inc(s_s0, 1)

                    def select(g):
                        k = 2 * c + g
                        for G in ada_groups(c, g):
                            dve_ada(dve, G)
                        dve.wait_ge(s_gen, k + 1)
                        if c == 0:
                            dve.wait_ge(s_zero, 5 + 3 * g)
                        for q in range(4):
                            V.copy_predicated(AT[g][:, q].rearrange("p (i a) t -> p i a t", i=2),
                                              selm[:, 2 * g:2 * g + 2, :].unsqueeze(1).broadcast_to([P, 2, 2, T]),
                                              ps[q][:].rearrange("p (i a t) -> p i a t", i=2, a=2)).then_inc(s_sel, 1)
                        for hh in range(2):
                            V.copy_predicated(Ab[g][:, hh:4:2, :], selm[:, 4 + g, :].unsqueeze(1).broadcast_to([P, 2, T]),
                                              v3(ps[4 + hh][:, 0:TT])).then_inc(s_sel, 1)

                    def first(g):
                        dve.wait_ge(s_sel, 6 * (2 * c + g + 1))
                        low, up = (Ab[0], AT[0][:, :, 0, :]) if g == 0 else (AT[1][:, :, 0, :], Ab[1])
                        inv.dve_first(dve, c, g, low, up)

                    sums(0)
                    unit(0)
                    sums(1)
                    select(0)
                    unit(1)
                    first(0)
                    select(1)
                    first(1)
                    dve_link(dve, V.scalar_tensor_tensor(bon, bon, pcol("rk", c, 1), r, ALU.mult, ALU.mult))
                    V.tensor_copy(bon, bon).then_inc(s_bon, 1)
                    if c < RWC - 1:
                        dve.wait_ge(s_exp, 8 * (c + 1))
                        raw_key(c + 1)
                    for l in range(1, LEVELS):
                        inv.dve_level(dve, c, l)
                        if l == 1 and c < RWC - 1:
                            unit_key(c + 1)
                        if l == 2 and c:
                            centre(c - 1)
                        if l == 4 and c:
                            norm(c - 1)
                    for g in range(2):
                        dve.wait_ge(s_Z, 2 * c + g + 1)
                        V.tensor_copy(Zs[g].rearrange("p q v -> p (q v)"), ps[g][:, TT:2 * TT]).then_inc(s_Zs, 1)
                    dve.wait_ge(s_Y, c + 1)
                    V.tensor_copy(yT[:, 4 + c, :], ps[6][:, 0:TT]).then_inc(s_Ys, 1)
                    for g in range(2):
                        dve.wait_ge(s_S, 2 * c + g + 1)
                        for hh in range(2):
                            rows = slice(64 * hh, 64 * hh + 64)
                            ins = V.tensor_scalar(sst[rows, g, c, :], ps[2 + g][rows, 64 * hh:64 * hh + 64],
                                                  eh[g][rows, 0:1], None, ALU.mult)
                        ins.then_inc(s_Ss, 1)
                    dve.wait_ge(s_bss, c + 1)
                    V.tensor_tensor(r, ps[6][:, TT:2 * TT], vc, ALU.mult).then_inc(s_bons, 1)
                centre(RWC - 1)
                norm(RWC - 1)
                dve_link.sync(dve)
                dve.wait_ge(s_gg, 1)
                for h in range(2):
                    dve_link.last(dve, V.tensor_tensor(y4[:, 512 * h:512 * h + 512], y4[:, 512 * h:512 * h + 512], ps[4 + h][:],
                                                       ALU.mult))
                dve_link.sync(dve)
                dve_scl(dve, 2)
                dve_scl(dve, 3)
        def pe_out_proj(pe, first, src, sig):
            for d in range(DC):
                if d == 0:
                    arrived(pe, first)
                    arrived(pe, first + 1)
                for j in range(DC):
                    mm = nc.tensor.matmul(ps[d // 2][:, (d % 2) * TT:(d % 2 + 1) * TT],
                                          tile_out(first + j // 4)[:, j % 4, d * P:(d + 1) * P], src[:, j, :],
                                          start=(j == 0), stop=(j == DC - 1))
                if d == DC - 1:
                    mm.then_inc(s_used, 2)
                elif d % 2:
                    mm.then_inc(sig, 1)

        def dve_residual(dve, sig, count, tile, layer, m):
            for b in range(4):
                if b == 3 or sig is None:
                    used(dve, tile)
                else:
                    dve.wait_ge(sig, count + b + 1)
                for d in (2 * b, 2 * b + 1):
                    for s in range(NS):
                        x = xT[:, d, s * T:(s + 1) * T]
                        ins = nc.vector.scalar_tensor_tensor(x, ps[b][:, (d % 2) * TT + s * T:(d % 2) * TT + (s + 1) * T],
                                                             mod[:, layer, m + d, s:s + 1], x, ALU.mult, ALU.add)
                ins.then_inc(s_x, 1)

        drop(m_rw)
        hT = take(DC, TT)
        sq1 = take(DC, TT)
        act4 = take(2, 4, TT)
        sgt = take(2, TT)
        n1 = Norm(1, sq1)
        s_op, s_gu, s_sil, s_act = sem("out_proj_done"), sem("gate_up_done"), sem("silu_done"), sem("act_ready")
        FC = FF // P
        with nc.Block() as block:
            @block.sync
            def _(sp):
                feed(sp, FIRST["ffn"] + 17 - 4)

            @block.gpsimd
            def _(pool):
                pass

            @block.scalar
            def _(act):
                n1.act_squares(act, 1)
                n1.act_root(act, ps[4])
                for m in range(FC):
                    if m % 2:
                        used(act, FIRST["ffn"] + 3 * (m // 4) + m % 4 // 2)
                    else:
                        act.wait_ge(s_gu, m // 2 + 1)
                    if m >= 2:
                        act.wait_ge(s_act, m - 1)
                    nc.scalar.activation(sgt[:, m % 2, :], ps[4 + m % 4][:, 0:TT], ACT.Silu).then_inc(s_sil, 1)

            @block.tensor
            def _(pe):
                pe_out_proj(pe, FIRST["even_out"], yT, s_op)
                n1.pe(pe, ps[4])
                m = 0
                for k in range(FFN_OUT_TILES):
                    for n in range(2):
                        if 2 * k + n == FFN_IN_TILES:
                            continue
                        tile = FIRST["ffn"] + 3 * k + n
                        arrived(pe, tile)
                        w = tile_in(tile)
                        for _ in range(2):
                            if m >= 4:
                                pe.wait_ge(s_act, m - 3)
                            f = (m % 2) * P
                            for half in range(2):
                                for j in range(DC):
                                    if m == 0 and half == 0:
                                        n1.h_ready(pe, j)
                                    mm = nc.tensor.matmul(ps[4 + m % 4][:, half * TT:(half + 1) * TT],
                                                          w[:, j, half * 256 + f:half * 256 + f + P], hT[:, j, :],
                                                          start=(j == 0), stop=(j == DC - 1))
                            mm.then_inc(s_used if m % 2 else s_gu, 1)
                            m += 1
                    tile = FIRST["ffn"] + (3 * k + 2 if k < 5 else 16)
                    arrived(pe, tile)
                    for f in range(4 * k, m):
                        pe.wait_ge(s_act, f + 1)
                        for d in range(DC):
                            mm = nc.tensor.matmul(ps[d // 2][:, (d % 2) * TT:(d % 2 + 1) * TT],
                                                  tile_out(tile)[:, f % 4, d * P:(d + 1) * P], act4[:, k % 2, f % 4, :],
                                                  start=(f == 0 and d % 2 == 0), stop=(f == FC - 1), skip_group_check=True)
                    mm.then_inc(s_used, 1)

            @block.vector
            def _(dve):
                dve_residual(dve, s_op, 0, FIRST["even_out"] + 1, 0, 16)
                n1.dve(dve)
                for m in range(FC):
                    dve.wait_ge(s_sil, m + 1)
                    if m >= 8 and m % 4 == 0:
                        used(dve, FIRST["ffn"] + 3 * (m // 4 - 2) + 2)
                    nc.vector.tensor_tensor(act4[:, (m // 4) % 2, m % 4, :], ps[4 + m % 4][:, TT:2 * TT], sgt[:, m % 2, :],
                                            ALU.mult).then_inc(s_act, 1)
                dve_residual(dve, None, 0, FIRST["ffn"] + 16, 0, 40)
        drop(0)
        cons[2] = take(NCONST[2])
        qkv = take(3 * GH, TT)
        sz = take(GH, TT)
        gg = take(NS, 16)
        beta = take(NS, 16)
        Gp = take(NS, 16)
        eG = take(NS, 16)
        nbe = take(NS, 16)
        eE = take(16)
        m_gd = floats[0]
        hT = take(DC, TT)
        sq2 = take(DC, TT)
        pad = take(4, NS, T + 2)
        tmp = take(2, NS, T)
        gdrow = take(2, 16)
        xa, xn = take(NS, 16), take(NS, 16)
        nrm4 = take(2, 4, TT)
        n2 = Norm(2, sq2)
        s_s5 = sem("silu5_done")
        P1 = EC
        s_q5, s_ss5, s_rt5 = sem("qk_squared"), sem("qk_sumsq_done"), sem("qk_root_done")
        s_xn, s_e5, s_l5, s_g5, s_cum, s_eg = (sem("gate_arg_ready"), sem("gate_exp_done"),
                                                     sem("gate_log_done"), sem("log_decay_ready"), sem("decay_sums_done"),
                                                     sem("decay_exps_done"))
        s_b5 = sem("beta_done")
        s_c5, s_nq = sem("odd_params_loaded"), sem("qk_normed")
        OC = 32
        with nc.Block() as block:
            @block.sync
            def _(sp):
                sp.dma_start(cons[2], A["con2"]).then_inc(s_c5, 16)
                sp.dma_start(gdrow.rearrange("p a c -> p (a c)"), A["gdrow"].partition_broadcast(P)).then_inc(s_c5, 16)
                feed(sp, FIRST["odd_in"] + ODD_IN_TILES - 4)

            @block.gpsimd
            def _(pool):
                nc.gpsimd.memset(pad, 0.0).then_inc(s_pz, 1)

            @block.scalar
            def _(act):
                n2.act_squares(act, 5)
                n2.act_root(act, ps[4])
                act.wait_ge(s_pz, 2)
                for m in range(OC):
                    projected(act, m, OC - 1, FIRST["odd_in"], EC - EVEN_IN_TILES)
                    src = v3(ps[m % 4][:, 0:TT])
                    if m < 24:
                        if m >= 4:
                            act.wait_ge(s_pc, P1 + m - 3)
                        nc.scalar.activation(pad[:, m % 4, :, 1:T + 1], src, ACT.Copy).then_inc(s_pad, 1)
                        act.wait_ge(s_pc, P1 + m + 1)
                        nc.scalar.activation(qkv[:, m, :], qkv[:, m, :], ACT.Silu).then_inc(s_s5, 1)
                        if m < 16 and m % 4 == 3:
                            act.wait_ge(s_s5, m + 1)
                            if m >= 4:
                                act.wait_ge(s_ss5, m // 4)
                            nc.scalar.activation(nrm4[:, 0], qkv[:, m - 3:m + 1, :], ACT.Square).then_inc(s_q5, 1)
                        if m % 4 == 3 and 7 <= m <= 19:
                            g4 = m // 4 - 1
                            act.wait_ge(s_ss5, g4 + 1)
                            if g4:
                                act.wait_ge(s_nq, g4)
                            for h in range(2):
                                nc.scalar.activation(nrm4[:, 1, 2 * h:2 * h + 2, :].rearrange("p c t -> p (c t)"), ps[5 + h][:],
                                                     ACT.Sqrt, bias=cc("eps6")).then_inc(s_rt5, 1)
                    else:
                        nc.scalar.activation(v3(sz[:, m - 24, :]), src, ACT.Silu).then_inc(s_pad, 1)
                nc.scalar.activation(gdrow[:, 0, :], gdrow[:, 0, :], ACT.Exp).then_inc(s_e5, 1)
                used(act, FIRST["odd_in"] + 8)
                nc.scalar.activation(beta, ps[7][:, 0:64].rearrange("p (s c) -> p s c", s=2)[:, :, 16:32], ACT.Sigmoid)\
                    .then_inc(s_b5, 1)
                act.wait_ge(s_xn, 1)
                nc.scalar.activation(xn, xn, ACT.Exp).then_inc(s_e5, 1)
                act.wait_ge(s_e5, 2)
                nc.scalar.activation(xn, xn, ACT.Ln, bias=cc("one")).then_inc(s_l5, 1)
                act.wait_ge(s_cum, 1)
                nc.scalar.activation(eG, ps[5][:, 0:32].rearrange("p (d s h) -> p s d h", d=2, s=2), ACT.Exp).then_inc(s_eg, 1)
                nc.scalar.activation(eE, ps[5][:, 32:48], ACT.Exp).then_inc(s_eg, 1)

            @block.tensor
            def _(pe):
                n2.pe(pe, ps[4])
                for m in range(OC):
                    n = FIRST["odd_in"] + m // 4
                    if m % 4 == 0:
                        arrived(pe, n)
                    if m >= 4:
                        pe.wait_ge(s_pad, P1 + m - 3)
                    f = m % 4
                    for j in range(DC):
                        if m == 0:
                            n2.h_ready(pe, j)
                        mm = nc.tensor.matmul(ps[m % 4][:, 0:TT], tile_in(n)[:, j, f * P:(f + 1) * P], hT[:, j, :],
                                              start=(j == 0), stop=(j == DC - 1))
                    mm.then_inc(s_used if f == 3 else s_p, 1)
                    if m % 4 == 2 and 6 <= m <= 18:
                        g4 = m // 4 - 1
                        pe.wait_ge(s_q5, g4 + 1)
                        if g4:
                            pe.wait_ge(s_rt5, 2 * g4)
                        for h in range(2):
                            mm = nc.tensor.matmul(ps[5 + h][:], ones, nrm4[:, 0, 2 * h:2 * h + 2, :]
                                                  .rearrange("p c t -> p (c t)"), start=True, stop=True)
                        mm.then_inc(s_ss5, 1)
                n = FIRST["odd_in"] + 8
                arrived(pe, n)
                for s in range(NS):
                    for j in range(DC):
                        mm = nc.tensor.matmul(ps[7][:, 32 * s:32 * s + 32], hT[:, j, s * T:(s + 1) * T], tile_in(n)[:, j, 0:32],
                                              start=(j == 0), stop=(j == DC - 1))
                mm.then_inc(s_used, 1)
                pe.wait_ge(s_g5, 1)
                pe.wait_ge(s_c5, 32)
                pe.wait_ge(s_rt5, 8)
                for d in range(2):
                    nc.tensor.matmul(ps[5][:, 16 * d:16 * d + 16], cc("tri_f" if d == 0 else "tri_b"),
                                     gg[:, :, 8 * d:8 * d + 8], start=True, stop=True)
                for d in range(2):
                    mm = nc.tensor.matmul(ps[5][:, 32 + 8 * d:40 + 8 * d], cc("tri_sf" if d == 0 else "tri_sb"),
                                          gg[:, 0, 8 * d:8 * d + 8], start=True, stop=True)
                mm.then_inc(s_cum, 1)

            @block.vector
            def _(dve):
                V = nc.vector
                n2.dve(dve)
                w = pcol("gdw")

                def scale_qk(g4):
                    dve.wait_ge(s_rt5, 2 * (g4 + 1))
                    b = nrm4[:, 1]
                    dve_link(dve, V.reciprocal(b, b))
                    dve.wait_ge(s_s5, 4 * g4 + 4)
                    seg = qkv[:, 4 * g4:4 * g4 + 4, :]
                    V.scalar_tensor_tensor(seg.rearrange("p c t -> p (c t)"), seg.rearrange("p c t -> p (c t)"),
                                           P ** -0.5 if g4 < 2 else 1.0, b.rearrange("p c t -> p (c t)"), ALU.mult, ALU.mult)\
                        .then_inc(s_nq, 1)

                for m in range(24):
                    dve.wait_ge(s_pad, P1 + m + 1)
                    left, mid, right = (pad[:, m % 4, :, k:k + T] for k in range(3))
                    out = v3(qkv[:, m, :])
                    a = tmp[:, 0]
                    dve_link(dve, V.tensor_scalar(a, mid, w[:, 24 + m:25 + m], None, ALU.mult))
                    dve_link(dve, V.scalar_tensor_tensor(out, left, w[:, m:m + 1], a, ALU.mult, ALU.add))
                    V.scalar_tensor_tensor(out, right, w[:, 48 + m:49 + m], out, ALU.mult, ALU.add).then_inc(s_pc, 1)
                    dve.wait_ge(s_pc, P1 + m + 1)
                    if m % 4 == 0 and 8 <= m <= 20:
                        scale_qk(m // 4 - 2)
                dve.wait_ge(s_c5, 32)
                used(dve, FIRST["odd_in"] + 8)
                dve.wait_ge(s_b5, 1)
                bcast = lambda i: gdrow[:, i, :].unsqueeze(1).broadcast_to([P, NS, 16])
                dve_link(dve, V.tensor_tensor(xa, ps[7][:, 0:64].rearrange("p (s c) -> p s c", s=2)[:, :, 0:16], bcast(1), ALU.add))
                fl = lambda ap: ap.rearrange("p s c -> p (s c)")
                V.scalar_tensor_tensor(fl(xn), fl(xa), -1.0, fl(xa), ALU.mult, ALU.min).then_inc(s_xn, 1)
                dve.wait_ge(s_l5, 1)
                dve_link(dve, V.scalar_tensor_tensor(fl(xa), fl(xa), 0.0, fl(xn), ALU.max, ALU.add))
                dve.wait_ge(s_e5, 1)
                dve_link(dve, V.tensor_tensor(xa, xa, bcast(0), ALU.mult))
                V.tensor_scalar(gg, xa, -1.0, None, ALU.mult).then_inc(s_g5, 1)
                V.tensor_scalar(nbe, beta, -1.0, None, ALU.mult)
                dve.wait_ge(s_eg, 2)
                dve_link(dve, V.tensor_copy(Gp, ps[5][:, 0:32].rearrange("p (d s h) -> p s d h", d=2, s=2)))
                dve_link(dve, V.tensor_scalar(eG, eG, -1.0, None, ALU.mult))
        drop(m_gd)
        m_inv = floats[0]
        inv = Inversion()
        m_qk = floats[0]
        QK = [take(4, T) for _ in range(2)]
        Am = [take(4, T) for _ in range(2)]
        Dg = [take(4, T) for _ in range(2)]
        Rh = [take(4, T) for _ in range(2)]
        kend = [take(2, T) for _ in range(2)]
        S0 = take(2, 2, P)
        qd = [take(2, T) for _ in range(2)]
        flat = lambda lo, n: arena[:, lo:lo + n]
        sto = Am[0].rearrange("p (h d) t -> p h d t", h=2)
        yg = qkv[:, 0:GH, :]
        ygf = yg.rearrange("p h t -> p (h t)")
        sqg, rsg = take(512), take(512)
        s_s05, s_kq, s_row, s_vk, s_vt5, s_ks = (sem("s0_loaded"), sem("kq_done"), sem("decay_rows_done"),
                                                 sem("vk_tok_major"), sem("v_copied"), sem("ks0_done"))
        s_df, s_gam, s_er, s_gm, s_qd = (sem("decay_args_ready"), sem("decays5_done"), sem("row_exps_done"),
                                         sem("decays_masked"), sem("q_decayed"))
        s_bt, s_btt, s_A, s_At, s_ats = (sem("kk_scores_ready"), sem("kk_transposed"), sem("A_ready"), sem("A_transposed"),
                                         sem("At_copied"))
        s_ke, s_R, s_V, s_Vs, s_O5, s_Os, s_S5, s_sts = (
            sem("k_end_ready"), sem("rhs5_ready"), sem("values_done"), sem("values_copied"), sem("out5_done"),
            sem("out5_copied"), sem("state5_done"), sem("state5_copied"))
        s_sq6, s_ss6, s_rt6 = sem("o_squared"), sem("o_sumsq_done"), sem("o_root_done")
        s_nm = sem("o_scaled")
        NORM_LEVEL = 2
        router = arena[:, ARENA - DC * NE:].rearrange("p (j e) -> p j e", j=DC)
        assert floats[0] <= ARENA - DC * NE
        PAIRS = GH // 2
        BT_BANK, AT_BANK = (6, 5), (7, 3)
        with nc.Block() as block:
            @block.sync
            def _(sp):
                for i in range(PAIRS):
                    if i:
                        sp.wait_ge(s_O5, i)
                    sp.dma_start(S0, A["s0gd"][:, 2 * i:2 * i + 2]).then_inc(s_s05, 16)
                    if i == 0:
                        sp.dma_start(router, A["router"]).then_inc(s_c5, 16)
                        feed(sp, FIRST["odd_out"])
                    sp.wait_ge(s_sts, i + 1)
                    sp.dma_start(O["sgd"][:, 2 * i:2 * i + 2], sto).then_inc(s_stored, 16)
                sp.wait_ge(s_stored, 16 * (PAIRS + 1))

            @block.gpsimd
            def _(pool):
                for i in range(PAIRS):
                    for g in range(2):
                        if i:
                            pool.wait_ge(s_V, 2 * i)
                            pool.wait_ge(s_Z, 2 * RWC)
                        inv.pool_reset(pool, g)
                    for g in range(2):
                        k = 2 * i + g
                        pool.wait_ge(s_gam, k + 1)
                        nc.gpsimd.affine_select(out=Dg[g], in_=Dg[g], pattern=[[0, 4], [1 if g == 0 else -1, T]],
                                                compare_op=ALU.is_ge, fill=0.0, base=0,
                                                channel_multiplier=-1 if g == 0 else 1).then_inc(s_gm, 1)
                        pool.wait_ge(s_er, k + 1)
                        nc.gpsimd.tensor_tensor(qd[g], qd[g], qkv[:, 2 * i:2 * i + 2, T:TT], ALU.mult).then_inc(s_qd, 1)

            @block.scalar
            def _(act):
                def root(i):
                    act.wait_ge(s_ss6, i + 1)
                    if i:
                        act.wait_ge(s_nm, i)
                    nc.scalar.activation(rsg, ps[6][:], ACT.Sqrt, scale=1.0 / P, bias=cc("eps6")).then_inc(s_rt6, 1)

                for i in range(PAIRS):
                    act.wait_ge(s_vk, 2 * i + 1)
                    if i:
                        act.wait_ge(s_V, 2 * i)
                    nc.scalar.activation(Rh[1].rearrange("p q v -> p (q v)"), ps[4][:], ACT.Copy).then_inc(s_vt5, 1)
                    for g in range(2):
                        k = 2 * i + g
                        act.wait_ge(s_df, k + 1)
                        nc.scalar.activation(Dg[g], Dg[g], ACT.Exp).then_inc(s_gam, 1)
                        act.wait_ge(s_row, k + 1)
                        if i:
                            act.wait_ge(s_O5, i)
                        nc.scalar.activation(qd[g].rearrange("p h t -> p (h t)"), ps[2 + g][:, TT:2 * TT], ACT.Exp)\
                            .then_inc(s_er, 1)
                    for g in range(2):
                        act.wait_ge(s_At, 2 * i + g + 1)
                        nc.scalar.activation(Dg[g].rearrange("p q t -> p (q t)"), ps[AT_BANK[g]][:], ACT.Copy).then_inc(s_ats, 1)
                    for l in range(1, LEVELS):
                        inv.act_level(act, RWC + i, l)
                        if l == NORM_LEVEL and i:
                            root(i - 1)
                    for g in range(2):
                        act.wait_ge(s_V, 2 * i + g + 1)
                        nc.scalar.activation(inv.X[g].rearrange("p q v -> p (q v)"), ps[g][:], ACT.Copy).then_inc(s_Vs, 1)
                    act.wait_ge(s_O5, i + 1)
                    nc.scalar.activation(qkv[:, 2 * i:2 * i + 2, :].rearrange("p h t -> p (h t)"), ps[6][:], ACT.Copy)\
                        .then_inc(s_Os, 1)
                    act.wait_ge(s_Os, i + 1)
                    nc.scalar.activation(sqg, ygf[:, 512 * i:512 * i + 512], ACT.Square).then_inc(s_sq6, 1)
                root(PAIRS - 1)

            @block.tensor
            def _(pe):
                tri = [cc("tri_f"), cc("tri_b")]

                def sum_squares(i):
                    pe.wait_ge(s_sq6, i + 1)
                    nc.tensor.matmul(ps[6][:], ones, sqg, start=True, stop=True).then_inc(s_ss6, 1)

                for i in range(PAIRS):
                    if i:
                        pe.wait_ge(s_Vs, 2 * i)
                        pe.wait_ge(s_U[1], (RWC + i) * NU[1])
                        pe.wait_ge(s_T[1], (RWC + i) * NT[1])
                        pe.wait_ge(s_U[0], (RWC + i) * NU[0])
                    for hh in range(2):
                        h = 2 * i + hh
                        for s in range(NS):
                            tok = slice(s * T, (s + 1) * T)
                            mm = nc.tensor.matmul(ps[hh][:, s * TT:(s + 1) * TT].rearrange("p (a t) -> p a t", a=2),
                                                  qkv[:, GH + h, tok], qkv[:, h:h + GH + 1:GH, tok], start=True, stop=True)
                    mm.then_inc(s_kq, 1)
                    for g in range(2):
                        for q in range(4):
                            s, hh = divmod(q, 2)
                            col = gg[:, s, 8 * g + 2 * i + hh:8 * g + 2 * i + hh + 1].broadcast_to([P, P])
                            mm = nc.tensor.matmul(ps[2 + g][:, q * T:(q + 1) * T], col, tri[g], start=True, stop=True)
                        mm.then_inc(s_row, 1)
                    for q in range(4):
                        s, hh = divmod(q, 2)
                        mm = nc.tensor.transpose(ps[4][:, q * T:(q + 1) * T], qkv[:, 2 * GH + 2 * i + hh, s * T:(s + 1) * T], ident)
                    mm.then_inc(s_vk, 1)
                    for hh in range(2):
                        mm = nc.tensor.transpose(ps[5][:, hh * T:(hh + 1) * T], qkv[:, GH + 2 * i + hh, 0:T], ident)
                    mm.then_inc(s_vk, 1)
                    pe.wait_ge(s_s05, 16 * (i + 1))
                    pe.wait_ge(s_vt5, i + 1)
                    for hh in range(2):
                        mm = nc.tensor.matmul(ps[4][:, hh * TT:(hh + 1) * TT], qkv[:, GH + 2 * i + hh, T:TT],
                                              S0[:, hh].rearrange("p d v -> p (d v)"), start=True, stop=True)
                    mm.then_inc(s_ks, 1)
                    if i:
                        pe.wait_ge(s_Os, i)
                        pe.wait_ge(s_sts, i)
                    pe.wait_ge(s_ke, i + 1)
                    for g in range(2):
                        pe.wait_ge(s_bt, 2 * i + g + 1)
                        for q in range(4):
                            mm = nc.tensor.transpose(ps[BT_BANK[g]][:, q * T:(q + 1) * T], Dg[g][:, q], ident)
                        mm.then_inc(s_btt, 1)
                    pe.wait_ge(s_er, 2 * i + 2)
                    pe.wait_ge(s_R, 2 * i + 2)
                    for g in range(2):
                        pe.wait_ge(s_A, 2 * i + g + 1)
                        for q in range(4):
                            mm = nc.tensor.transpose(ps[AT_BANK[g]][:, q * T:(q + 1) * T], Am[g][:, q], ident)
                        mm.then_inc(s_At, 1)
                    pe.wait_ge(s_ats, 2 * i + 1)
                    up = [Dg[0], Am[1]]
                    for l in range(1, LEVELS):
                        inv.pe_level(pe, RWC + i, l, up)
                        if l == NORM_LEVEL and i:
                            sum_squares(i - 1)
                    for g in range(2):
                        inv.pe_final(pe, RWC + i, g)
                        for q in range(4):
                            mm = nc.tensor.matmul(ps[g][:, q * T:(q + 1) * T], inv.final[g][:, q], Rh[g][:, q], start=True, stop=True)
                        mm.then_inc(s_V, 1)
                    pe.wait_ge(s_Vs, 2 * i + 2)
                    pe.wait_ge(s_qd, 2 * i + 2)
                    if i:
                        pe.wait_ge(s_rt6, i)
                    for hh in range(2):
                        for s in range(NS):
                            q = 2 * s + hh
                            out = ps[6][:, hh * TT + s * T:hh * TT + (s + 1) * T]
                            for g in range(2):
                                if s:
                                    nc.tensor.matmul(out, S0[:, hh, g], qd[g][:, hh], start=(g == 0), stop=False)
                                mm = nc.tensor.matmul(out, inv.X[g][:, q], QK[g][:, q], start=(g == 0 and s == 0), stop=(g == 1))
                    mm.then_inc(s_O5, 1)
                    for hh in range(2):
                        for g in range(2):
                            mm = nc.tensor.matmul(ps[7][:, (2 * hh + g) * T:(2 * hh + g + 1) * T], kend[g][:, hh],
                                                  inv.X[g][:, hh], start=True, stop=True)
                    mm.then_inc(s_S5, 1)
                sum_squares(PAIRS - 1)

            @block.vector
            def _(dve):
                V = nc.vector

                def norm(i):
                    dve.wait_ge(s_rt6, i + 1)
                    y, z = (ap.rearrange("p h t -> p (h t)")[:, 512 * i:512 * i + 512] for ap in (yg, sz))
                    dve_link(dve, V.reciprocal(rsg, rsg))
                    V.tensor_tensor(y, y, rsg, ALU.mult).then_inc(s_nm, 1)
                    dve.wait_ge(s_nm, i + 1)
                    dve_link.last(dve, V.scalar_tensor_tensor(y, y, pcol("normg"), z, ALU.mult, ALU.mult))

                for i in range(PAIRS):
                    h0 = 2 * i
                    for g in range(2):
                        k = 2 * i + g
                        dve.wait_ge(s_row, k + 1)
                        for q in range(4):
                            s, hh = divmod(q, 2)
                            ins = V.tensor_scalar(Dg[g][:, q], ps[2 + g][:, q * T:(q + 1) * T],
                                                  Gp[:, s, 8 * g + h0 + hh:8 * g + h0 + hh + 1], 0.0, ALU.subtract, ALU.min)
                        ins.then_inc(s_df, 1)
                    dve.wait_ge(s_vk, 2 * i + 2)
                    for g in range(2):
                        for hh in range(2):
                            c = 8 * g + h0 + hh
                            ins = V.tensor_scalar(kend[g][:, hh], ps[5][:, hh * T:(hh + 1) * T], eE[:, c:c + 1], None, ALU.mult)
                    ins.then_inc(s_ke, 1)
                    dve.wait_ge(s_vt5, i + 1)
                    dve.wait_ge(s_ks, i + 1)
                    for g in range(2):
                        for hh in range(2):
                            c = 8 * g + h0 + hh
                            dve_link(dve, V.scalar_tensor_tensor(Rh[g][:, 2 + hh], ps[4][:, hh * TT + g * T:hh * TT + (g + 1) * T],
                                                                 eG[:, 1, c:c + 1], Rh[1][:, 2 + hh], ALU.mult, ALU.add))
                        for q in range(4):
                            s, hh = divmod(q, 2)
                            c = 8 * g + h0 + hh
                            ins = V.tensor_scalar(Rh[g][:, q], Rh[1][:, q] if s == 0 else Rh[g][:, q], beta[:, s, c:c + 1],
                                                  None, ALU.mult)
                        ins.then_inc(s_R, 1)
                    dve.wait_ge(s_kq, i + 1)
                    if i:
                        dve.wait_ge(s_stored, 16 * (i + 1))
                    for g in range(2):
                        k = 2 * i + g
                        dve.wait_ge(s_gm, k + 1)
                        for hh in range(2):
                            kq = ps[hh][:].rearrange("p (s a t) -> p s a t", s=2, a=2)
                            d = Dg[g][:, hh:4:2]
                            dve_link.last(dve, V.tensor_tensor(QK[g][:, hh:4:2], kq[:, :, 0], d, ALU.mult))
                        dve_link.sync(dve)
                        for hh in range(2):
                            kq = ps[hh][:].rearrange("p (s a t) -> p s a t", s=2, a=2)
                            d = Dg[g][:, hh:4:2]
                            ins = V.tensor_tensor(d, kq[:, :, 1], d, ALU.mult)
                        ins.then_inc(s_bt, 1)
                    for g in range(2):
                        dve.wait_ge(s_btt, 2 * i + g + 1)
                        for q in range(4):
                            s, hh = divmod(q, 2)
                            c = 8 * g + h0 + hh
                            ins = V.scalar_tensor_tensor(Am[g][:, q], ps[BT_BANK[g]][:, q * T:(q + 1) * T], nbe[:, s, c:c + 1],
                                                         selm[:, 4 + g, :], ALU.mult, ALU.mult)
                        ins.then_inc(s_A, 1)
                    dve.wait_ge(s_A, 2 * i + 2)
                    for g in range(2):
                        dve.wait_ge(s_ats, 2 * i + g + 1)
                        low, up = (Am[0], Dg[0]) if g == 0 else (Dg[1], Am[1])
                        inv.dve_first(dve, RWC + i, g, low, up)
                    for l in range(1, LEVELS):
                        inv.dve_level(dve, RWC + i, l)
                        if l == NORM_LEVEL and i:
                            norm(i - 1)
                    dve.wait_ge(s_S5, i + 1)
                    V.tensor_copy(sto.rearrange("p h d t -> p (h d t)"), ps[7][:]).then_inc(s_sts, 1)
                norm(PAIRS - 1)
                dve_link.sync(dve)
        HALF = T // 2
        drop(NCONST[2])
        yg7 = take(GH, TT)
        hT = take(DC, TT)
        htok = take(NS, D)
        hA = take(DC, T)
        hB = take(DC, T)
        moe = take(DC, TT)
        m_route = floats[0]
        rows16 = NE * 2 + 1
        pos = take(NS, rows16)
        wgt = take(NS, 2 * NE)
        Psel = take(NS, T)
        Pw = take(2, NS, T)
        posh = take(NS, rows16)
        flag = take(2)
        few = take(2 * NE).bitcast(I32)
        m_experts = floats[0]
        sq3 = take(DC, TT)
        L, cnt, wd, sel = take(NS, NE), take(NS, NE), take(NS, NE), take(NS, NE)
        cg, ce = take(NS, NE, NE), take(NS, NE, NE)
        s1 = take(2, NS, NE)
        top = take(NS, NE)
        lv = take(4, NS)
        n3 = Norm(3, sq3)
        s_lg, s_cnt7, s_e7, s_rk, s_P, s_Pw, s_flag = (
            sem("logits_done"), sem("selection_ready"), sem("route_exp_done"), sem("ranks_done"),
            sem("slots_ready"), sem("slot_weights_ready"), sem("overflow_known"))
        s_ht, s_htc, s_gat, s_hB, s_hA = (sem("h_tok_major"), sem("h_tok_copied"), sem("gathered"), sem("gather_copied"),
                                                 sem("expert_h_ready"))
        s_dl = sem("gate_diff_ready")
        s_tr8, s_aT, s_ye, s_Ct, s_C, s_sc, s_acc = (
            sem("act_transposed"), sem("act_t_copied"), sem("y_copied"),
            sem("weights_transposed"), sem("weights_copied"), sem("scattered"), sem("accumulated"))
        over = flag.bitcast(I32)[:, 0:1]

        def dve_slots(dve, out, it, weights, pos=pos):
            for s in range(NS):
                p = pos[:, s, bass.ds(it, 1)]
                if weights:
                    ins = nc.vector.tensor_scalar(out[:, s, :], cc("iota"), p, wgt[:, s, bass.ds(it, 1)], ALU.is_equal, ALU.mult)
                else:
                    ins = nc.vector.tensor_scalar(out[:, s, :], cc("iota"), p, None, ALU.is_equal)
            return ins

        def pe_gather(pe, half):
            for j in range(4 * half, 4 * half + 4):
                for s in range(NS):
                    mm = nc.tensor.matmul(ps[5][:, (j % 4) * T:(j % 4 + 1) * T], htok[:, s, j * P:(j + 1) * P], Psel[:, s, :],
                                          start=(s == 0), stop=(s == 1))
            mm.then_inc(s_gat, 1)

        def act_gather(act, half):
            nc.scalar.activation(hB[:, 4 * half:4 * half + 4, :].rearrange("p j t -> p (j t)"), ps[5][:], ACT.Copy)\
                .then_inc(s_hB, 1)

        with nc.Block() as block:
            @block.sync
            def _(sp):
                feed(sp, STREAM_TILES)

            @block.gpsimd
            def _(pool):
                nc.gpsimd.memset(moe, 0.0)
                for s in (s_tr8, s_aT, s_Ct, s_acc):
                    pool.sem_inc(s, 1)

            @block.scalar
            def _(act):
                n3.act_squares(act, 9)
                n3.act_root(act, ps[4])
                for k in range(4):
                    act.wait_ge(s_ht, k + 1)
                    nc.scalar.activation(htok[:, k // 2, 512 * (k % 2):512 * (k % 2) + 512], ps[k][:], ACT.Copy).then_inc(s_htc, 1)
                act.wait_ge(s_dl, 1)
                nc.scalar.activation(lv[:, 2], lv[:, 1], ACT.Exp).then_inc(s_e7, 1)
                for half in range(2):
                    act.wait_ge(s_gat, half + 1)
                    act_gather(act, half)

            @block.tensor
            def _(pe):
                pe_out_proj(pe, FIRST["odd_out"], yg7, s_op)
                n3.pe(pe, ps[4])
                pe.wait_ge(s_c5, 48)
                for s in range(NS):
                    for j in range(DC):
                        if s == 0:
                            n3.h_ready(pe, j)
                        mm = nc.tensor.matmul(ps[6][:, 8 * s:8 * s + 8], hT[:, j, s * T:(s + 1) * T], router[:, j, :],
                                              start=(j == 0), stop=(j == DC - 1))
                mm.then_inc(s_lg, 1)
                for k in range(4):
                    for j in range(4):
                        mm = nc.tensor.transpose(ps[k][:, j * P:(j + 1) * P],
                                                 hT[:, 4 * (k % 2) + j, (k // 2) * T:(k // 2 + 1) * T], ident)
                    mm.then_inc(s_ht, 1)
                pe.wait_ge(s_cnt7, 1)
                nc.tensor.matmul(ps[7][:, 0:8], cc("tri_sb"), sel[:, 0, :], start=True, stop=True)
                nc.tensor.matmul(ps[7][:, 8:16], cc("tri_sb"), sel[:, 1, :], start=True, stop=False)
                nc.tensor.matmul(ps[7][:, 8:16], ones, sel[:, 0, :], start=False, stop=True)
                nc.tensor.matmul(ps[7][:, 16:24], ones, sel[:, 0, :], start=True, stop=False)
                nc.tensor.matmul(ps[7][:, 16:24], ones, sel[:, 1, :], start=False, stop=True).then_inc(s_rk, 1)
                pe.wait_ge(s_htc, 4)
                pe.wait_ge(s_P, 1)
                pe_gather(pe, 0)
                pe.wait_ge(s_hB, 1)
                pe_gather(pe, 1)

            @block.vector
            def _(dve):
                V = nc.vector
                dve_residual(dve, s_op, 3, FIRST["odd_out"] + 1, 1, 16)
                n3.dve(dve)
                dve.wait_ge(s_lg, 1)
                dve_link(dve, V.tensor_copy(L.rearrange("p s e -> p (s e)"), ps[6][:, 0:16]))
                for s in range(NS):
                    other = L[:, s, :].unsqueeze(1).broadcast_to([P, NE, NE])
                    own = L[:, s, :].unsqueeze(2).broadcast_to([P, NE, NE])
                    tie = cc("tie").rearrange("p (a b) -> p a b", a=NE)
                    dve_link.last(dve, V.tensor_tensor(cg[:, s], other, own, ALU.is_gt))
                    dve_link(dve, V.tensor_tensor(ce[:, s], other, own, ALU.is_equal))
                    dve_link(dve, V.tensor_tensor(ce[:, s], ce[:, s], tie, ALU.mult))
                dve_link(dve, V.tensor_tensor(cg.rearrange("p s a b -> p (s a b)"), cg.rearrange("p s a b -> p (s a b)"),
                                              ce.rearrange("p s a b -> p (s a b)"), ALU.add))
                dve_link(dve, V.tensor_reduce(cnt, cg, AX.X, ALU.add))
                dve_link.last(dve, V.tensor_scalar(s1[:, 0], cnt, 0.0, None, ALU.is_equal))
                dve_link.last(dve, V.tensor_scalar(s1[:, 1], cnt, 1.0, None, ALU.is_equal))
                dve_link.sync(dve)
                V.tensor_scalar(sel, cnt, 1.5, None, ALU.is_lt).then_inc(s_cnt7, 1)
                dve_link.last(dve, V.tensor_tensor(top, s1[:, 0], L, ALU.mult))
                dve_link.last(dve, V.tensor_tensor(wd, s1[:, 1], L, ALU.mult))
                dve_link.sync(dve)
                dve_link.last(dve, V.tensor_reduce(lv[:, 0], top, AX.X, ALU.add))
                dve_link.last(dve, V.tensor_reduce(lv[:, 1], wd, AX.X, ALU.add))
                dve_link.sync(dve)
                V.tensor_tensor(lv[:, 1], lv[:, 1], lv[:, 0], ALU.subtract).then_inc(s_dl, 1)
                dve.wait_ge(s_e7, 1)
                dve_link(dve, V.tensor_scalar(lv[:, 3], lv[:, 2], 1.0, None, ALU.add))
                dve_link(dve, V.reciprocal(lv[:, 3], lv[:, 3]))
                dve_link(dve, V.tensor_tensor(lv[:, 2], lv[:, 2], lv[:, 3], ALU.mult))
                for s in range(NS):
                    dve_link(dve, V.tensor_scalar(wd[:, s], s1[:, 0, s], lv[:, 3, s:s + 1], None, ALU.mult))
                    for r in range(2):
                        dve_link.last(dve, V.scalar_tensor_tensor(wgt[:, s, 8 * r:8 * r + 8], s1[:, 1, s], lv[:, 2, s:s + 1], wd[:, s],
                                                                  ALU.mult, ALU.add))
                dve_link.sync(dve)
                dve.wait_ge(s_rk, 1)
                dve_link(dve, V.tensor_scalar(pos[:, :, 0:8], sel, -4096.0, 4096.0, ALU.mult, ALU.add))
                dve_link(dve, V.tensor_tensor(pos[:, :, 0:8], pos[:, :, 0:8], ps[7][:, 0:16].rearrange("p (s e) -> p s e", s=2),
                                              ALU.add))
                dve_link.last(dve, V.tensor_scalar(pos[:, :, 8:16], pos[:, :, 0:8], -float(T), None, ALU.add))
                dve_link.last(dve, V.memset(pos[:, :, 16:17], 4096.0))
                for r in range(2):
                    dve_link.last(dve, V.tensor_scalar(few[:, NE * r:NE * r + NE], ps[7][:, 16:24], float(T * r + HALF), None,
                                                       ALU.is_le))
                dve_link(dve, V.tensor_reduce(flag[:, 1:2], ps[7][:, 16:24], AX.X, ALU.max))
                V.tensor_scalar(over, flag[:, 1:2], float(T), None, ALU.is_gt).then_inc(s_flag, 1)
                dve_link.sync(dve)
                V.tensor_scalar(posh, pos, float(HALF), None, ALU.add)
                dve_slots(dve, Psel, 0, False).then_inc(s_P, 1)
                dve.wait_ge(s_hB, 2)
                V.tensor_copy(hA, hB).then_inc(s_hA, 1)

        drop(m_route)
        floats[0] = m_experts
        sgl = take(2, 512)
        actb = take(2, 512)
        actT = take(2, 4, T)
        ye = take(D)
        Cw = take(2, TT)
        sq4, yout = take(DC, TT), hT
        n4 = Norm(None, sq4)
        KC = EFF // 512
        TG = [0] + [2 + 3 * (k - 1) for k in range(1, KC)]
        TU = [t + 1 for t in TG]
        TO = [TG[k + 1] + 2 for k in range(KC - 1)] + [EXP_TILES - 1]
        BANKS = [2, 3, 4, 5]

        def used8(eng, it, t):
            eng.wait_ge(s_used, it * EXP_TILES + (STREAM_TILES + t + 1))

        def arrived8(eng, it, t):
            n = STREAM_TILES + t
            eng.wait_ge(s_slot[n % RING], it * (16 * EXP_TILES // RING) + 16 * (n // RING + 1))

        def rounds(eng, expert, after=lambda it: None):
            def body(it):
                some = eng.value_load(few[0:1, bass.ds(it, 1)], min_val=0, max_val=1)
                with eng.If(some > 0):
                    expert(it, True)
                with eng.If(some < 1):
                    expert(it, False)
                after(it)

            with eng.Fori(0, NE) as it:
                body(it)
            eng.wait_ge(s_flag, 1)
            more = eng.value_load(over[0:1, 0:1], min_val=0, max_val=1)
            with eng.If(more > 0):
                with eng.Fori(NE, 2 * NE) as it:
                    body(it)

        with nc.Block() as block:
            @block.sync
            def _(sp):
                def load(it, e, t):
                    n = STREAM_TILES + t
                    sp.dma_start(slot(n), A["experts"][bass.ds(e, 1), t % EXP_TILES].rearrange("a p c -> (a p) c"))\
                        .then_inc(s_slot[n % RING], 16)

                def tail_tiles(it, e):
                    for t in range(RING, EXP_TILES):
                        used8(sp, it, t - RING)
                        load(it, e, t)

                def next_tiles(it, e):
                    for t in range(EXP_TILES, EXP_TILES + RING):
                        used8(sp, it, t - RING)
                        load(it, e + 1, t)

                with sp.Fori(0, NE - 1) as e:
                    tail_tiles(e, e)
                    next_tiles(e, e)
                tail_tiles(NE - 1, NE - 1)
                sp.wait_ge(s_flag, 1)
                more = sp.value_load(over[0:1, 0:1], min_val=0, max_val=1)
                with sp.If(more > 0):
                    next_tiles(NE - 1, -1)
                    with sp.Fori(0, NE - 1) as e:
                        tail_tiles(e + NE, e)
                        next_tiles(e + NE, e)
                    tail_tiles(2 * NE - 1, NE - 1)
                for b in range(4):
                    n4.h_ready(sp, 2 * b + 1)
                    sp.dma_start(O["y"][:, 2 * b:2 * b + 2], yout[:, 2 * b:2 * b + 2]).then_inc(s_stored, 16)
                sp.wait_ge(s_stored, 16 * (PAIRS + 5))

            @block.gpsimd
            def _(pool):
                pass

            @block.scalar
            def _(act):
                def expert(it, small):
                    g0 = it * KC
                    n = 256 if small else 512
                    flat = lambda k: actT[:, k % 2].rearrange("p f t -> p (f t)")[:, 0:n]
                    for k in range(KC):
                        used8(act, it, TG[k])
                        act.wait_ge(s_act, g0 + (FC + max(k - 1, 0)))
                        nc.scalar.activation(sgl[:, k % 2, 0:n], ps[2 * (k % 2)][:, 0:n], ACT.Silu).then_inc(s_sil, 1)
                        if k:
                            act.wait_ge(s_tr8, g0 + k + 1)
                            if k >= 2:
                                used8(act, it, TO[k - 2])
                            nc.scalar.activation(flat(k - 1), ps[4][:, 0:n], ACT.Copy).then_inc(s_aT, 1)
                        if k in (2, 3):
                            act.wait_ge(s_hA, it + 1)
                            act.wait_ge(s_gat, 2 * it + (k + 1))
                            act_gather(act, k - 2)
                        if k == 4:
                            act.wait_ge(s_Ct, it + 2)
                            m = 2 if small else 1
                            nc.scalar.activation(Cw[:, 0:m].rearrange("p a t -> p (a t)"), ps[5][:, 0:m * TT], ACT.Copy)\
                                .then_inc(s_C, 1)
                    act.wait_ge(s_tr8, g0 + KC + 1)
                    nc.scalar.activation(flat(KC - 1), ps[4][:, 0:n], ACT.Copy).then_inc(s_aT, 1)
                    used8(act, it, TO[KC - 1])
                    for h in range(2):
                        src = ps[6][:, 256 * h:256 * h + 256] if small else ps[6 + h][:]
                        nc.scalar.activation(ye[:, n * h:n * h + n], src, ACT.Copy).then_inc(s_ye, 1)
                rounds(act, expert)
                n4.act_squares(act, 13)
                n4.act_root(act, ps[0])

            @block.tensor
            def _(pe):
                def transposes(it, k, small):
                    pe.wait_ge(s_act, it * KC + (FC + k + 1))
                    pe.wait_ge(s_aT, it * KC + (k + 1))
                    for f in range(2 if small else 4):
                        mm = nc.tensor.transpose(ps[4][:, f * T:(f + 1) * T], actb[:, k % 2, f * P:(f + 1) * P], ident)
                    mm.then_inc(s_tr8, 1)

                def in_product(t, out, small):
                    w = tile_in(STREAM_TILES + t)
                    for j in range(DC):
                        if small:
                            for c in range(2):
                                mm = nc.tensor.matmul(out[HALF * c:HALF * c + HALF, 0:256], hA[:, j, 0:HALF],
                                                      w[:, j, 256 * c:256 * c + 256], start=(j == 0), stop=(j == DC - 1),
                                                      tile_position=(0, HALF * c))
                        else:
                            mm = nc.tensor.matmul(out[:], hA[:, j, :], w[:, j, :], start=(j == 0), stop=(j == DC - 1))
                    mm.then_inc(s_used, 1)

                def project(it, k, small):
                    n = STREAM_TILES + TO[k]
                    pe.wait_ge(s_aT, it * KC + (k + 2))
                    arrived8(pe, it, TO[k])
                    for f in range(4):
                        for h in range(2):
                            w = tile_out(n)[:, f, 512 * h:512 * h + 512]
                            start, stop = (k == 0 and f == 0), (k == KC - 1 and f == 3)
                            if small:
                                o = HALF * (f // 2)
                                mm = nc.tensor.matmul(ps[6][HALF * h:HALF * h + HALF, :], actT[:, k % 2, f % 2, o:o + HALF], w,
                                                      start=start, stop=stop, tile_position=(0, HALF * h))
                            else:
                                mm = nc.tensor.matmul(ps[6 + h][:], actT[:, k % 2, f, :], w, start=start, stop=stop)
                    mm.then_inc(s_used, 1)

                def expert(it, small):
                    pe.wait_ge(s_hA, it + 1)
                    for k in range(KC):
                        pe.wait_ge(s_act, it * KC + (FC + max(k - 1, 0)))
                        if k == 1:
                            pe.wait_ge(s_acc, it * 4 + 1)
                        for half, t in enumerate((TG[k], TU[k])):
                            arrived8(pe, it, t)
                            if half and k:
                                transposes(it, k - 1, small)
                            in_product(t, ps[2 * (k % 2) + half], small)
                        if k:
                            project(it, k - 1, small)
                        if k == 2:
                            pe.wait_ge(s_P, it + 2)
                            pe_gather(pe, 0)
                        if k == 3:
                            pe.wait_ge(s_hB, 2 * it + 3)
                            pe_gather(pe, 1)
                        if k == 4:
                            pe.wait_ge(s_hB, 2 * it + 4)
                            pe.wait_ge(s_Pw, it + 1)
                            for m in range(2 if small else 1):
                                for s in range(NS):
                                    mm = nc.tensor.transpose(ps[5][:, m * TT + s * T:m * TT + (s + 1) * T], Pw[:, m, s, :], ident)
                            mm.then_inc(s_Ct, 1)
                    transposes(it, KC - 1, small)
                    project(it, KC - 1, small)
                    pe.wait_ge(s_C, it + 1)
                    pe.wait_ge(s_ye, 2 * it + 2)
                    for b in range(4):
                        for d in (2 * b, 2 * b + 1):
                            m, o = divmod(d, 4) if small else (0, d)
                            mm = nc.tensor.matmul(ps[BANKS[b]][:, (d % 2) * TT:(d % 2 + 1) * TT], ye[:, o * P:(o + 1) * P],
                                                  Cw[:, m], start=True, stop=True)
                        mm.then_inc(s_sc, 1)
                rounds(pe, expert)
                n4.pe(pe, ps[0])

            @block.vector
            def _(dve):
                V = nc.vector

                def expert(it, small):
                    n = 256 if small else 512
                    dve.wait_ge(s_Ct, it + 1)
                    if small:
                        dve_slots(dve, Pw[:, 1], it, True, posh)
                    dve_slots(dve, Pw[:, 0], it, True).then_inc(s_Pw, 1)
                    dve.wait_ge(s_gat, 2 * it + 2)
                    dve_slots(dve, Psel, it + 1, False).then_inc(s_P, 1)
                    for k in range(KC):
                        dve.wait_ge(s_sil, it * KC + (FC + k + 1))
                        used8(dve, it, TU[k])
                        dve.wait_ge(s_tr8, it * KC + (max(k - 1, 0) + 1))
                        V.tensor_tensor(actb[:, k % 2, 0:n], ps[2 * (k % 2) + 1][:, 0:n], sgl[:, k % 2, 0:n], ALU.mult)\
                            .then_inc(s_act, 1)
                    dve.wait_ge(s_hB, 2 * it + 4)
                    V.tensor_copy(hA, hB).then_inc(s_hA, 1)
                    for b in range(4):
                        dve.wait_ge(s_sc, 4 * it + (b + 1))
                        m = moe[:, 2 * b:2 * b + 2, :].rearrange("p d t -> p (d t)")
                        V.tensor_tensor(m, m, ps[BANKS[b]][:], ALU.add).then_inc(s_acc, 1)
                rounds(dve, expert, lambda it: dve.wait_ge(s_acc, 4 * it + 5))
                for d in range(DC):
                    for s in range(NS):
                        x = xT[:, d, s * T:(s + 1) * T]
                        ins = V.scalar_tensor_tensor(x, moe[:, d, s * T:(s + 1) * T], mod[:, 1, 40 + d, s:s + 1], x, ALU.mult, ALU.add)
                    if d % 2:
                        ins.then_inc(s_x, 1)
                n4.dve(dve, yout)


def _cols(v, chunks):
    v = np.asarray(v, np.float32).reshape(-1)
    out = np.zeros((chunks * P,), np.float32)
    out[:v.size] = v
    return out.reshape(chunks, P).T


def _in_tiles(w, groups):
    out = np.zeros((len(groups), P, 8, 512), np.float32)
    wj = w.reshape(8, P, w.shape[1])
    for t, ranges in enumerate(groups):
        at = 0
        for a, b in ranges:
            out[t, :, :, at:at + b - a] = wj[:, :, a:b].transpose(1, 0, 2)
            at += b - a
    return out.reshape(len(groups), P, TILE)


def _out_tiles(w):
    k = -(-w.shape[0] // 512)
    full = np.zeros((k * 512, 1024), np.float32)
    full[:w.shape[0]] = w
    return full.reshape(k, 4, P, 1024).transpose(0, 2, 1, 3).reshape(k, P, TILE)


def _by(n, step=512):
    return [[(a, min(a + step, n))] for a in range(0, n, step)]


def pack(i):
    i = {k: np.asarray(v) for k, v in i.items()}
    table, masks, feats, window, posT = constants()
    par = {}
    c0 = i["c_ctx"].reshape(8, P)
    c1 = i["c"].reshape(8, P)
    par["cond"] = np.stack([c0, c1], -1).transpose(1, 0, 2).reshape(P, 16)
    for l in range(2):
        par[f"ada_b{l}"] = _cols(i["ada_b"][l], 48)
        par[f"gmix{l}"] = _cols(i["norm_mix_g"][l], 8)
        par[f"gffn{l}"] = _cols(i["norm_ffn_g"][l], 8)
    par["gfin"] = _cols(i["final_norm_g"], 8)
    par["hyw"] = np.concatenate([_cols(i["e_hy_conv_w"][0, k], 12) for k in range(3)], 1)
    par["hyb"] = _cols(i["e_hy_conv_b"], 12)
    par["mu"] = _cols(i["e_rw_mu"], 14)
    par["w0"] = np.concatenate([_cols(i["e_rw_w0"][0, d], 4) for d in range(2)], 1)
    par["a0"] = np.concatenate([_cols(i["e_rw_a0"][0, d], 4) for d in range(2)], 1)
    par["kk"], par["ka"], par["rk"] = (_cols(i[n], 4) for n in ("e_rw_kk", "e_rw_ka", "e_rw_rk"))
    par["lnw"], par["lnb"] = _cols(i["e_rw_ln_w"], 4), _cols(i["e_rw_ln_b"], 4)
    par["gdw"] = np.concatenate([_cols(i["o_conv_w"][0, k], 24) for k in range(3)], 1)
    par["normg"] = _cols(i["o_norm_g"], 1)
    for k in (1, 2):
        par[f"hfb{k}"] = _cols(i[f"e_hf_b{k}"], 1)
        par[f"hff{k}"] = _cols(i[f"e_hf_freq{k}"], 1)
    x = np.concatenate([i["x_prompt"][0], i["x_sample"][0]], 0)
    hfw = np.zeros((64, 128 + 2048), np.float32)
    hfw[:33, :64] = i["e_hf_w1"][0]
    hfw[:, 64:128] = i["e_hf_w2"][0]
    hfw[:, 128:] = i["e_hf_w3"][0]
    ada = [_in_tiles(i["ada_w"][l], _by(6144)) for l in range(2)]
    ffn_in = _in_tiles(i["e_ffn_w_in"][0], [[(a, a + 256), (FF + a, FF + a + 256)] for a in range(0, FF, 256)])
    ffn_out = _out_tiles(i["e_ffn_w_out"][0])
    ffn = []
    for k in range(FFN_OUT_TILES):
        ffn += [ffn_in[2 * k:2 * k + 2], ffn_out[k:k + 1]]
    parts = {"ada0a": ada[0][:4], "ada0b": ada[0][4:], "ada1": ada[1],
             "even_in": _in_tiles(i["e_w_in"][0], _by(3296)), "even_out": _out_tiles(i["e_w_out"][0]),
             "ffn": np.concatenate(ffn), "odd_in": _in_tiles(i["o_w_in"][0], _by(4128)),
             "odd_out": _out_tiles(i["o_w_out"][0])}
    stream = np.concatenate([parts[n] for n, _ in STREAM])
    experts = np.empty((NE, EXP_TILES, P, TILE), np.float32)
    for e in range(NE):
        gu = _in_tiles(i["o_moe_w_in"][0, e], [[(a + g, a + g + 512)] for a in range(0, EFF, 512) for g in (0, EFF)])
        wo = _out_tiles(i["o_moe_w_out"][0, e])
        for k in range(7):
            at = 3 * k - 1 if k else 0
            experts[e, at:at + 2] = gu[2 * k:2 * k + 2]
            experts[e, 3 * k + 4 if k < 6 else 20] = wo[k]
    f = lambda a: np.ascontiguousarray(a, dtype=a.dtype)
    out = {
        "par": f(np.concatenate([par[n].reshape(P, k) for n, k in PARAM_SIZES], 1)),
        "con0": table[0], "con1": table[1], "con2": table[2], "masks": masks, "feats": feats, "window": window, "pos": posT,
        "xT": f(x.T.reshape(8, P, TT).transpose(1, 0, 2)),
        "hfw": hfw, "hbias": f(i["e_hy_bias"].reshape(1024)),
        "stream": stream, "experts": experts,
        "lora": f(np.concatenate([i["e_rw_w2"].reshape(64, 512), i["e_rw_a2"].reshape(64, 512)], 0)),
        "g2": f(i["e_rw_g2"][0]),
        "s0rw": f(i["state_rwkv"][0, 0].reshape(2, 4, 2, 64, 64).transpose(2, 4, 0, 1, 3).reshape(P, 2, 4, 64)),
        "s0gd": f(i["state_gdn"][0, 0].transpose(2, 1, 0, 3)),
        "gdrow": f(np.concatenate([i["o_A_log"].reshape(16), i["o_dt_bias"].reshape(16)])),
        "router": f(i["o_router"][0].reshape(8, P, 8).transpose(1, 0, 2)),
    }
    return out


OUTS = {"y": (P, DC, TT), "srw": (P, 2, 4, 64), "sgd": (P, GH, 2, P)}


def unpack(r):
    y = r["y"].transpose(2, 1, 0).reshape(TT, D)
    srw = r["srw"].reshape(2, 64, 2, 4, 64).transpose(2, 3, 0, 4, 1).reshape(1, 1, 2, 8, 64, 64)
    sgd = r["sgd"].transpose(2, 1, 0, 3).reshape(1, 1, 2, GH, P, P)
    c = np.ascontiguousarray
    return c(y[:T].reshape(1, T, D)), c(y[T:].reshape(1, T, D)), c(srw), c(sgd)


def kernel(**inputs):
    import concourse.bacc as bacc
    from concourse.bass_utils import run_bass_kernel_spmd

    nc = bacc.Bacc("TRN2", target_bir_lowering=False, num_devices=1)
    arrays, A = {}, {}
    for name, a in pack(inputs).items():
        arrays["in_" + name] = a
        A[name] = nc.dram_tensor("in_" + name, a.shape, mybir.dt.from_np(a.dtype), kind="ExternalInput").ap()
    O = {n: nc.dram_tensor("out_" + n, s, F32, kind="ExternalOutput").ap() for n, s in OUTS.items()}
    program(nc, A, O)
    r = run_bass_kernel_spmd(nc, [arrays], core_ids=[0])
    return unpack({n: np.asarray(r.results[0]["out_" + n]) for n in OUTS})
```
